# Optimizing a Trainium2 kernel written in Bass

```python
import math
import jax
import jax.numpy as jnp
from jax import lax
import numpy as np

D_MODEL = 2048
BATCH = 1
SEQ = 256
DEPTH = 2

N_A_LAYERS = DEPTH // 2
N_B_LAYERS = DEPTH - N_A_LAYERS
RW_HEAD = 64
RW_HEADS = D_MODEL // RW_HEAD
LORA_DECAY = 96
LORA_A = 128
LORA_V = 64
LORA_G = 256
N_SHIFT_MIX = 6
GN_EPS = 64e-5
NSA_HEADS = 16
NSA_GROUPS = 4
NSA_REP = NSA_HEADS // NSA_GROUPS
NSA_HD = D_MODEL // NSA_HEADS
N_KV_PARTS = 6
CMP_STRIDE = 16
CMP_LEN = 2 * CMP_STRIDE
SEL_BLOCK = 64
SEL_TOP = 16
WINDOW = 512
QBLK = 128
N_BRANCH = 3
SEL_FORCE = 1e4
NEG_INF = -1e30
REL_BUCKETS = 32
REL_MAX_DIST = 128
D_FF = 4 * D_MODEL
NORM_EPS = 1e-6

kernel_name = 'rwkv7_nsa_yoco_hybrid'

def rmsnorm(x, g):
    xf = x.astype(jnp.float32)
    y = xf * lax.rsqrt(jnp.mean(xf * xf, axis=-1, keepdims=True) + NORM_EPS)
    return (y * g.astype(jnp.float32)).astype(x.dtype)

def t5_bucket(dist):
    n = jnp.maximum(dist, 0)
    max_exact = REL_BUCKETS // 2
    nf = jnp.maximum(n, 1).astype(jnp.float32)
    large = max_exact + (jnp.log(nf / max_exact) / math.log(REL_MAX_DIST / max_exact)
                         * (REL_BUCKETS - max_exact)).astype(jnp.int32)
    large = jnp.minimum(large, REL_BUCKETS - 1)
    return jnp.where(n < max_exact, n, large)

def sqrelu_mlp(xn, w_up, w_down):
    return jnp.square(jax.nn.relu(xn @ w_up)) @ w_down

def _rwkv7_step(S, inp):
    r, w, k, v, a, b = inp
    sa = jnp.einsum('bhij,bhj->bhi', S, a)
    S = S * w[:, :, None, :] + sa[..., None] * b[:, :, None, :] + v[..., None] * k[:, :, None, :]
    return S, jnp.einsum('bhij,bhj->bhi', S, r)

def rwkv7_time_mix(xn, mu, wr, wk, wv, wo, w0, w1, w2, a0, a1, a2, g1, g2,
                   k_k, k_a, r_k, lnx_w, lnx_b, v_first, v0, v1, v2):
    B, T, C = xn.shape
    H, N = RW_HEADS, RW_HEAD
    f32 = jnp.float32
    xx = jnp.pad(xn[:, :-1], ((0, 0), (1, 0), (0, 0))) - xn
    xr, xw, xk, xv, xa, xg = [xn + xx * mu[i] for i in range(N_SHIFT_MIX)]
    r = xr @ wr
    w = -jax.nn.softplus(-(w0 + jnp.tanh(xw @ w1) @ w2)) - 0.5
    k = xk @ wk
    v = xv @ wv
    if v_first is None:
        v_first = v
    else:
        v = v + (v_first - v) * jax.nn.sigmoid(v0 + (xv @ v1) @ v2)
    a = jax.nn.sigmoid(a0 + (xa @ a1) @ a2)
    g = jax.nn.sigmoid(xg @ g1) @ g2
    kk = (k * k_k).astype(f32).reshape(B, T, H, N)
    kk = kk * lax.rsqrt(jnp.maximum(jnp.sum(kk * kk, -1, keepdims=True), 1e-24))
    k = k * (1.0 + (a - 1.0) * k_a)

    def heads(u):
        return u.astype(f32).reshape(B, T, H, N)

    rf, kf, vf, af = heads(r), heads(k), heads(v), heads(a)
    decay = jnp.exp(-jnp.exp(heads(w)))
    xs = tuple(jnp.moveaxis(u, 1, 0) for u in (rf, decay, kf, vf, -kk, kk * af))
    S0 = jnp.zeros((B, H, N, N), f32)
    _, y = lax.scan(_rwkv7_step, S0, xs)
    y = jnp.moveaxis(y, 0, 1)
    mean = jnp.mean(y, -1, keepdims=True)
    var = jnp.mean(jnp.square(y - mean), -1, keepdims=True)
    y = ((y - mean) * lax.rsqrt(var + GN_EPS)).reshape(B, T, C) * lnx_w + lnx_b
    bonus = (jnp.sum(rf * kf * r_k, -1, keepdims=True) * vf).reshape(B, T, C)
    out = ((y + bonus) * g).astype(xn.dtype) @ wo
    return out, v_first

def compress_blocks(u, pe, w1, b1, w2):
    B, T, G, D = u.shape
    u16 = u.reshape(B, T // CMP_STRIDE, CMP_STRIDE, G, D)
    blocks = jnp.concatenate([u16[:, :-1], u16[:, 1:]], axis=2) + pe[None, None, :, None, :]
    flat = blocks.transpose(0, 1, 3, 2, 4).reshape(B, T // CMP_STRIDE - 1, G, CMP_LEN * D)
    return jax.nn.gelu(flat @ w1 + b1) @ w2

def nsa_shared_kv(h, kv_norm_g, w_kv, cmp_pe, cmp_w1, cmp_b1, cmp_w2):
    B, T, _ = h.shape
    G, D = NSA_GROUPS, NSA_HD
    kv = (rmsnorm(h, kv_norm_g) @ w_kv).reshape(B, T, N_KV_PARTS, G, D)
    kc = compress_blocks(kv[:, :, 0], cmp_pe[0], cmp_w1[0], cmp_b1[0], cmp_w2[0])
    vc = compress_blocks(kv[:, :, 1], cmp_pe[1], cmp_w1[1], cmp_b1[1], cmp_w2[1])
    n_s = T // SEL_BLOCK
    ks = kv[:, :, 2].reshape(B, n_s, SEL_BLOCK, G, D).transpose(0, 3, 1, 2, 4)
    vs = kv[:, :, 3].reshape(B, n_s, SEL_BLOCK, G, D).transpose(0, 3, 1, 2, 4)
    pad = ((0, 0), (WINDOW, 0), (0, 0), (0, 0))
    kw = jnp.pad(kv[:, :, 4], pad)
    vw = jnp.pad(kv[:, :, 5], pad)
    return kc, vc, ks, vs, kw, vw

def nsa_attention(hn, wq, wo, rel_bias, kc, vc, ks, vs, kw, vw):
    B, T, _ = hn.shape
    G, R, D = NSA_GROUPS, NSA_REP, NSA_HD
    f32 = jnp.float32
    n_c = kc.shape[1]
    n_s = ks.shape[2]
    top = min(SEL_TOP, n_s)
    n_qb = T // QBLK
    proj = hn @ wq
    q = (proj[..., :NSA_HEADS * D] * (D ** -0.5)).reshape(B, n_qb, QBLK, G, R, D).transpose(1, 0, 2, 3, 4, 5)
    gates = jax.nn.sigmoid(proj[..., NSA_HEADS * D:].astype(f32)).reshape(
        B, n_qb, QBLK, G, R, N_BRANCH).transpose(1, 0, 2, 3, 4, 5)
    table = rel_bias.astype(f32)
    table_g = table.reshape(REL_BUCKETS, G, R).transpose(1, 0, 2)
    cmp_end = jnp.arange(n_c) * CMP_STRIDE + (CMP_LEN - 1)
    blk_start = jnp.arange(n_s) * SEL_BLOCK
    overlap = (((cmp_end[:, None] - (CMP_LEN - 1)) <= (blk_start[None, :] + SEL_BLOCK - 1))
               & (cmp_end[:, None] >= blk_start[None, :])).astype(f32)
    b_idx = jnp.arange(B)[:, None, None, None]
    g_idx = jnp.arange(G)[None, :, None, None]
    sel_off = jnp.arange(SEL_BLOCK)

    def head_bias(dist):
        bias = table[t5_bucket(dist)]
        return bias.reshape(dist.shape + (G, R)).transpose(2, 3, 0, 1)

    def block(args):
        qb, gb, qi = args
        t = qi * QBLK + jnp.arange(QBLK)
        m_c = cmp_end[None, :] <= t[:, None]
        s_c = jnp.einsum('bqgrd,bcgd->bgrqc', qb, kc).astype(f32) + head_bias(t[:, None] - cmp_end[None, :])
        p_c = jnp.where(m_c, jax.nn.softmax(jnp.where(m_c, s_c, NEG_INF), axis=-1), 0.0)
        o_c = jnp.einsum('bgrqc,bcgd->bqgrd', p_c, vc)
        imp = jnp.einsum('bgrqc,cs->bgqs', p_c, overlap)
        blk_ok = blk_start[None, :] <= t[:, None]
        forced = (blk_start[None, :] == (t[:, None] // SEL_BLOCK) * SEL_BLOCK) | (blk_start[None, :] == 0)
        score = jnp.where(forced, SEL_FORCE, jnp.where(blk_ok, imp, -SEL_FORCE))
        _, idx = lax.top_k(score, top)
        k_sel = ks[b_idx, g_idx, idx]
        v_sel = vs[b_idx, g_idx, idx]
        dist_s = t[None, None, :, None, None] - (idx[..., None] * SEL_BLOCK + sel_off)
        m_s = dist_s >= 0
        bias_s = jnp.moveaxis(table_g[g_idx[..., None], t5_bucket(dist_s)], -1, 2)
        s_s = jnp.einsum('bqgrd,bgqkld->bgrqkl', qb, k_sel).astype(f32) + bias_s
        s_s = jnp.where(m_s[:, :, None], s_s, NEG_INF).reshape(B, G, R, QBLK, top * SEL_BLOCK)
        p_s = jax.nn.softmax(s_s, axis=-1).reshape(B, G, R, QBLK, top, SEL_BLOCK)
        o_s = jnp.einsum('bgrqkl,bgqkld->bqgrd', p_s, v_sel)
        kwb = lax.dynamic_slice_in_dim(kw, qi * QBLK, WINDOW + QBLK, axis=1)
        vwb = lax.dynamic_slice_in_dim(vw, qi * QBLK, WINDOW + QBLK, axis=1)
        kpos = qi * QBLK - WINDOW + jnp.arange(WINDOW + QBLK)
        dist_w = t[:, None] - kpos[None, :]
        m_w = (dist_w >= 0) & (dist_w < WINDOW) & (kpos[None, :] >= 0)
        s_w = jnp.einsum('bqgrd,bkgd->bgrqk', qb, kwb).astype(f32) + head_bias(dist_w)
        p_w = jax.nn.softmax(jnp.where(m_w, s_w, NEG_INF), axis=-1)
        o_w = jnp.einsum('bgrqk,bkgd->bqgrd', p_w, vwb)
        o = gb[..., 0:1] * o_c + gb[..., 1:2] * o_s + gb[..., 2:3] * o_w
        return o.astype(hn.dtype)

    out = lax.map(block, (q, gates, jnp.arange(n_qb)))
    out = out.transpose(1, 0, 2, 3, 4, 5).reshape(B, T, NSA_HEADS * D)
    return out @ wo

def setup_inputs(seed: int = 0) -> dict:
    key = jax.random.key(seed)
    keys = iter(jax.random.split(key, 48))
    f32 = jnp.float32

    def nrm(shape, scale):
        return jax.random.normal(next(keys), shape, f32) * scale

    def gain(shape):
        return 1.0 + 0.02 * jax.random.normal(next(keys), shape, f32)

    def unif(shape, lo, hi):
        return jax.random.uniform(next(keys), shape, f32, lo, hi)

    nA, nB, D = N_A_LAYERS, N_B_LAYERS, D_MODEL
    H, N = RW_HEADS, RW_HEAD
    HB, G, HD = NSA_HEADS, NSA_GROUPS, NSA_HD
    sD = D ** -0.5
    return {
        'x': nrm((BATCH, SEQ, D), 1.0),
        'a_norm_g': gain((nA, D)),
        'rw_mu': unif((nA, N_SHIFT_MIX, D), 0.0, 1.0),
        'rw_wr': nrm((nA, D, D), sD),
        'rw_wk': nrm((nA, D, D), sD),
        'rw_wv': nrm((nA, D, D), sD),
        'rw_wo': nrm((nA, D, D), 0.5 * sD),
        'rw_w0': unif((nA, D), -6.0, -1.0),
        'rw_w1': nrm((nA, D, LORA_DECAY), sD),
        'rw_w2': nrm((nA, LORA_DECAY, D), 0.1 * LORA_DECAY ** -0.5),
        'rw_a0': nrm((nA, D), 0.1),
        'rw_a1': nrm((nA, D, LORA_A), sD),
        'rw_a2': nrm((nA, LORA_A, D), 0.1 * LORA_A ** -0.5),
        'rw_v0': nrm((nA - 1, D), 0.1),
        'rw_v1': nrm((nA - 1, D, LORA_V), sD),
        'rw_v2': nrm((nA - 1, LORA_V, D), 0.1 * LORA_V ** -0.5),
        'rw_g1': nrm((nA, D, LORA_G), sD),
        'rw_g2': nrm((nA, LORA_G, D), LORA_G ** -0.5),
        'rw_kk': 0.85 + nrm((nA, D), 0.02),
        'rw_ka': gain((nA, D)),
        'rw_rk': nrm((nA, H, N), 0.1),
        'rw_lnx_w': gain((nA, D)),
        'rw_lnx_b': nrm((nA, D), 0.02),
        'kv_norm_g': gain((D,)),
        'w_kv': nrm((D, N_KV_PARTS * G * HD), sD),
        'cmp_pe': nrm((2, CMP_LEN, HD), 0.1),
        'cmp_w1': nrm((2, CMP_LEN * HD, HD), (CMP_LEN * HD) ** -0.5),
        'cmp_b1': nrm((2, HD), 0.02),
        'cmp_w2': nrm((2, HD, HD), HD ** -0.5),
        'b_norm_g': gain((nB, D)),
        'nsa_wq': nrm((nB, D, HB * HD + N_BRANCH * HB), sD),
        'nsa_wo': nrm((nB, HB * HD, D), 0.5 * (HB * HD) ** -0.5),
        'rel_bias': nrm((REL_BUCKETS, HB), 0.5),
        'm_norm_g': gain((DEPTH, D)),
        'mlp_up': nrm((DEPTH, D, D_FF), sD),
        'mlp_down': nrm((DEPTH, D_FF, D), 0.5 * D_FF ** -0.5),
        'final_norm_g': gain((D,)),
    }

def reference(x, a_norm_g, rw_mu, rw_wr, rw_wk, rw_wv, rw_wo, rw_w0, rw_w1, rw_w2,
              rw_a0, rw_a1, rw_a2, rw_v0, rw_v1, rw_v2, rw_g1, rw_g2, rw_kk, rw_ka, rw_rk,
              rw_lnx_w, rw_lnx_b, kv_norm_g, w_kv, cmp_pe, cmp_w1, cmp_b1, cmp_w2,
              b_norm_g, nsa_wq, nsa_wo, rel_bias, m_norm_g, mlp_up, mlp_down, final_norm_g):
    h = x
    v_first = None
    for layer in range(DEPTH):
        if layer < N_A_LAYERS:
            i = layer
            if i == 0:
                v0, v1, v2 = None, None, None
            else:
                v0, v1, v2 = rw_v0[i - 1], rw_v1[i - 1], rw_v2[i - 1]
            y, v_first = rwkv7_time_mix(
                rmsnorm(h, a_norm_g[i]), rw_mu[i], rw_wr[i], rw_wk[i], rw_wv[i], rw_wo[i],
                rw_w0[i], rw_w1[i], rw_w2[i], rw_a0[i], rw_a1[i], rw_a2[i], rw_g1[i], rw_g2[i],
                rw_kk[i], rw_ka[i], rw_rk[i], rw_lnx_w[i], rw_lnx_b[i], v_first, v0, v1, v2)
        else:
            j = layer - N_A_LAYERS
            if layer == N_A_LAYERS:
                kc, vc, ks, vs, kw, vw = nsa_shared_kv(h, kv_norm_g, w_kv, cmp_pe, cmp_w1, cmp_b1, cmp_w2)
            y = nsa_attention(rmsnorm(h, b_norm_g[j]), nsa_wq[j], nsa_wo[j], rel_bias,
                              kc, vc, ks, vs, kw, vw)
        h = h + y
        h = h + sqrelu_mlp(rmsnorm(h, m_norm_g[layer]), mlp_up[layer], mlp_down[layer])
    return rmsnorm(h, final_norm_g)


_drawn_inputs = setup_inputs


def setup_inputs(seed=0):
    import zlib

    import numpy as np

    out = dict(_drawn_inputs(seed))
    spreads = {}
    factors = {'a_norm_g': 5.16,
     'rw_w1': 64.0,
     'rw_w2': 64.0,
     'rw_a0': 4.43,
     'rw_a1': 4.883,
     'rw_a2': 4.812,
     'rw_kk': 64.0,
     'rw_ka': 8.0,
     'rw_lnx_w': 64.0,
     'rw_lnx_b': 64.0,
     'kv_norm_g': 64.0,
     'cmp_pe': 40.136,
     'cmp_b1': 64.0,
     'b_norm_g': 64.0,
     'm_norm_g': 28.152,
     'final_norm_g': 8.063,
     'rw_w0': 3.662,
     'cmp_w1': 3.241,
     'cmp_w2': 2.704,
     'rel_bias': 8.0}
    for name, (base, spread) in spreads.items():
        noise = np.random.default_rng([zlib.crc32(name.encode()), seed]).standard_normal(out[name].shape)
        drawn = base * np.exp(spread * noise) if base else spread * noise
        out[name] = jnp.asarray(drawn.astype(out[name].dtype))
    for name, factor in factors.items():
        out[name] = (out[name] * factor).astype(out[name].dtype)
    return out
```

```python
import math
from contextlib import ExitStack

import numpy as np
import concourse.bass as bass
from concourse import mybir

F32 = mybir.dt.float32
F32R = mybir.dt.float32r
ALU = mybir.AluOpType
ACT = mybir.ActivationFunctionType
AX = mybir.AxisListType

P = 128
D = 2048
T = 256
TT = T // P
KT = D // P
SLAB = 512
NS = D // SLAB
KC = 2
CPS = KT // KC
RING = 4
FF = 4 * D
NG = FF // D
LW, LA, LG = 96, 128, 256
NORM_EPS = 1e-6
GN_EPS = 64e-5
CH = 64
HEADS_A = 32
PAIRS = 4
NGRP = KT // PAIRS
HB, GB, HD = 16, 4, 128
REP = HB // GB
KVW = 6 * GB * HD
NCB = T // 16 - 1
BUCKETS, MAXDIST = 32, 128
NEG = -1e30
LEVELS = (2, 4, 8, 16, 32)

PARAMS = ['a_norm_g', 'mu0', 'mu1', 'mu2', 'mu3', 'mu4', 'mu5', 'rw_w0', 'rw_a0', 'rw_kk', 'rw_ka',
          'rw_rk', 'rw_lnx_w', 'rw_lnx_b', 'kv_norm_g', 'b_norm_g', 'm0', 'm1']
PROW = 6 * KT

C_ID, C_ONES, C_CAUSAL, C_LOW, C_L1, C_T1, C_LV = 0, 128, 256, 512, 640, 768, 896
C_W = C_LV + 128 * len(LEVELS)


def constants():
    c = np.zeros((P, C_W), np.float32)
    s, t = np.arange(P)[:, None], np.arange(P)[None, :]
    same = s // CH == t // CH
    c[:, C_ID:C_ID + P] = s == t
    c[:, C_ONES:C_ONES + P] = same
    c[:, C_CAUSAL:C_CAUSAL + P] = same & (s < t)
    c[:, C_CAUSAL + P:C_CAUSAL + 2 * P] = same & (s <= t)
    c[:, C_LOW:C_LOW + P] = same & (s > t)

    def level(m):
        return (s // (2 * m) == t // (2 * m)) & (s % (2 * m) < m) & (t % (2 * m) >= m)
    c[:, C_L1:C_L1 + P] = level(1).T
    c[:, C_T1:C_T1 + P] = level(1)
    for n, m in enumerate(LEVELS):
        c[:, C_LV + P * n:C_LV + P * (n + 1)] = level(m)
    return c


def constants2():
    c = np.zeros((P, 512 + TT), np.float32)
    exact = BUCKETS // 2
    for dist in range(-T + 1, T):
        n = max(dist, 0)
        if n < exact:
            b = n
        else:
            b = min(BUCKETS - 1, exact + int(np.log(np.float32(n / exact)) / math.log(MAXDIST / exact) * (BUCKETS - exact)))
        c[b, T + dist] = dist >= 0
        c[BUCKETS, T + dist] = NEG if dist < 0 else 0.0
    for tt in range(TT):
        c[:, 512 + tt] = tt * P + np.arange(P) >= 31
    return c


def build(nc, **t):
    ctx = ExitStack()
    with ctx:
        def sem(name):
            return ctx.enter_context(nc.semaphore(name))

        def at(name, addr, shape, dt=F32):
            return nc.alloc_sbuf_tensor_at(name, shape, dt, offset=addr)

        A0 = 16640
        cst = at("cst", A0, [P, C_W])
        par = at("par", A0 + 6144, [P, len(PARAMS) * KT])
        small = at("small", A0 + 7424, [P, 64])
        H_AT = A0 + 8192
        XB_AT = H_AT + 16384
        XA_AT = XB_AT + 32768
        RAW_AT = XA_AT + 32768
        WHI_AT = RAW_AT + 16384
        WORK = WHI_AT + 32768
        TOP = 229344
        LH_AT = TOP - 4096
        h = at("h", H_AT, [P, TT, D])
        xbh = at("xbh", XB_AT, [P, KT, T], F32R)
        xbl = at("xbl", XB_AT + 16384, [P, KT, T], F32R)
        xah = at("xah", XA_AT, [P, KT, T], F32R)
        xal = at("xal", XA_AT + 16384, [P, KT, T], F32R)
        raw = at("raw", RAW_AT, [P, RING, KC, SLAB])
        whi = at("whi", WHI_AT, [P, RING, KC, SLAB], F32R)
        wlo = at("wlo", WHI_AT + 16384, [P, RING, KC, SLAB], F32R)
        lora_h = at("lora_h", LH_AT, [P, 4, T])
        bank = [nc.alloc_psum_tensor(f"bank{i}", [P, 512], F32) for i in range(8)]
        rkv = nc.dram_tensor("rkv_scratch", [3, T, D], F32, kind="Internal").ap()

        ident = cst[:, C_ID:C_ID + P]

        def col(name, k):
            n = PARAMS.index(name) * KT + k
            return par[:, n:n + 1]

        raw_in = [sem(f"raw_in{i}") for i in range(RING)]
        hi_ready = sem("hi_ready")
        lo_ready = sem("lo_ready")
        w_used = sem("w_used")
        acc_free = sem("acc_free")
        stream = {'chunk': 0, 'slab': 0}

        def later(n, first):
            return not isinstance(n, int) or n > first

        def load_chunk(eng, w, G, c, k0, n0):
            if later(G, RING - 1):
                eng.wait_ge(lo_ready, G - (RING - 1))
            src = w[bass.ds(k0, KC * P), bass.ds(n0, SLAB)].rearrange("(k p) n -> p k n", p=P)
            eng.dma_start(raw[:, c % RING], src).then_inc(raw_in[c % RING], 16)

        def split_hi(act, G, uses, c):
            act.wait_ge(raw_in[c % RING], 16 * (uses + 1))
            if later(G, RING - 1):
                act.wait_ge(w_used, G - (RING - 1))
            nc.scalar.activation(whi[:, c % RING], raw[:, c % RING], ACT.Copy).then_inc(hi_ready, 1)

        def split_lo(dve, G, c):
            dve.wait_ge(hi_ready, G + 1)
            nc.vector.tensor_tensor(out=wlo[:, c % RING], in0=raw[:, c % RING],
                                    in1=whi[:, c % RING].bitcast(F32), op=ALU.subtract).then_inc(lo_ready, 1)

        def slab_matmuls(pe, G0, S, half, xh, xl, before=None):
            if later(S, 1):
                pe.wait_ge(acc_free, S - 1)
            for c in range(CPS):
                if before:
                    before(c)
                pe.wait_ge(lo_ready, G0 + c + 1)
                for j in range(KC):
                    k = c * KC + j
                    for tt in range(TT):
                        acc, tok = bank[2 * half + tt], slice(tt * P, (tt + 1) * P)
                        nc.tensor.matmul(acc[:], xh[:, k, tok], whi[:, c % RING, j], start=(k == 0), stop=False)
                        nc.tensor.matmul(acc[:], xh[:, k, tok], wlo[:, c % RING, j], start=False, stop=False)
                        last = nc.tensor.matmul(acc[:], xl[:, k, tok], whi[:, c % RING, j],
                                                start=False, stop=(k == KT - 1))
                last.then_inc(w_used, 1)

        def pe_unit(pe, unit, xh, xl, before=None):
            def step(i):
                for half in range(2):
                    slab_matmuls(pe, unit['chunk'] + 2 * CPS * i + CPS * half, unit['slab'] + 2 * i + half,
                                 half, xh, xl, before)
            n = unit['slabs'] // 2
            first = 1 if unit['slab'] == 0 else 0
            if first:
                step(0)
            if n > first:
                with pe.Fori(first, n) as i:
                    step(i)

        def sp_unit(sp, w, unit):
            def step(s):
                for c in range(CPS):
                    load_chunk(sp, w, unit['chunk'] + CPS * s + c, c, c * KC * P, s * SLAB)
            first = 1 if unit['slab'] == 0 else 0
            if first:
                step(0)
            with sp.Fori(first, unit['slabs']) as s:
                step(s)

        def new_unit(slabs):
            u = dict(stream, slabs=slabs)
            stream['chunk'] += slabs * CPS
            stream['slab'] += slabs
            return u

        xnT = at("xnT", WORK, [P, KT, T + 1])
        xs = at("xs", WORK + 16512, [P, TT, D])
        xx = at("xx", WORK + 16512, [P, KT, T])
        stage = at("stage", WORK + 32896, [P, 2, TT, SLAB])
        w1s = at("w1s", WORK + 41088, [P, KT, LW])
        a1s = at("a1s", WORK + 47232, [P, KT, LA])
        g1s = at("g1s", H_AT, [P, KT, LG])
        NMIX = 6
        mix = at("mix", WORK + 55424, [P, 2, NMIX, T])
        assert WORK + 55424 + 2 * NMIX * T * 4 <= LH_AT
        prow = at("prow", XA_AT, [PROW, 3, P])
        ss, rstd = small[:, 0:2], small[:, 2:4]
        eps_t = small[:, 4:5]

        consts_in = sem("consts_in")
        rows_in = sem("rows_in")
        x_in = sem("x_in")
        lora_in = sem("lora_in")
        par_T = sem("par_T")
        par_ready = sem("par_ready")
        eps_set = sem("eps_set")

        norm_ss, norm_var, norm_std, norm_r = sem("norm_ss"), sem("norm_var"), sem("norm_std"), sem("norm_r")
        norm_xs, norm_T = sem("norm_xs"), sem("norm_T")
        norms = {'n': 0}

        def act_norm_sum(act, n, ready, xs):
            ready(act)
            for tt in range(TT):
                last = nc.scalar.activation(xs[:, tt], h[:, tt], ACT.Square, accum_out=ss[:, tt:tt + 1])
                last.then_inc(norm_ss, 1)

        def act_norm_sqrt(act, n):
            act.wait_ge(norm_var, n + 1)
            nc.scalar.activation(rstd, rstd, ACT.Sqrt).then_inc(norm_std, 1)

        def dve_norm(dve, n, xs):
            dve.wait_ge(norm_ss, 2 * (n + 1))
            nc.vector.tensor_scalar(rstd, ss, 1.0 / D, NORM_EPS, ALU.mult, ALU.add).then_inc(norm_var, 1)
            dve.wait_ge(norm_std, n + 1)
            nc.vector.reciprocal(rstd, rstd).then_inc(norm_r, 1)
            dve.wait_ge(norm_r, n + 1)
            for tt in range(TT):
                nc.vector.tensor_scalar(xs[:, tt], h[:, tt], rstd[:, tt:tt + 1], None, ALU.mult).then_inc(norm_xs, 1)

        def pe_norm(pe, n, xs):
            pe.wait_ge(norm_xs, 2 * (n + 1))
            for b in range(8):
                for j in range(2):
                    for tt in range(TT):
                        k = 2 * b + j
                        last = nc.tensor.transpose(bank[b][:, j * T + tt * P:j * T + (tt + 1) * P],
                                                   xs[:, tt, k * P:(k + 1) * P], ident)
                last.then_inc(norm_T, 1)

        xn_ready = sem("xn_ready")
        pad_set = sem("pad_set")
        xx_ready = sem("xx_ready")
        mixed = sem("mixed")
        mix_hi = sem("mix_hi")
        mix_lo = sem("mix_lo")
        mix_used = sem("mix_used")
        lora_ready = sem("lora_ready")
        rkv_out = [sem(f"rkv_out{i}") for i in range(2)]
        units = [new_unit(NS) for _ in range(3)]
        order = ['rw_wr', 'rw_wk', 'rw_wv']
        MU = {'r': 'mu0', 'w': 'mu1', 'k': 'mu2', 'v': 'mu3', 'a': 'mu4', 'g': 'mu5'}

        with nc.Block() as block:
            @block.sync
            def _(sp):
                sp.dma_start(h[:], t['x'].rearrange("b (t p) d -> p (b t) d", p=P)).then_inc(x_in, 16)
                sp.dma_start(cst[:], t['consts']).then_inc(consts_in, 16)
                for u, name in zip(units, order):
                    sp_unit(sp, t[name][0], u)

            @block.gpsimd
            def _(pool):
                nc.gpsimd.memset(xnT[:, :, 0:1], 0.0).then_inc(pad_set, 1)
                pool.dma_start(prow[:, 0], t['par_rows'][0]).then_inc(rows_in, 16)
                pool.dma_start(prow[:, 1], t['par_rows'][1]).then_inc(rows_in, 16)
                pool.dma_start(prow[:, 2], t['par_rows'][2]).then_inc(rows_in, 16)
                pool.dma_start(w1s[:], t['rw_w1'][0].rearrange("(k p) n -> p k n", p=P)).then_inc(lora_in, 16)
                pool.dma_start(a1s[:], t['rw_a1'][0].rearrange("(k p) n -> p k n", p=P)).then_inc(lora_in, 16)
                pool.wait_ge(norm_xs, 2)
                pool.dma_start(g1s[:], t['rw_g1'][0].rearrange("(k p) n -> p k n", p=P)).then_inc(lora_in, 16)
                for n in range(3 * NS):
                    u, s = divmod(n, NS)
                    pool.wait_ge(acc_free, n + 1)
                    pool.dma_start(rkv[u].rearrange("(t p) d -> p t d", p=P)[:, :, s * SLAB:(s + 1) * SLAB],
                                   stage[:, n % 2]).then_inc(rkv_out[n % 2], 16)
                for i in range(2):
                    pool.wait_ge(rkv_out[i], 16 * (3 * NS // 2))

            def rkv_evac(act, n):
                act.wait_ge(w_used, CPS * (n + 1))
                if n >= 2:
                    act.wait_ge(rkv_out[n % 2], 16 * (n // 2))
                nc.scalar.activation(stage[:, n % 2, 0], bank[2 * (n % 2)][:], ACT.Copy)
                nc.scalar.activation(stage[:, n % 2, 1], bank[2 * (n % 2) + 1][:], ACT.Copy)\
                    .then_inc(acc_free, 1)

            @block.scalar
            def _(act):
                act_norm_sum(act, 0, lambda e: e.wait_ge(x_in, 16), xs)
                act_norm_sqrt(act, 0)
                act.wait_ge(par_ready, 1)
                for k in range(KT):
                    if k % 2 == 0:
                        act.wait_ge(norm_T, k // 2 + 1)
                    if k == 0:
                        act.wait_ge(pad_set, 1)
                    nc.scalar.activation(xnT[:, k, 1:T + 1], bank[k // 2][:, (k % 2) * T:(k % 2 + 1) * T], ACT.Copy,
                                         scale=col('a_norm_g', k)).then_inc(xn_ready, 1)
                split_hi(act, 0, 0, 0)
                for k in range(KT):
                    act.wait_ge(mixed, k + 1)
                    nc.scalar.activation(xah[:, k], mix[:, k % 2, 0], ACT.Copy).then_inc(mix_hi, 1)
                act.wait_ge(mix_used, KT)
                nc.scalar.activation(lora_h[0:LW, 0], bank[4][0:LW, 0:T], ACT.Tanh)
                nc.scalar.activation(lora_h[:, 1], bank[5][:, 0:T], ACT.Copy)
                for j in range(2):
                    last = nc.scalar.activation(lora_h[:, 2 + j], bank[6 + j][:, 0:T], ACT.Sigmoid)
                last.then_inc(lora_ready, 1)
                for G in range(1, 3 * NS * CPS):
                    c = G % CPS
                    split_hi(act, G, G // RING, c)
                    if c == 2 and G >= CPS:
                        rkv_evac(act, G // CPS - 1)
                    if G % 2 == 1 and 1 <= G // 32 + 1 <= 2:
                        n = KT * (G // 32 + 1) + (G % 32) // 2
                        act.wait_ge(mixed, n + 1)
                        xh = (xbh, xah)[G // 32]
                        nc.scalar.activation(xh[:, n % KT], mix[:, n % 2, 0], ACT.Copy).then_inc(mix_hi, 1)
                rkv_evac(act, 3 * NS - 1)

            @block.vector
            def _(dve):
                dve.wait_ge(par_T, 1)
                nc.vector.tensor_copy(par[:].rearrange("p (a n) -> p a n", a=3),
                                      bank[7][:, 0:3 * PROW].rearrange("p (a n) -> p a n", a=3)).then_inc(par_ready, 1)
                dve_norm(dve, 0, xs)
                dve.wait_ge(par_ready, 1)
                dve.wait_ge(norm_T, 8)
                for k in range(KT):
                    dve.wait_ge(xn_ready, k + 1)
                    nc.vector.tensor_tensor(out=xx[:, k], in0=xnT[:, k, 0:T], in1=xnT[:, k, 1:T + 1],
                                            op=ALU.subtract).then_inc(xx_ready, 1)

                def lo(k, n, xh, xl):
                    dve.wait_ge(mix_hi, n + 1)
                    nc.vector.tensor_tensor(out=xl[:, k], in0=mix[:, n % 2, 0], in1=xh[:, k].bitcast(F32),
                                            op=ALU.subtract).then_inc(mix_lo, 1)

                def blend(dst, k, name):
                    return nc.vector.scalar_tensor_tensor(out=dst, in0=xx[:, k], scalar=col(MU[name], k),
                                                          in1=xnT[:, k, 1:T + 1], op0=ALU.mult, op1=ALU.add)
                for k in range(KT):
                    dve.wait_ge(xx_ready, k + 1)
                    if k >= 2:
                        dve.wait_ge(mix_used, k - 1)
                    if k >= 2:
                        dve.wait_ge(mix_lo, k - 1)
                    for j, name in enumerate('rwag'):
                        last = blend(mix[:, k % 2, j], k, name)
                    last.then_inc(mixed, 1)
                    if k:
                        lo(k - 1, k - 1, xah, xal)
                lo(KT - 1, KT - 1, xah, xal)
                for G in range(3 * NS * CPS):
                    c = G % CPS
                    split_lo(dve, G, c)
                    if G % 2 == 0 and G // 32 < 2:
                        k = (G % 32) // 2
                        n = KT * (G // 32 + 1) + k
                        if n == KT:
                            dve.wait_ge(mix_used, KT)
                        dve.wait_ge(mix_lo, n - 1)
                        blend(mix[:, n % 2, 0], k, 'kv'[G // 32]).then_inc(mixed, 1)
                        if G // 32 == 1 and k == 0:
                            dve.wait_ge(w_used, NS * CPS)
                    if G % 2 == 1 and G // 32 < 2:
                        k = (G % 32) // 2
                        xh, xl = ((xbh, xbl), (xah, xal))[G // 32]
                        lo(k, KT * (G // 32 + 1) + k, xh, xl)

            @block.tensor
            def _(pe):
                pe.wait_ge(consts_in, 16)
                pe.wait_ge(rows_in, 48)
                for a in range(3):
                    last = nc.tensor.transpose(bank[7][:, a * PROW:(a + 1) * PROW], prow[:, a], ident[0:PROW, 0:PROW])
                last.then_inc(par_T, 1)
                pe.wait_ge(par_ready, 1)
                pe_norm(pe, 0, xs)
                pe.wait_ge(lora_in, 48)
                pe.wait_ge(xn_ready, KT)
                for k in range(KT):
                    pe.wait_ge(mixed, k + 1)
                    first, end = k == 0, k == KT - 1
                    nc.tensor.matmul(bank[4][0:LW, 0:T], w1s[:, k], mix[:, k % 2, 1], start=first, stop=end)
                    nc.tensor.matmul(bank[5][:, 0:T], a1s[:, k], mix[:, k % 2, 2], start=first, stop=end)
                    for j in range(2):
                        last = nc.tensor.matmul(bank[6 + j][:, 0:T], g1s[:, k, j * P:(j + 1) * P], mix[:, k % 2, 3],
                                                start=first, stop=end)
                    last.then_inc(mix_used, 1)
                for u, (xh, xl), n in zip(units, ((xah, xal), (xbh, xbl), (xah, xal)), (1, 2, 3)):
                    pe.wait_ge(mix_lo, KT * n)
                    pe_unit(pe, u, xh, xl)


        cursor = [XA_AT]

        def place(name, shape, dt=F32):
            n = 4 * math.prod(shape[1:])
            cursor[0] += n
            assert cursor[0] <= LH_AT
            return at(name, cursor[0] - n, shape, dt)

        UN = 2 * PAIRS * TT
        NCH = T // CH
        rkvg = at("rkvg", H_AT, [P, 3, TT, SLAB])
        gp = at("gp", H_AT + 12288, [P, 8, PAIRS])
        zeros = at("zeros", H_AT + 12416, [P, CH])
        rT, kT, vT, gT, dec, aT, nkk, tmp = (place(n, [P, PAIRS, T]) for n in
                                             ("rT", "kT", "vT", "gT", "dec", "aT", "nkk", "tmp"))
        prod = place("prod", [P, PAIRS * NCH, CH + 1])
        ipr = place("ipr", [P, PAIRS, T])
        ar = place("ar", [P, PAIRS, TT, 2, P])
        bt, kt_ = place("bt", [P, PAIRS, T]), place("kt_", [P, PAIRS, T])
        bh, kh = place("bh", [P, TT, SLAB]), place("kh", [P, TT, SLAB])
        Lm, X, XT, Z = (place(n, [P, UN, P]) for n in ("Lm", "X", "XT", "Z"))
        mk = place("mk", [P, UN, 2, P])
        rbt = place("rbt", [P, UN, P])
        sd = place("sd", [P, PAIRS, 2, CH])
        sp_ = place("sp_", [P, PAIRS, CH])
        w1b, sab = place("w1b", [P, SLAB]), place("sab", [P, SLAB])
        w2g, a2g, g2g = place("w2g", [LW, SLAB]), place("a2g", [P, SLAB]), place("g2g", [P, 2, SLAB])
        yT, dT = rT, kT
        lnw, lnb = 5, 6

        def unit(h, pair, tt):
            return h * 8 + pair * 2 + tt

        rkvg_in = sem("rkvg_in")
        l2_in = sem("l2_in")
        grp_done = sem("grp_done")
        zero_set = sem("zero_set")
        sd_zero = sem("sd_zero")
        gp_ready = sem("gp_ready")
        tr_ps = sem("tr_ps")
        r_ready, k_ready, v_ready = sem("r_ready"), sem("k_ready"), sem("v_ready")
        l2_ps = sem("l2_ps")
        w_sig, a_ready, g_ready, dec_ready = sem("w_sig"), sem("a_ready"), sem("g_ready"), sem("dec_ready")
        kk_raw, kk_sq, kk_ps, kk_max, kk_std = sem("kk_raw"), sem("kk_sq"), sem("kk_ps"), sem("kk_max"), sem("kk_std")
        bon_ready, bon_ps = sem("bon_ready"), sem("bon_ps")
        factors = sem("factors")
        s3_ps = sem("s3_ps")
        s3_read = sem("s3_read")
        l_ps, l_ready = sem("l_ps"), sem("l_ready")
        x0_ready = sem("x0_ready")
        z_ps, z_ready, x_ps, x_ready = sem("z_ps"), sem("z_ready"), sem("x_ps"), sem("x_ready")
        hat_ready, hat_ps, hat_read = sem("hat_ready"), sem("hat_ps"), sem("hat_read")
        w1_ps, w1_ready, sa_ps, sa_ready = sem("w1_ps"), sem("w1_ready"), sem("sa_ps"), sem("sa_ready")
        s_ps, s_ready, y_ps, y_ready = sem("s_ps"), sem("s_ready"), sem("y_ps"), sem("y_ready")
        mean_ps, d_ready, d_sq, var_ps, var_ready, std_ready = (sem(n) for n in (
            "mean_ps", "d_ready", "d_sq", "var_ps", "var_ready", "std_ready"))
        o_ready, o_hi = sem("o_ready"), sem("o_hi")
        dlink = sem("dlink")
        DL = 16
        NLV = len(LEVELS)

        def bc(ap, n):
            return ap.unsqueeze(1).to_broadcast([ap.shape[0], n, ap.shape[-1]])

        with nc.Block() as block:
            @block.sync
            def _(sp):
                with sp.Fori(0, NGRP) as g:
                    sp.wait_ge(grp_done, g + 1)
                    cols = bass.ds(g * SLAB, SLAB)
                    for u in range(3):
                        sp.dma_start(rkvg[:, u], rkv[u].rearrange("(t p) d -> p t d", p=P)[:, :, cols])\
                            .then_inc(rkvg_in, 16)
                    sp.dma_start(w2g[:], t['rw_w2'][0][:, cols]).then_inc(l2_in, 16)
                    sp.dma_start(a2g[:], t['rw_a2'][0][:, cols]).then_inc(l2_in, 16)
                    sp.dma_start(g2g[:], t['rw_g2'][0].rearrange("(k p) n -> p k n", p=P)[:, :, cols])\
                        .then_inc(l2_in, 16)

            @block.gpsimd
            def _(pool):
                nc.gpsimd.memset(prod[:, :, 0:1], 1.0)
                nc.gpsimd.memset(sab[:], 0.0)
                nc.gpsimd.memset(w1b[:], 0.0)
                nc.gpsimd.memset(zeros[:], 0.0).then_inc(zero_set, 1)
                with pool.Fori(0, NGRP) as g:
                    pool.wait_ge(grp_done, g + 1)
                    for q in range(4):
                        us = slice(4 * q, 4 * q + 4)
                        pool.wait_ge(l_ready, g * 4 + q + 1)
                        nc.gpsimd.tensor_tensor(out=X[:, us], in0=Lm[:, us], in1=bc(cst[:, C_L1:C_L1 + P], 4),
                                                op=ALU.mult).then_inc(x0_ready, 1)
                        pool.wait_ge(x0_ready, g * 8 + 2 * q + 1)
                        nc.gpsimd.tensor_tensor(out=XT[:, us], in0=XT[:, us], in1=bc(ident, 4), op=ALU.add)
                        nc.gpsimd.tensor_tensor(out=X[:, us], in0=X[:, us], in1=bc(ident, 4),
                                                op=ALU.add).then_inc(x0_ready, 1)

            @block.scalar
            def _(act):
                flat = lambda b: b[:].rearrange("p a n -> p (a n)")
                with act.Fori(0, NGRP) as g:
                    act.wait_ge(tr_ps, g * 3 + 1)
                    for j in range(2):
                        last = nc.scalar.activation(flat(rT)[:, j * 512:(j + 1) * 512], bank[j][:], ACT.Copy)
                    last.then_inc(r_ready, 1)
                    act.wait_ge(tr_ps, g * 3 + 3)
                    for j in range(2):
                        last = nc.scalar.activation(flat(vT)[:, j * 512:(j + 1) * 512], bank[4 + j][:], ACT.Copy)
                    last.then_inc(v_ready, 1)
                    act.wait_ge(gp_ready, g + 1)
                    act.wait_ge(l2_ps, g * 3 + 1)
                    for p in range(PAIRS):
                        last = nc.scalar.activation(dec[:, p], bank[6 + p // 2][:, (p % 2) * T:(p % 2 + 1) * T],
                                                    ACT.Sigmoid, bias=gp[:, 0, p:p + 1])
                    last.then_inc(w_sig, 1)
                    act.wait_ge(l2_ps, g * 3 + 2)
                    for p in range(PAIRS):
                        last = nc.scalar.activation(aT[:, p], bank[p // 2][:, (p % 2) * T:(p % 2 + 1) * T],
                                                    ACT.Sigmoid, bias=gp[:, 1, p:p + 1])
                    last.then_inc(a_ready, 1)
                    act.wait_ge(w_sig, g + 1)
                    nc.scalar.activation(dec[:], dec[:], ACT.Exp, scale=-math.exp(-0.5)).then_inc(dec_ready, 1)
                    act.wait_ge(kk_raw, g + 1)
                    nc.scalar.activation(tmp[:], nkk[:], ACT.Square).then_inc(kk_sq, 1)
                    act.wait_ge(l2_ps, g * 3 + 3)
                    for j in range(2):
                        last = nc.scalar.activation(flat(gT)[:, j * 512:(j + 1) * 512], bank[2 + j][:], ACT.Copy)
                    last.then_inc(g_ready, 1)
                    act.wait_ge(kk_max, g + 1)
                    nc.scalar.activation(tmp[:], tmp[:], ACT.Sqrt).then_inc(kk_std, 1)
                    for tt in range(TT):
                        act.wait_ge(hat_ps, g * 2 + tt + 1)
                        nc.scalar.activation(bh[:, tt], bank[tt][:], ACT.Copy)
                        nc.scalar.activation(kh[:, tt], bank[2 + tt][:], ACT.Copy).then_inc(hat_read, 1)
                    for c in range(NCH):
                        rows = slice(CH * (c % 2), CH * (c % 2) + CH)
                        act.wait_ge(w1_ps, g * NCH + c + 1)
                        nc.scalar.activation(w1b[rows], bank[4][rows], ACT.Copy).then_inc(w1_ready, 1)
                        act.wait_ge(y_ps, g * NCH + c + 1)
                        nc.scalar.activation(yT[:, :, c * CH:(c + 1) * CH],
                                             bank[6 + c % 2][:, 0:PAIRS * CH].rearrange("p (a n) -> p a n", n=CH),
                                             ACT.Copy).then_inc(y_ready, 1)
                    act.wait_ge(d_ready, g + 1)
                    nc.scalar.activation(tmp[:], dT[:], ACT.Square).then_inc(d_sq, 1)
                    act.wait_ge(var_ready, g + 1)
                    nc.scalar.activation(tmp[:], tmp[:], ACT.Sqrt).then_inc(std_ready, 1)
                    act.wait_ge(o_ready, g + 1)
                    nc.scalar.activation(xbh[:, bass.ds(g * PAIRS, PAIRS)], dT[:], ACT.Copy).then_inc(o_hi, 1)

            @block.vector
            def _(dve):
                links = [0]
                flat = lambda b: b[:].rearrange("p a n -> p (a n)")
                parv = par[:].rearrange("p (a k) -> p a k", k=KT)
                first_p = PARAMS.index('rw_w0')
                chunked = lambda b: b[:].rearrange("p a (c n) -> p (a c) n", n=CH)
                tiled = lambda x: ar[:, :, :, x].rearrange("p a t (c n) -> p (a t) c n", n=CH)
                tile3 = lambda b: b[:].rearrange("p a (t c n) -> p (a t) c n", t=TT, n=CH)
                pr3 = prod[:].rearrange("p (a c) n -> p a c n", c=2)
                nc.vector.memset(yT[:, 0, 0:1], 0.0).then_inc(grp_done, 1)
                with dve.Fori(0, NGRP) as g:
                    def link(ins):
                        links[0] += 1
                        ins.then_inc(dlink, 1)
                        dve.wait_ge(dlink, g * DL + links[0])

                    dve.wait_ge(grp_done, g + 1)
                    link(nc.vector.tensor_copy(gp[:, 0:7], parv[:, first_p:first_p + 7, bass.ds(g * PAIRS, PAIRS)]))
                    nc.vector.memset(sd[:], 0.0).then_inc(sd_zero, 1)
                    nc.vector.tensor_scalar(gp[:, 7], gp[:, 3], -1.0, 1.0, ALU.mult, ALU.add).then_inc(gp_ready, 1)
                    dve.wait_ge(tr_ps, g * 3 + 2)
                    for j in range(2):
                        last = nc.vector.tensor_copy(flat(kT)[:, j * 512:(j + 1) * 512], bank[2 + j][:])
                    last.then_inc(k_ready, 1)
                    dve.wait_ge(k_ready, g + 1)
                    for p in range(PAIRS):
                        last = nc.vector.tensor_scalar(nkk[:, p], kT[:, p], gp[:, 2, p:p + 1], None, ALU.mult)
                    last.then_inc(kk_raw, 1)
                    dve.wait_ge(gp_ready, g + 1)
                    dve.wait_ge(a_ready, g + 1)
                    for p in range(PAIRS):
                        last = nc.vector.tensor_scalar(ipr[:, p], aT[:, p], gp[:, 3, p:p + 1], gp[:, 7, p:p + 1],
                                                       ALU.mult, ALU.add)
                    link(last)
                    link(nc.vector.tensor_tensor(out=kT[:], in0=kT[:], in1=ipr[:], op=ALU.mult))
                    dve.wait_ge(dec_ready, g + 1)
                    dve.wait_ge(zero_set, 1)
                    for n in range(PAIRS * NCH):
                        last = nc.vector.tensor_tensor_scan(prod[:, n, 1:CH + 1], chunked(dec)[:, n], zeros[:], 1.0,
                                                            ALU.mult, ALU.add)
                    link(last)
                    link(nc.vector.reciprocal(chunked(ipr), prod[:, :, 1:CH + 1]))
                    dve.wait_ge(r_ready, g + 1)
                    nc.vector.tensor_tensor(out=tiled(1), in0=tile3(rT), in1=pr3[:, :, :, 1:CH + 1], op=ALU.mult)
                    nc.vector.tensor_tensor(out=kt_[:], in0=kT[:], in1=ipr[:], op=ALU.mult)
                    for p in range(PAIRS):
                        last = nc.vector.scalar_tensor_tensor(out=dec[:, p], in0=rT[:, p], scalar=gp[:, 4, p:p + 1],
                                                              in1=kT[:, p], op0=ALU.mult, op1=ALU.mult)
                    last.then_inc(bon_ready, 1)
                    dve.wait_ge(kk_ps, g + 1)
                    for j in range(2):
                        last = nc.vector.tensor_scalar(flat(tmp)[:, j * 512:(j + 1) * 512], bank[4 + j][:], 1e-24, None,
                                                       ALU.max)
                    last.then_inc(kk_max, 1)
                    dve.wait_ge(kk_std, g + 1)
                    link(nc.vector.reciprocal(tmp[:], tmp[:]))
                    link(nc.vector.scalar_tensor_tensor(out=nkk[:], in0=nkk[:], scalar=-1.0, in1=tmp[:],
                                                        op0=ALU.mult, op1=ALU.mult))
                    nc.vector.tensor_tensor(out=tiled(0), in0=tile3(nkk), in1=pr3[:, :, :, 0:CH], op=ALU.mult)
                    link(nc.vector.scalar_tensor_tensor(out=bt[:], in0=nkk[:], scalar=-1.0, in1=aT[:],
                                                        op0=ALU.mult, op1=ALU.mult))
                    nc.vector.tensor_tensor(out=bt[:], in0=bt[:], in1=ipr[:], op=ALU.mult).then_inc(factors, 1)
                    dve.wait_ge(bon_ps, g + 1)
                    dve.wait_ge(v_ready, g + 1)
                    for j in range(2):
                        last = nc.vector.tensor_tensor(out=flat(vT)[:, j * 512:(j + 1) * 512],
                                                       in0=flat(vT)[:, j * 512:(j + 1) * 512], in1=bank[6 + j][:],
                                                       op=ALU.mult)
                    link(last)
                    for h_ in range(2):
                        for p in range(PAIRS):
                            j = h_ * PAIRS + p
                            dve.wait_ge(s3_ps, g * 8 + j + 1)
                            u = unit(h_, p, 0)
                            ps = bank[j % 2][:].rearrange("p (t n) -> p t n", t=2)
                            nc.vector.tensor_tensor(out=XT[:, u:u + 2], in0=ps[:, :, 0:P],
                                                    in1=bc(cst[:, C_T1:C_T1 + P], 2), op=ALU.mult)
                            nc.vector.tensor_tensor(out=rbt[:, u:u + 2], in0=ps[:, :, P:2 * P],
                                                    in1=bc(cst[:, C_CAUSAL + P:C_CAUSAL + 2 * P], 2), op=ALU.mult)
                            nc.vector.tensor_tensor(
                                out=mk[:, u:u + 2].rearrange("p t x n -> p t (x n)"),
                                in0=bank[2 + j % 2][:].rearrange("p (t n) -> p t n", t=2),
                                in1=bc(cst[:, C_CAUSAL:C_CAUSAL + 2 * P], 2), op=ALU.mult).then_inc(s3_read, 1)
                            if p % 2:
                                q = j // 2
                                dve.wait_ge(l_ps, g * 4 + q + 1)
                                nc.vector.tensor_tensor(out=Lm[:, 4 * q:4 * q + 4],
                                                        in0=bank[4 + q % 2][:].rearrange("p (t n) -> p t n", t=4),
                                                        in1=bc(cst[:, C_LOW:C_LOW + P], 4),
                                                        op=ALU.mult).then_inc(l_ready, 1)
                    dve.wait_ge(s3_ps, g * 8 + 8)
                    pc = prod[:, :, CH:CH + 1].to_broadcast([P, PAIRS * NCH, CH])
                    nc.vector.tensor_tensor(out=chunked(kt_), in0=chunked(kt_), in1=pc, op=ALU.mult)
                    nc.vector.tensor_tensor(out=chunked(bt), in0=chunked(bt), in1=pc, op=ALU.mult)\
                        .then_inc(hat_ready, 1)
                    for n in range(NLV):
                        mask = cst[:, C_LV + P * n:C_LV + P * (n + 1)]
                        for q in range(4):
                            dve.wait_ge(z_ps, g * 4 * NLV + 4 * n + q + 1)
                            nc.vector.tensor_tensor(out=Z[:, 4 * q:4 * q + 4],
                                                    in0=bank[q][:].rearrange("p (t n) -> p t n", t=4),
                                                    in1=bc(mask, 4), op=ALU.mult).then_inc(z_ready, 1)
                        for q in range(4):
                            dve.wait_ge(x_ps, g * 4 * NLV + 4 * n + q + 1)
                            us = slice(4 * q, 4 * q + 4)
                            if n < NLV - 1:
                                nc.vector.tensor_tensor(out=X[:, us], in0=X[:, us], op=ALU.add,
                                                        in1=bank[6 + q % 2][:].rearrange("p (t n) -> p t n", t=4))
                            nc.vector.tensor_tensor(out=XT[:, us], in0=XT[:, us], op=ALU.add,
                                                    in1=bank[4 + q % 2][:].rearrange("p (t n) -> p t n", t=4))\
                                .then_inc(x_ready, 1)
                    for c in range(NCH):
                        rows = slice(CH * (c % 2), CH * (c % 2) + CH)
                        if c < NCH - 1:
                            if c == 0:
                                dve.wait_ge(sd_zero, g + 1)
                            for h_ in range(2):
                                hr = slice(CH * h_, CH * h_ + CH)
                                pr = prod[hr].rearrange("p (a c) n -> p a c n", c=NCH)[:, :, c, CH:CH + 1]
                                last = nc.vector.tensor_tensor(out=sp_[hr], in0=sd[hr, :, h_],
                                                               in1=pr.to_broadcast([CH, PAIRS, CH]), op=ALU.mult)
                            link(last)
                        dve.wait_ge(sa_ps, g * NCH + c + 1)
                        nc.vector.tensor_copy(sab[rows], bank[5][rows]).then_inc(sa_ready, 1)
                        if c < NCH - 1:
                            dve.wait_ge(s_ps, g * (NCH - 1) + c + 1)
                            for h_ in range(2):
                                hr = slice(CH * h_, CH * h_ + CH)
                                last = nc.vector.tensor_tensor(
                                    out=sd[hr, :, h_], in0=sp_[hr],
                                    in1=bank[0][hr, 0:PAIRS * CH].rearrange("p (a n) -> p a n", n=CH), op=ALU.add)
                            last.then_inc(s_ready, 1)
                            dve.wait_ge(s_ready, g * (NCH - 1) + c + 1)
                    dve.wait_ge(mean_ps, g + 1)
                    dve.wait_ge(y_ready, g * NCH + NCH)
                    for j in range(2):
                        half = slice(j * 512, (j + 1) * 512)
                        last = nc.vector.scalar_tensor_tensor(out=flat(dT)[:, half], in0=bank[1 + j][:],
                                                              scalar=-1.0 / CH, in1=flat(yT)[:, half],
                                                              op0=ALU.mult, op1=ALU.add)
                    last.then_inc(d_ready, 1)
                    dve.wait_ge(var_ps, g + 1)
                    for j in range(2):
                        last = nc.vector.tensor_scalar(flat(tmp)[:, j * 512:(j + 1) * 512], bank[3 + j][:], 1.0 / CH,
                                                       GN_EPS, ALU.mult, ALU.add)
                    last.then_inc(var_ready, 1)
                    dve.wait_ge(std_ready, g + 1)
                    link(nc.vector.reciprocal(tmp[:], tmp[:]))
                    link(nc.vector.tensor_tensor(out=dT[:], in0=dT[:], in1=tmp[:], op=ALU.mult))
                    for p in range(PAIRS):
                        last = nc.vector.tensor_scalar(dT[:, p], dT[:, p], gp[:, lnw, p:p + 1], gp[:, lnb, p:p + 1],
                                                       ALU.mult, ALU.add)
                    link(last)
                    link(nc.vector.tensor_tensor(out=dT[:], in0=dT[:], in1=vT[:], op=ALU.add))
                    dve.wait_ge(g_ready, g + 1)
                    nc.vector.tensor_tensor(out=dT[:], in0=dT[:], in1=gT[:], op=ALU.mult).then_inc(o_ready, 1)
                    dve.wait_ge(o_hi, g + 1)
                    nc.vector.tensor_tensor(out=xbl[:, bass.ds(g * PAIRS, PAIRS)], in0=dT[:],
                                            in1=xbh[:, bass.ds(g * PAIRS, PAIRS)].bitcast(F32),
                                            op=ALU.subtract).then_inc(grp_done, 1)
                assert links[0] == DL, links[0]

            @block.tensor
            def _(pe):
                ones = cst[:, C_ONES:C_ONES + P]

                def head_sums(x, b0, done):
                    for j in range(2):
                        last = nc.tensor.matmul(bank[b0 + j][:], ones, x[:].rearrange("p a n -> p (a n)")[:, j * 512:(j + 1) * 512],
                                                start=True, stop=True)
                    last.then_inc(done, 1)
                with pe.Fori(0, NGRP) as g:
                    pe.wait_ge(grp_done, g + 1)
                    pe.wait_ge(rkvg_in, 16 * (g * 3 + 3))
                    for u in range(3):
                        for p in range(PAIRS):
                            for tt in range(TT):
                                last = nc.tensor.transpose(
                                    bank[2 * u + p // 2][:, (p % 2) * T + tt * P:(p % 2) * T + (tt + 1) * P],
                                    rkvg[:, u, tt, p * P:(p + 1) * P], ident)
                        last.then_inc(tr_ps, 1)
                    pe.wait_ge(l2_in, 16 * (g * 3 + 3))
                    for p in range(PAIRS):
                        last = nc.tensor.matmul(bank[6 + p // 2][:, (p % 2) * T:(p % 2 + 1) * T],
                                                w2g[:, p * P:(p + 1) * P], lora_h[0:LW, 0], start=True, stop=True)
                    last.then_inc(l2_ps, 1)
                    pe.wait_ge(r_ready, g + 1)
                    for p in range(PAIRS):
                        last = nc.tensor.matmul(bank[p // 2][:, (p % 2) * T:(p % 2 + 1) * T],
                                                a2g[:, p * P:(p + 1) * P], lora_h[:, 1], start=True, stop=True)
                    last.then_inc(l2_ps, 1)
                    pe.wait_ge(k_ready, g + 1)
                    for p in range(PAIRS):
                        for j in range(2):
                            last = nc.tensor.matmul(bank[2 + p // 2][:, (p % 2) * T:(p % 2 + 1) * T],
                                                    g2g[:, j, p * P:(p + 1) * P], lora_h[:, 2 + j],
                                                    start=(j == 0), stop=(j == 1))
                    last.then_inc(l2_ps, 1)
                    pe.wait_ge(kk_sq, g + 1)
                    pe.wait_ge(v_ready, g + 1)
                    head_sums(tmp, 4, kk_ps)
                    pe.wait_ge(bon_ready, g + 1)
                    pe.wait_ge(w_sig, g + 1)
                    head_sums(dec, 6, bon_ps)
                    pe.wait_ge(factors, g + 1)
                    pe.wait_ge(g_ready, g + 1)
                    pe.wait_ge(a_ready, g + 1)
                    for h_ in range(2):
                        hr = slice(CH * h_, CH * h_ + CH)
                        for p in range(PAIRS):
                            j = h_ * PAIRS + p
                            if j >= 2:
                                pe.wait_ge(s3_read, g * 8 + j - 1)
                            for x, b0 in ((bt, 0), (kt_, 2)):
                                for tt in range(TT):
                                    last = nc.tensor.matmul(bank[b0 + j % 2][:, tt * T:(tt + 1) * T],
                                                            x[hr, p, tt * P:(tt + 1) * P],
                                                            ar[hr, p, tt].rearrange("p x n -> p (x n)"),
                                                            start=True, stop=True)
                            last.then_inc(s3_ps, 1)
                            q = j // 2
                            if p % 2 == 0 and q >= 2:
                                pe.wait_ge(l_ready, g * 4 + q - 1)
                            for tt in range(TT):
                                last = nc.tensor.matmul(bank[4 + q % 2][:, (p % 2) * T + tt * P:(p % 2) * T + (tt + 1) * P],
                                                        ar[hr, p, tt, 0], bt[hr, p, tt * P:(tt + 1) * P],
                                                        start=True, stop=True)
                            if p % 2:
                                last.then_inc(l_ps, 1)
                    pe.wait_ge(s3_read, g * 8 + 8)
                    for n in range(NLV):
                        for q in range(4):
                            if n == 0:
                                pe.wait_ge(x0_ready, g * 8 + 2 * q + 2)
                            else:
                                pe.wait_ge(x_ready, g * 4 * NLV + 4 * (n - 1) + q + 1)
                            for k in range(4):
                                u = 4 * q + k
                                last = nc.tensor.matmul(bank[q][:, k * P:(k + 1) * P], Lm[:, u], XT[:, u],
                                                        start=True, stop=True)
                            last.then_inc(z_ps, 1)
                        for q in range(4):
                            pe.wait_ge(z_ready, g * 4 * NLV + 4 * n + q + 1)
                            if q >= 2:
                                pe.wait_ge(x_ready, g * 4 * NLV + 4 * n + q - 1)
                            for k in range(4):
                                u = 4 * q + k
                                last = nc.tensor.matmul(bank[4 + q % 2][:, k * P:(k + 1) * P], X[:, u], Z[:, u],
                                                        start=True, stop=True)
                                if n < NLV - 1:
                                    last = nc.tensor.matmul(bank[6 + q % 2][:, k * P:(k + 1) * P], Z[:, u], X[:, u],
                                                            start=True, stop=True)
                            last.then_inc(x_ps, 1)
                    pe.wait_ge(hat_ready, g + 1)
                    for tt in range(TT):
                        for p in range(PAIRS):
                            nc.tensor.transpose(bank[tt][:, p * P:(p + 1) * P], bt[:, p, tt * P:(tt + 1) * P], ident)
                        for p in range(PAIRS):
                            last = nc.tensor.transpose(bank[2 + tt][:, p * P:(p + 1) * P],
                                                       kt_[:, p, tt * P:(tt + 1) * P], ident)
                        last.then_inc(hat_ps, 1)
                    pe.wait_ge(x_ready, (g + 1) * 4 * NLV)
                    pe.wait_ge(sd_zero, g + 1)
                    pe.wait_ge(hat_read, g * 2 + 2)
                    for c in range(NCH):
                        tt, half = divmod(c, 2)
                        rows = slice(CH * half, CH * half + CH)
                        v_of = lambda p, h_: rkvg[:, 2, tt, p * P + h_ * CH:p * P + (h_ + 1) * CH]
                        if c:
                            pe.wait_ge(s_ready, g * (NCH - 1) + c)
                        for p in range(PAIRS):
                            nc.tensor.matmul(bank[4][rows, p * P:(p + 1) * P], ar[:, p, tt, 0, rows],
                                             sd[:, p].rearrange("p x n -> p (x n)"), start=True, stop=False)
                            for h_ in range(2):
                                last = nc.tensor.matmul(bank[4][rows, p * P + h_ * CH:p * P + (h_ + 1) * CH],
                                                        mk[:, unit(h_, p, tt), 0, rows], v_of(p, h_),
                                                        start=False, stop=(h_ == 1))
                        last.then_inc(w1_ps, 1)
                        if c >= 2:
                            pe.wait_ge(y_ready, g * NCH + c - 1)
                        for p in range(PAIRS):
                            yb = bank[6 + c % 2]
                            nc.tensor.matmul(yb[:, p * CH:(p + 1) * CH], sd[:, p].rearrange("p x n -> p (x n)"),
                                             ar[:, p, tt, 1, rows], start=(p == 0), stop=False, skip_group_check=True)
                            for h_ in range(2):
                                nc.tensor.matmul(yb[h_ * CH:(h_ + 1) * CH, p * CH:(p + 1) * CH], v_of(p, h_),
                                                 mk[:, unit(h_, p, tt), 1, rows], start=False, stop=False,
                                                 skip_group_check=True)
                        pe.wait_ge(w1_ready, g * NCH + c + 1)
                        for p in range(PAIRS):
                            for h_ in range(2):
                                cs = slice(p * P + h_ * CH, p * P + (h_ + 1) * CH)
                                last = nc.tensor.matmul(bank[5][rows, cs], XT[:, unit(h_, p, tt), rows],
                                                        w1b[:, cs], start=True, stop=True)
                        last.then_inc(sa_ps, 1)
                        pe.wait_ge(sa_ready, g * NCH + c + 1)
                        def y_sa(p, h_):
                            cs = slice(p * P + h_ * CH, p * P + (h_ + 1) * CH)
                            return nc.tensor.matmul(bank[6 + c % 2][h_ * CH:(h_ + 1) * CH, p * CH:(p + 1) * CH],
                                                    sab[:, cs], rbt[:, unit(h_, p, tt), rows], start=False,
                                                    stop=(p == PAIRS - 1), skip_group_check=True)
                        y_sa(0, 0)
                        if c < NCH - 1:
                            for p in range(PAIRS):
                                for h_ in range(2):
                                    cs = slice(p * P + h_ * CH, p * P + (h_ + 1) * CH)
                                    out = bank[0][h_ * CH:(h_ + 1) * CH, p * CH:(p + 1) * CH]
                                    nc.tensor.matmul(out, bh[rows, tt, cs], sab[rows, cs], start=True, stop=False)
                                    last = nc.tensor.matmul(out, kh[rows, tt, cs], rkvg[rows, 2, tt, cs],
                                                            start=False, stop=True)
                            last.then_inc(s_ps, 1)
                        for p in range(PAIRS):
                            for h_ in range(2):
                                if p or h_:
                                    last = y_sa(p, h_)
                        last.then_inc(y_ps, 1)
                    pe.wait_ge(y_ready, g * NCH + NCH)
                    head_sums(yT, 1, mean_ps)
                    pe.wait_ge(d_sq, g + 1)
                    head_sums(tmp, 3, var_ps)

        xs2 = at("xs2", WORK, [P, TT, D])
        u_ = at("u_", WORK + 16384, [P, 2, TT, SLAB])
        u2 = at("u2", WORK + 24576, [P, 2, TT, SLAB])
        kvs = at("kvs", WORK + 16384, [P, TT, 6, SLAB])
        qs = at("qs", WORK + 40960, [P, TT, D])
        gw = at("gw", WORK + 57344, [P, KT, 48])
        gwh = at("gwh", WORK + 60416, [P, KT, 48], F32R)
        gwl = at("gwl", WORK + 63488, [P, KT, 48], F32R)
        gates = at("gates", WORK + 66560, [P, TT, 48])

        h_in = sem("h_in")
        norm_hi, norm_lo = sem("norm_hi"), sem("norm_lo")
        sq_ready, hT_ps, hT_hi, hT_lo = sem("sq_ready"), sem("hT_ps"), sem("hT_hi"), sem("hT_lo")
        h_done = sem("h_done")
        gw_in, gw_hi, gw_lo, gate_ps = sem("gw_in"), sem("gw_hi"), sem("gw_lo"), sem("gate_ps")
        splits = {'n': 0}
        HPG = NS * 2
        CPG = HPG * CPS

        def act_split_norm(act, n, base, name, xh, again=False):
            for k in range(KT):
                act.wait_ge(norm_T, 8 * n + k // 2 + 1)
                if again:
                    act.wait_ge(norm_lo, base - KT + (k | 1) + 1)
                nc.scalar.activation(xh[:, k], bank[k // 2][:, (k % 2) * T:(k % 2 + 1) * T], ACT.Copy,
                                     scale=col(name, k)).then_inc(norm_hi, 1)

        def dve_split_norm(dve, base, name, xh, xl):
            for k in range(KT):
                dve.wait_ge(norm_hi, base + (k | 1) + 1)
                nc.vector.scalar_tensor_tensor(out=xl[:, k], in0=bank[k // 2][:, (k % 2) * T:(k % 2 + 1) * T],
                                               scalar=col(name, k), in1=xh[:, k].bitcast(F32),
                                               op0=ALU.mult, op1=ALU.subtract).then_inc(norm_lo, 1)

        def add_slab(dve, S, s, half):
            dve.wait_ge(w_used, CPS * S + CPS)
            for tt in range(TT):
                last = nc.vector.tensor_tensor(out=h[:, tt, s * SLAB:(s + 1) * SLAB],
                                               in0=h[:, tt, s * SLAB:(s + 1) * SLAB],
                                               in1=bank[2 * half + tt][:], op=ALU.add)
            last.then_inc(acc_free, 1)

        def act_mlp(act, layer, cb, sb):
            with act.Fori(0, NG) as g:
                for s in range(HPG):
                    for c in range(CPS):
                        split_hi(act, g * CPG + cb + s * CPS + c, g * (CPG // RING) + (cb + s * CPS + c) // RING, c)
                        if c == 2 and 1 <= s <= NS:
                            half = (s - 1) % 2
                            act.wait_ge(w_used, g * CPG + cb + s * CPS)
                            if s >= 3:
                                act.wait_ge(sq_ready, g * NS + layer * NG * NS + s - 2)
                            for tt in range(TT):
                                last = nc.scalar.activation(u_[:, half, tt], bank[2 * half + tt][:], ACT.Relu)
                            last.then_inc(acc_free, 1)
                        if c == CPS - 1 and 1 <= s <= NS:
                            n = g * NS + layer * NG * NS + s
                            act.wait_ge(hT_ps, n)
                            for j in range(2):
                                last = nc.scalar.activation(
                                    xbh[:, (s - 1) * 4 + 2 * j:(s - 1) * 4 + 2 * j + 2].rearrange("p a n -> p (a n)"),
                                    bank[4 + j][:], ACT.Copy)
                            last.then_inc(hT_hi, 1)

        def pool_mlp(pool, layer, cb, sb):
            with pool.Fori(0, NG) as g:
                for s in range(NS):
                    pool.wait_ge(acc_free, g * HPG + sb + s + 1)
                    if layer or s >= 2:
                        pool.wait_ge(hT_ps, g * NS + layer * NG * NS + s - 1)
                    nc.gpsimd.tensor_tensor(out=u2[:, s % 2], in0=u_[:, s % 2], in1=u_[:, s % 2],
                                            op=ALU.mult).then_inc(sq_ready, 1)

        def dve_mlp(dve, layer, cb, sb):
            with dve.Fori(0, NG) as g:
                for s in range(HPG):
                    for c in range(CPS):
                        split_lo(dve, g * CPG + cb + s * CPS + c, c)
                        if c == 2 and s > NS:
                            add_slab(dve, g * HPG + sb + s - 1, s - 1 - NS, (s - 1) % 2)
                        if c == CPS - 1 and 1 <= s <= NS:
                            n = g * NS + layer * NG * NS + s
                            dve.wait_ge(hT_hi, n)
                            for j in range(2):
                                kk = slice((s - 1) * 4 + 2 * j, (s - 1) * 4 + 2 * j + 2)
                                last = nc.vector.tensor_tensor(
                                    out=xbl[:, kk].rearrange("p a n -> p (a n)"), in0=bank[4 + j][:],
                                    in1=xbh[:, kk].bitcast(F32).rearrange("p a n -> p (a n)"), op=ALU.subtract)
                            last.then_inc(hT_lo, 1)
                add_slab(dve, g * HPG + sb + HPG - 1, NS - 1, 1)

        def pe_mlp(pe, layer, cb, sb, nlo):
            with pe.Fori(0, NG) as g:
                for s in range(HPG):
                    def before(c):
                        if s < NS:
                            pe.wait_ge(norm_lo, nlo + 2 * c + 2 if s == 0 and c >= 2 else nlo + 16 if s else nlo + 4)
                        if c == 4 and 1 <= s <= NS:
                            n = g * NS + layer * NG * NS + s
                            pe.wait_ge(sq_ready, n)
                            if layer or s > 1:
                                pe.wait_ge(hT_lo, n - 1)
                            for j in range(4):
                                for tt in range(TT):
                                    last = nc.tensor.transpose(
                                        bank[4 + j // 2][:, (j % 2) * T + tt * P:(j % 2) * T + (tt + 1) * P],
                                        u2[:, (s - 1) % 2, tt, j * P:(j + 1) * P], ident)
                            last.then_inc(hT_ps, 1)
                        if s >= NS:
                            pe.wait_ge(hT_lo, g * NS + layer * NG * NS + (NS - 1 if s == NS and c < 6 else NS))
                    xh, xl = (xah, xal) if s < NS else (xbh, xbl)
                    slab_matmuls(pe, g * CPG + cb + s * CPS, g * HPG + sb + s, s % 2, xh, xl, before)

        def sp_mlp(sp, layer, cb, sb):
            with sp.Fori(0, NG) as g:
                for s in range(HPG):
                    for c in range(CPS):
                        G = g * CPG + cb + s * CPS + c
                        if s < NS:
                            load_chunk(sp, t['mlp_up'][layer], G, c, c * KC * P, g * D + s * SLAB)
                        else:
                            load_chunk(sp, t['mlp_down'][layer], G, c, g * D + c * KC * P, (s - NS) * SLAB)

        def act_unit(act, unit, evac):
            for s in range(unit['slabs']):
                for c in range(CPS):
                    G = unit['chunk'] + s * CPS + c
                    split_hi(act, G, G // RING, c)
                    if c == 2 and s:
                        evac(s - 1)
            evac(unit['slabs'] - 1)

        def dve_unit(dve, unit, evac):
            for s in range(unit['slabs']):
                for c in range(CPS):
                    split_lo(dve, unit['chunk'] + s * CPS + c, c)
                    if c == 2 and s:
                        evac(s - 1)
            evac(unit['slabs'] - 1)

        def nothing(s):
            pass

        u_wo = new_unit(NS)
        mlp0 = dict(stream)
        new_unit(HPG * NG)
        u_kv = new_unit(6)
        u_q = new_unit(NS)

        with nc.Block() as block:
            @block.sync
            def _(sp):
                sp.dma_start(h[:], t['x'].rearrange("b (t p) d -> p (b t) d", p=P)).then_inc(h_in, 16)
                sp_unit(sp, t['rw_wo'][0], u_wo)
                sp_mlp(sp, 0, mlp0['chunk'], mlp0['slab'])
                sp_unit(sp, t['w_kv'], u_kv)
                sp_unit(sp, t['nsa_wq'][0], u_q)

            @block.gpsimd
            def _(pool):
                pool.dma_start(gw[:], t['nsa_wq'][0][:, D:D + 48].rearrange("(k p) n -> p k n", p=P))\
                    .then_inc(gw_in, 16)
                pool_mlp(pool, 0, mlp0['chunk'], mlp0['slab'])

            @block.scalar
            def _(act):
                act_unit(act, u_wo, nothing)
                act_norm_sum(act, 1, lambda e: e.wait_ge(acc_free, mlp0['slab']), xs2)
                act_norm_sqrt(act, 1)
                act_split_norm(act, 1, 0, 'm0', xah)
                act_mlp(act, 0, mlp0['chunk'], mlp0['slab'])
                act_norm_sum(act, 2, lambda e: e.wait_ge(acc_free, u_kv['slab']), xs2)
                act_norm_sqrt(act, 2)
                act_split_norm(act, 2, KT, 'kv_norm_g', xah)
                act_split_norm(act, 2, 2 * KT, 'b_norm_g', xbh, again=True)
                act.wait_ge(gw_in, 16)
                nc.scalar.activation(gwh[:], gw[:], ACT.Copy).then_inc(gw_hi, 1)

                def kv_evac(s):
                    act.wait_ge(w_used, u_kv['chunk'] + CPS * (s + 1))
                    for tt in range(TT):
                        last = nc.scalar.activation(kvs[:, tt, s], bank[2 * (s % 2) + tt][:], ACT.Copy)
                    last.then_inc(acc_free, 1)

                def q_evac(s):
                    act.wait_ge(w_used, u_q['chunk'] + CPS * (s + 1))
                    for tt in range(TT):
                        last = nc.scalar.activation(qs[:, tt, s * SLAB:(s + 1) * SLAB], bank[2 * (s % 2) + tt][:],
                                                    ACT.Copy, scale=HD ** -0.5)
                    last.then_inc(acc_free, 1)
                act_unit(act, u_kv, kv_evac)
                act_unit(act, u_q, q_evac)
                act.wait_ge(gate_ps, 1)
                for tt in range(TT):
                    nc.scalar.activation(gates[:, tt], bank[6 + tt][:, 0:48], ACT.Sigmoid)

            @block.vector
            def _(dve):
                dve.wait_ge(h_in, 16)
                dve_unit(dve, u_wo, lambda s: add_slab(dve, u_wo['slab'] + s, s, s % 2))
                dve_norm(dve, 1, xs2)
                dve_split_norm(dve, 0, 'm0', xah, xal)
                dve_mlp(dve, 0, mlp0['chunk'], mlp0['slab'])
                dve_norm(dve, 2, xs2)
                dve_split_norm(dve, KT, 'kv_norm_g', xah, xal)
                dve_split_norm(dve, 2 * KT, 'b_norm_g', xbh, xbl)
                dve.wait_ge(gw_hi, 1)
                nc.vector.tensor_tensor(out=gwl[:], in0=gw[:], in1=gwh[:].bitcast(F32),
                                        op=ALU.subtract).then_inc(gw_lo, 1)
                dve_unit(dve, u_kv, nothing)
                dve_unit(dve, u_q, nothing)

            @block.tensor
            def _(pe):
                pe_unit(pe, u_wo, xbh, xbl)
                pe_norm(pe, 1, xs2)
                pe_mlp(pe, 0, mlp0['chunk'], mlp0['slab'], 0)
                pe_norm(pe, 2, xs2)
                pe.wait_ge(norm_lo, 3 * KT)
                pe_unit(pe, u_kv, xah, xal)
                pe_unit(pe, u_q, xbh, xbl)
                pe.wait_ge(gw_lo, 1)
                for tt in range(TT):
                    for k in range(KT):
                        tok = slice(tt * P, (tt + 1) * P)
                        nc.tensor.matmul(bank[6 + tt][:, 0:48], xbh[:, k, tok], gwh[:, k], start=(k == 0), stop=False)
                        nc.tensor.matmul(bank[6 + tt][:, 0:48], xbh[:, k, tok], gwl[:, k], start=False, stop=False)
                        last = nc.tensor.matmul(bank[6 + tt][:, 0:48], xbl[:, k, tok], gwh[:, k], start=False,
                                                stop=(k == KT - 1))
                last.then_inc(gate_ps, 1)

        CP = (0, 1, 2, 4)
        kT4 = at("kT4", XA_AT, [P, 4, GB, T])
        xc = at("xc", XA_AT + 16384, [P, 2, 32, GB * NCB])
        cw1 = at("cw1", XA_AT + 31744, [P, 2, 32, P])
        tb = at("tb", XA_AT + 64512, [P, HB, T])
        tbr = at("tbr", XB_AT, [P, HB, T])
        qg = at("qg", XA_AT + 31744, [P, TT, SLAB])
        qT4 = at("qT4", XA_AT + 35840, [P, REP, T])
        vg = at("vg", XA_AT + 39936, [P, TT, 2, HD])
        vcg = at("vcg", XA_AT + 41984, [P, HD])
        s0 = at("s0", XA_AT + 42496, [P, 2, 2, P])
        s1 = at("s1", XA_AT + 44544, [P, 2, 2, T])
        sc = at("sc", XA_AT + 48640, [P, 2, TT, 16])
        pt1 = at("pt1", XA_AT + 48896, [P, 2, SLAB])
        pt2 = at("pt2", XA_AT + 52992, [P, 2, 256])
        ptc = at("ptc", XA_AT + 55040, [P, 2, T])
        mx = at("mx", XA_AT + 57088, [P, 2, 6])
        sm = at("sm", XA_AT + 57152, [P, 2, 6])
        cst2 = at("cst2", WORK, [P, 512 + TT])
        dist_of = cst2[0:BUCKETS + 1, 0:512]
        row_ok = cst2[:, 512:512 + TT]
        tabx = at("tabx", WORK + 4128, [BUCKETS + 1, HB])
        grow = at("grow", WORK + 4224, [HB, 512])
        tbc = at("tbc", WORK + 6272, [P, TT, HB, 16])
        cw2 = at("cw2", WORK + 8320, [P, 2, P])
        pebr = at("pebr", WORK + 9344, [66, P])
        peb = at("peb", WORK + 9856, [P, 66])
        hid = at("hid", WORK + 10144, [GB * NCB, 2, P])
        gel = at("gel", WORK + 11168, [P, 2, GB * NCB])
        kcT = at("kcT", WORK + 11680, [P, GB * NCB])
        vcs = at("vcs", WORK + 11936, [NCB, GB, HD])
        dist_scratch = nc.dram_tensor("dist_scratch", [HB, 512], F32, kind="Internal").ap()

        c2_in, cw_in, tab_in = sem("c2_in"), sem("cw_in"), sem("tab_in")
        tab_one, tb_ready = sem("tab_one"), sem("tb_ready")
        kT_ps, kT_act, kT_dve = sem("kT_ps"), sem("kT_act"), sem("kT_dve")
        peb_ps, peb_ready, dist_ps, dist_ready, dist_out, tb_in = (
            sem("peb_ps"), sem("peb_ready"), sem("dist_ps"), sem("dist_ready"), sem("dist_out"), sem("tb_in"))
        bc_ps, xc_ready, hid_ps, hid_ready, hidT_ps, gel_ready = (sem(n) for n in (
            "bc_ps", "xc_ready", "hid_ps", "hid_ready", "hidT_ps", "gel_ready"))
        kc_ps, kc_ready, gates_ok = sem("kc_ps"), sem("kc_ready"), sem("gates_ok")
        grp_in, qT_ps, qT_ready = sem("grp_in"), sem("qT_ps"), sem("qT_ready")
        pad0 = sem("pad0")
        sc_ps, biased, maxed, sums, weights, pT_ps, pT1, pT2, o_ps, oa_hi, oa_lo = (sem(n) for n in (
            "sc_ps", "biased", "maxed", "sums", "weights", "pT_ps", "pT1", "pT2", "o_ps", "oa_hi", "oa_lo"))
        alink = sem("alink")
        AL = 3 * REP

        with nc.Block() as block:
            @block.sync
            def _(sp):
                sp.dma_start(cst2[:], t['consts2']).then_inc(c2_in, 16)
                sp.dma_start(tabx[0:BUCKETS], t['rel_bias']).then_inc(tab_in, 16)
                sp.dma_start(pebr[0:64], t['cmp_pe'].rearrange("a l d -> (a l) d")).then_inc(c2_in, 16)
                sp.dma_start(pebr[64:66], t['cmp_b1']).then_inc(c2_in, 16)
                sp.dma_start(cw2[:], t['cmp_w2'].rearrange("a k n -> k a n")).then_inc(cw_in, 16)
                for a in range(2):
                    sp.dma_start(cw1[:, a], t['cmp_w1'][a].rearrange("(l d) n -> d l n", d=P)).then_inc(cw_in, 16)
                sp.wait_ge(dist_ready, 1)
                sp.dma_start(dist_scratch, grow[:]).then_inc(dist_out, 16)
                sp.wait_ge(dist_out, 16)
                for a in range(HB):
                    skew = bass.AP(tensor=dist_scratch.tensor, offset=512 * a + P + 1, ap=[[1, P], [1, T]])
                    sp.dma_start(tbr[:, a], skew).then_inc(tb_in, 16)

            @block.gpsimd
            def _(pool):
                nc.gpsimd.memset(tabx[BUCKETS:BUCKETS + 1], 1.0).then_inc(tab_one, 1)
                pool.wait_ge(kc_ready, 1)
                nc.gpsimd.memset(vcg[:], 0.0)
                nc.gpsimd.memset(ptc[:], 0.0).then_inc(pad0, 1)
                pool.wait_ge(pad0, 1)
                with pool.Fori(0, GB) as g:
                    pool.wait_ge(oa_lo, g * REP + 1)
                    nc.gpsimd.tensor_copy(qg[:], qs[:, :, bass.ds(g * SLAB, SLAB)])
                    for b in range(2):
                        nc.gpsimd.tensor_copy(vg[:, :, b], kvs[:, :, 3 + 2 * b, bass.ds(g * HD, HD)])
                    nc.gpsimd.tensor_copy(vcg[0:NCB], vcs[:, bass.ds(g, 1)].rearrange("p a n -> p (a n)"))\
                        .then_inc(grp_in, 1)

            @block.scalar
            def _(act):
                for j in range(0, 8, 2):
                    act.wait_ge(kT_ps, j + 1)
                    nc.scalar.activation(kT4[:, j // 2, (j % 2) * 2:(j % 2) * 2 + 2].rearrange("p a n -> p (a n)"),
                                         bank[j][:], ACT.Copy).then_inc(kT_act, 1)
                act.wait_ge(dist_ps, 1)
                nc.scalar.activation(grow[:], bank[1][0:HB], ACT.Copy).then_inc(dist_ready, 1)
                act.wait_ge(hid_ps, 1)
                for a in range(2):
                    last = nc.scalar.activation(hid[:, a], bank[4 + a][0:GB * NCB, 0:P], ACT.Copy)
                last.then_inc(hid_ready, 1)
                act.wait_ge(hidT_ps, 1)
                for a in range(2):
                    last = nc.scalar.activation(gel[:, a], bank[6][:, a * 64:a * 64 + GB * NCB], ACT.Gelu_apprx_tanh,
                                                bias=peb[:, 64 + a:65 + a])
                last.then_inc(gel_ready, 1)
                with act.Fori(0, GB) as g:
                    act.wait_ge(qT_ps, g + 1)
                    for j in range(2):
                        last = nc.scalar.activation(qT4[:, 2 * j:2 * j + 2].rearrange("p a n -> p (a n)"),
                                                    bank[6 + j][:], ACT.Copy)
                    last.then_inc(qT_ready, 1)

                    def exps(r):
                        b = r % 2
                        act.wait_ge(maxed, g * REP + r + 1)
                        for tt in range(TT):
                            nc.scalar.activation(sc[:, b, tt, 0:NCB], sc[:, b, tt, 0:NCB], ACT.Exp,
                                                 bias=mx[:, b, 3 * tt:3 * tt + 1], accum_out=sm[:, b, 3 * tt:3 * tt + 1])
                            for br in range(2):
                                s = (s0, s1)[tt][:, b, br]
                                n = 3 * tt + 1 + br
                                last = nc.scalar.activation(s, s, ACT.Exp, bias=mx[:, b, n:n + 1],
                                                            accum_out=sm[:, b, n:n + 1])
                        last.then_inc(sums, 1)
                    exps(0)
                    for r in range(REP):
                        if r < REP - 1:
                            exps(r + 1)
                        act.wait_ge(pT_ps, g * REP + r + 1)
                        nc.scalar.activation(pt1[:, r % 2], bank[4][:], ACT.Copy).then_inc(pT1, 1)
                        act.wait_ge(o_ps, g * REP + r + 1)
                        nc.scalar.activation(xbh[:, bass.ds(g * REP + r, 1)].rearrange("p a n -> p (a n)"),
                                             bank[6 + r % 2][:, 0:T], ACT.Copy).then_inc(oa_hi, 1)

            @block.vector
            def _(dve):
                for j in range(1, 8, 2):
                    dve.wait_ge(kT_ps, j + 1)
                    nc.vector.tensor_copy(kT4[:, j // 2, (j % 2) * 2:(j % 2) * 2 + 2].rearrange("p a n -> p (a n)"),
                                          bank[j][:]).then_inc(kT_dve, 1)
                dve.wait_ge(peb_ps, 1)
                nc.vector.tensor_copy(peb[:], bank[0][:, 0:66]).then_inc(peb_ready, 1)
                dve.wait_ge(bc_ps, 1)
                for tt in range(TT):
                    nc.vector.tensor_copy(tbc[:, tt, :, 0:NCB].rearrange("p h c -> p c h"),
                                          bank[2 + tt][:, 0:NCB * HB].rearrange("p (c h) -> p c h", h=HB))
                dve.wait_ge(c2_in, 16)
                for tt in range(TT):
                    last = nc.vector.tensor_scalar(gates[:, tt].rearrange("p (h b) -> p h b", b=3)[:, :, 0],
                                                   gates[:, tt].rearrange("p (h b) -> p h b", b=3)[:, :, 0],
                                                   row_ok[:, tt:tt + 1], None, ALU.mult)
                last.then_inc(gates_ok, 1)
                dve.wait_ge(peb_ready, 1)
                dve.wait_ge(kT_act, 4)
                dve.wait_ge(kT_dve, 4)
                for a in range(2):
                    for gg in range(GB):
                        for hf in range(2):
                            src = kT4[:, a, gg, hf * 16:hf * 16 + NCB * 16].rearrange("p (c l) -> p c l", l=16)
                            dst = xc[:, a, hf * 16:hf * 16 + 16, gg * NCB:(gg + 1) * NCB].rearrange("p l c -> p c l")
                            pe_ = peb[:, a * 32 + hf * 16:a * 32 + hf * 16 + 16]
                            last = nc.vector.tensor_tensor(out=dst, in0=src, in1=bc(pe_, NCB), op=ALU.add)
                last.then_inc(xc_ready, 1)
                dve.wait_ge(kc_ps, 1)
                nc.vector.tensor_copy(kcT[:], bank[7][:, 0:GB * NCB])
                nc.vector.tensor_copy(vcs[:].rearrange("p a n -> p (a n)"), bank[0][0:NCB]).then_inc(kc_ready, 1)
                dve.wait_ge(tb_in, 16 * (HB))
                nc.vector.tensor_copy(tb[:], tbr[:, :, ::-1]).then_inc(tb_ready, 1)
                nc.vector.memset(mx[:, 0, 0:1], 0.0).then_inc(oa_lo, 1)
                dve.wait_ge(tb_ready, 1)
                dve.wait_ge(gates_ok, 1)
                links = [0]
                with dve.Fori(0, GB) as g:
                    def link(ins):
                        links[0] += 1
                        ins.then_inc(alink, 1)
                        dve.wait_ge(alink, g * AL + links[0])

                    def bias(r):
                        b = r % 2
                        a = bass.ds(g * REP + r, 1)
                        A, B = bank[b], bank[2 + b]
                        dve.wait_ge(sc_ps, g * REP + r + 1)
                        if r >= 2:
                            dve.wait_ge(pT_ps, g * REP + r - 1)
                        nc.vector.tensor_tensor(out=s0[:, b], in0=A[:, 0:256].rearrange("p (a n) -> p a n", a=2),
                                                in1=tb[:, a, P:T].to_broadcast([P, 2, P]), op=ALU.add)
                        nc.vector.tensor_tensor(out=s1[:, b], in0=B[:].rearrange("p (a n) -> p a n", a=2),
                                                in1=tb[:, a].to_broadcast([P, 2, T]), op=ALU.add)
                        nc.vector.tensor_tensor(out=sc[:, b, :, 0:NCB],
                                                in0=A[:, 256:288].rearrange("p (a n) -> p a n", n=16)[:, :, 0:NCB],
                                                in1=tbc[:, :, a, 0:NCB].rearrange("p t a n -> p (t a) n"),
                                                op=ALU.add).then_inc(biased, 1)
                        dve.wait_ge(biased, g * REP + r + 1)
                        m3 = mx[:, b].rearrange("p (t n) -> p t n", t=2)
                        nc.vector.reduce_max(m3[:, 0, 1:3], s0[:, b], AX.X)
                        nc.vector.reduce_max(m3[:, 1, 1:3], s1[:, b], AX.X)
                        link(nc.vector.reduce_max(m3[:, :, 0], sc[:, b, :, 0:NCB], AX.X))
                        nc.vector.tensor_scalar(mx[:, b], mx[:, b], -1.0, None, ALU.mult).then_inc(maxed, 1)
                    bias(0)
                    for r in range(REP):
                        b = r % 2
                        if r < REP - 1:
                            bias(r + 1)
                        dve.wait_ge(sums, g * REP + r + 1)
                        link(nc.vector.reciprocal(sm[:, b], sm[:, b]))
                        s3 = sm[:, b].rearrange("p (t n) -> p t n", t=2)
                        link(nc.vector.tensor_tensor(out=s3, in0=s3, in1=gates[:, :, bass.ds((g * REP + r) * 3, 3)],
                                                     op=ALU.mult))
                        nc.vector.tensor_tensor(out=s0[:, b], in0=s0[:, b], op=ALU.mult,
                                                in1=sm[:, b, 1:3].unsqueeze(2).to_broadcast([P, 2, P]))
                        nc.vector.tensor_tensor(out=s1[:, b], in0=s1[:, b], op=ALU.mult,
                                                in1=sm[:, b, 4:6].unsqueeze(2).to_broadcast([P, 2, T]))
                        nc.vector.tensor_tensor(out=sc[:, b, :, 0:NCB], in0=sc[:, b, :, 0:NCB], op=ALU.mult,
                                                in1=s3[:, :, 0:1].to_broadcast([P, 2, NCB])).then_inc(weights, 1)
                        dve.wait_ge(pT_ps, g * REP + r + 1)
                        nc.vector.tensor_copy(pt2[:, b], bank[5][:, 0:256])
                        nc.vector.tensor_copy(ptc[0:NCB, b], bank[5][0:NCB, 256:512]).then_inc(pT2, 1)
                        dve.wait_ge(oa_hi, g * REP + r + 1)
                        a = bass.ds(g * REP + r, 1)
                        nc.vector.tensor_tensor(out=xbl[:, a].rearrange("p a n -> p (a n)"), in0=bank[6 + b][:, 0:T],
                                                in1=xbh[:, a].bitcast(F32).rearrange("p a n -> p (a n)"),
                                                op=ALU.subtract).then_inc(oa_lo, 1)
                assert links[0] == AL, links[0]

            @block.tensor
            def _(pe):
                for n, part in enumerate(CP):
                    for j in range(2):
                        for k in range(2):
                            gg = 2 * j + k
                            for tt in range(TT):
                                last = nc.tensor.transpose(bank[2 * n + j][:, k * T + tt * P:k * T + (tt + 1) * P],
                                                           kvs[:, tt, part, gg * HD:(gg + 1) * HD], ident)
                        last.then_inc(kT_ps, 1)
                pe.wait_ge(c2_in, 48)
                pe.wait_ge(kT_act, 1)
                nc.tensor.transpose(bank[0][:, 0:66], pebr[:], ident[0:66, 0:66]).then_inc(peb_ps, 1)
                pe.wait_ge(tab_in, 16)
                pe.wait_ge(tab_one, 1)
                pe.wait_ge(kT_dve, 1)
                nc.tensor.matmul(bank[1][0:HB], tabx[:], dist_of, start=True, stop=True).then_inc(dist_ps, 1)
                pe.wait_ge(kT_act, 2)
                pe.wait_ge(kT_dve, 2)
                for tt in range(TT):
                    for c in range(NCB):
                        i0 = T + P * tt - (31 + 16 * c)
                        last = nc.tensor.matmul(bank[2 + tt][:, c * HB:(c + 1) * HB], dist_of[:, i0:i0 + P], tabx[:],
                                                start=True, stop=True)
                last.then_inc(bc_ps, 1)
                pe.wait_ge(cw_in, 48)
                pe.wait_ge(xc_ready, 1)
                pe.wait_ge(kT_act, 4)
                pe.wait_ge(kT_dve, 4)
                for a in range(2):
                    for l in range(32):
                        last = nc.tensor.matmul(bank[4 + a][0:GB * NCB, 0:P], xc[:, a, l], cw1[:, a, l],
                                                start=(l == 0), stop=(l == 31))
                last.then_inc(hid_ps, 1)
                pe.wait_ge(hid_ready, 1)
                for a in range(2):
                    last = nc.tensor.transpose(bank[6][:, a * 64:a * 64 + GB * NCB], hid[:, a],
                                               ident[0:GB * NCB, 0:GB * NCB])
                last.then_inc(hidT_ps, 1)
                pe.wait_ge(gel_ready, 1)
                nc.tensor.matmul(bank[7][:, 0:GB * NCB], cw2[:, 0], gel[:, 0], start=True, stop=True)
                for gg in range(GB):
                    last = nc.tensor.matmul(bank[0][0:NCB, gg * HD:(gg + 1) * HD],
                                            gel[:, 1, gg * NCB:(gg + 1) * NCB], cw2[:, 1], start=True, stop=True)
                last.then_inc(kc_ps, 1)
                pe.wait_ge(dist_ready, 1)
                pe.wait_ge(kc_ready, 1)
                with pe.Fori(0, GB) as g:
                    pe.wait_ge(grp_in, g + 1)
                    pe.wait_ge(oa_lo, g * REP + 1)
                    for r in range(REP):
                        for tt in range(TT):
                            last = nc.tensor.transpose(bank[6 + r // 2][:, (r % 2) * T + tt * P:(r % 2) * T + (tt + 1) * P],
                                                       qg[:, tt, r * HD:(r + 1) * HD], ident)
                    last.then_inc(qT_ps, 1)
                    pe.wait_ge(qT_ready, g + 1)

                    def scores(r):
                        b = r % 2
                        A, B = bank[b], bank[2 + b]
                        if r >= 2:
                            pe.wait_ge(biased, g * REP + r - 1)
                        nc.tensor.matmul(A[:, 0:256].rearrange("p (a n) -> p a n", a=2), qT4[:, r, 0:P],
                                         kT4[:, 2:4, bass.ds(g, 1), 0:P].rearrange("p a b n -> p (a b) n"),
                                         start=True, stop=True)
                        nc.tensor.matmul(B[:].rearrange("p (a n) -> p a n", a=2), qT4[:, r, P:T],
                                         kT4[:, 2:4, bass.ds(g, 1)].rearrange("p a b n -> p (a b) n"),
                                         start=True, stop=True)
                        for tt in range(TT):
                            last = nc.tensor.matmul(A[:, 256 + 16 * tt:256 + 16 * tt + NCB], qT4[:, r, tt * P:(tt + 1) * P],
                                                    kcT[:, bass.ds(g * NCB, NCB)], start=True, stop=True)
                        last.then_inc(sc_ps, 1)
                    scores(0)
                    for r in range(REP):
                        b = r % 2
                        if r < REP - 1:
                            scores(r + 1)
                        pe.wait_ge(weights, g * REP + r + 1)
                        if r:
                            pe.wait_ge(pT1, g * REP + r)
                            pe.wait_ge(pT2, g * REP + r)
                        for br in range(2):
                            nc.tensor.transpose(bank[4][:, br * 256:br * 256 + P], s0[:, b, br], ident)
                            nc.tensor.transpose(bank[4][:, br * 256 + P:br * 256 + 2 * P], s1[:, b, br, 0:P], ident)
                            nc.tensor.transpose(bank[5][:, br * P:(br + 1) * P], s1[:, b, br, P:T], ident)
                        for tt in range(TT):
                            last = nc.tensor.transpose(bank[5][0:NCB, 256 + tt * P:256 + (tt + 1) * P],
                                                       sc[:, b, tt, 0:NCB], ident)
                        last.then_inc(pT_ps, 1)
                        pe.wait_ge(pT1, g * REP + r + 1)
                        pe.wait_ge(pT2, g * REP + r + 1)
                        if r >= 2:
                            pe.wait_ge(oa_lo, g * REP + r)
                        O = bank[6 + b]
                        for br in range(2):
                            nc.tensor.matmul(O[:, 0:T], vg[:, 0, br], pt1[:, b, br * T:(br + 1) * T],
                                             start=(br == 0), stop=False)
                        for br in range(2):
                            nc.tensor.matmul(O[:, P:T], vg[:, 1, br], pt2[:, b, br * P:(br + 1) * P],
                                             start=False, stop=False)
                        nc.tensor.matmul(O[:, 0:T], vcg[:], ptc[:, b], start=False, stop=True).then_inc(o_ps, 1)

        u_wo2 = new_unit(NS)
        mlp1 = dict(stream)
        new_unit(HPG * NG)
        fg = at("fg", WORK + 32768, [P, D])
        fg_in, y_out, out_ready = sem("fg_in"), sem("y_out"), sem("out_ready")

        with nc.Block() as block:
            @block.sync
            def _(sp):
                sp_unit(sp, t['nsa_wo'][0], u_wo2)
                sp_mlp(sp, 1, mlp1['chunk'], mlp1['slab'])
                for tt in range(TT):
                    sp.wait_ge(out_ready, tt + 1)
                    sp.dma_start(t['y'][0].rearrange("(t p) d -> p t d", p=P)[:, tt], xs2[:, tt])\
                        .then_inc(y_out, 16)
                sp.wait_ge(y_out, 16 * (TT))

            @block.gpsimd
            def _(pool):
                pool.dma_start(fg[:], t['final_norm_g'].partition_broadcast(P)).then_inc(fg_in, 16)
                pool_mlp(pool, 1, mlp1['chunk'], mlp1['slab'])

            @block.scalar
            def _(act):
                act_unit(act, u_wo2, nothing)
                act_norm_sum(act, 3, lambda e: e.wait_ge(acc_free, mlp1['slab']), xs2)
                act_norm_sqrt(act, 3)
                act_split_norm(act, 3, 3 * KT, 'm1', xah)
                act_mlp(act, 1, mlp1['chunk'], mlp1['slab'])
                act_norm_sum(act, 4, lambda e: e.wait_ge(acc_free, stream['slab']), xs2)
                act_norm_sqrt(act, 4)

            @block.vector
            def _(dve):
                dve_unit(dve, u_wo2, lambda s: add_slab(dve, u_wo2['slab'] + s, s, s % 2))
                dve_norm(dve, 3, xs2)
                dve_split_norm(dve, 3 * KT, 'm1', xah, xal)
                dve_mlp(dve, 1, mlp1['chunk'], mlp1['slab'])
                dve.wait_ge(norm_ss, 10)
                nc.vector.tensor_scalar(rstd, ss, 1.0 / D, NORM_EPS, ALU.mult, ALU.add).then_inc(norm_var, 1)
                dve.wait_ge(norm_std, 5)
                nc.vector.reciprocal(rstd, rstd).then_inc(norm_r, 1)
                dve.wait_ge(norm_r, 5)
                dve.wait_ge(fg_in, 16)
                for tt in range(TT):
                    nc.vector.scalar_tensor_tensor(out=xs2[:, tt], in0=h[:, tt], scalar=rstd[:, tt:tt + 1], in1=fg[:],
                                                   op0=ALU.mult, op1=ALU.mult).then_inc(out_ready, 1)

            @block.tensor
            def _(pe):
                pe_unit(pe, u_wo2, xbh, xbl)
                pe_norm(pe, 3, xs2)
                pe_mlp(pe, 1, mlp1['chunk'], mlp1['slab'], 3 * KT)

INS = ['x', 'consts', 'consts2', 'par_rows', 'rw_w1', 'rw_a1', 'rw_g1', 'rw_wr', 'rw_wk', 'rw_wv', 'rw_w2', 'rw_a2',
       'rw_g2', 'rw_wo', 'mlp_up', 'mlp_down', 'w_kv', 'nsa_wq', 'nsa_wo', 'rel_bias', 'cmp_pe', 'cmp_w1', 'cmp_b1',
       'cmp_w2', 'final_norm_g']
OUTS = {'y': (1, T, D)}


def kernel(**inputs):
    import numpy as _np
    import concourse.bacc as _bacc
    from concourse import mybir as _mybir
    from concourse.bass_utils import run_bass_kernel_spmd as _run
    nc = _bacc.Bacc("TRN2", target_bir_lowering=False, num_devices=1)
    ins = {k: _np.asarray(v) for k, v in inputs.items()}
    rows = {n: ins[n] for n in PARAMS if n in ins}
    for j in range(6):
        rows[f'mu{j}'] = ins['rw_mu'][0, j]
    for j in range(2):
        rows[f'm{j}'] = ins['m_norm_g'][j]
    ins['par_rows'] = _np.concatenate([_np.reshape(rows[n], (KT, P)) for n in PARAMS]).reshape(3, PROW, P)
    ins['consts'], ins['consts2'] = constants(), constants2()
    arrays, args = {}, {}
    for name in INS:
        a = _np.ascontiguousarray(ins[name])
        arrays[f"in_{name}"] = a
        args[name] = nc.dram_tensor(f"in_{name}", a.shape, _mybir.dt.from_np(a.dtype), kind="ExternalInput").ap()
    for name, shape in OUTS.items():
        args[name] = nc.dram_tensor(f"out_{name}", shape, _mybir.dt.float32, kind="ExternalOutput").ap()
    build(nc, **args)
    r = _run(nc, [arrays], core_ids=[0])
    got = tuple(r.results[0][f"out_{n}"] for n in OUTS)
    return got[0]
```

```python
import math
from contextlib import ExitStack

import numpy as np
import concourse.bass as bass
from concourse import mybir

F32 = mybir.dt.float32
F32R = mybir.dt.float32r
ALU = mybir.AluOpType
ACT = mybir.ActivationFunctionType
AX = mybir.AxisListType

P = 128
D = 2048
T = 256
TT = T // P
KT = D // P
SLAB = 512
NS = D // SLAB
KC = 2
CPS = KT // KC
RING = 4
FF = 4 * D
NG = FF // D
LW, LA, LG = 96, 128, 256
NORM_EPS = 1e-6
GN_EPS = 64e-5
CH = 64
HEADS_A = 32
PAIRS = 4
NGRP = KT // PAIRS
HB, GB, HD = 16, 4, 128
REP = HB // GB
KVW = 6 * GB * HD
NCB = T // 16 - 1
BUCKETS, MAXDIST = 32, 128
NEG = -1e30
LEVELS = (2, 4, 8, 16, 32)

PARAMS = ['a_norm_g', 'mu0', 'mu1', 'mu2', 'mu3', 'mu4', 'mu5', 'rw_w0', 'rw_a0', 'rw_kk', 'rw_ka',
          'rw_rk', 'rw_lnx_w', 'rw_lnx_b', 'kv_norm_g', 'b_norm_g', 'm0', 'm1']
PROW = 6 * KT

C_ID, C_ONES, C_CAUSAL, C_LOW, C_L1, C_T1, C_LV = 0, 128, 256, 512, 640, 768, 896
C_W = C_LV + 128 * len(LEVELS)


def constants():
    c = np.zeros((P, C_W), np.float32)
    s, t = np.arange(P)[:, None], np.arange(P)[None, :]
    same = s // CH == t // CH
    c[:, C_ID:C_ID + P] = s == t
    c[:, C_ONES:C_ONES + P] = same
    c[:, C_CAUSAL:C_CAUSAL + P] = same & (s < t)
    c[:, C_CAUSAL + P:C_CAUSAL + 2 * P] = same & (s <= t)
    c[:, C_LOW:C_LOW + P] = same & (s > t)

    def level(m):
        return (s // (2 * m) == t // (2 * m)) & (s % (2 * m) < m) & (t % (2 * m) >= m)
    c[:, C_L1:C_L1 + P] = level(1).T
    c[:, C_T1:C_T1 + P] = level(1)
    for n, m in enumerate(LEVELS):
        c[:, C_LV + P * n:C_LV + P * (n + 1)] = level(m)
    return c


def constants2():
    c = np.zeros((P, 512 + TT), np.float32)
    exact = BUCKETS // 2
    for dist in range(-T + 1, T):
        n = max(dist, 0)
        if n < exact:
            b = n
        else:
            b = min(BUCKETS - 1, exact + int(np.log(np.float32(n / exact)) / math.log(MAXDIST / exact) * (BUCKETS - exact)))
        c[b, T + dist] = dist >= 0
        c[BUCKETS, T + dist] = NEG if dist < 0 else 0.0
    for tt in range(TT):
        c[:, 512 + tt] = tt * P + np.arange(P) >= 31
    return c


def build(nc, **t):
    ctx = ExitStack()
    with ctx:
        def sem(name):
            return ctx.enter_context(nc.semaphore(name))

        def at(name, addr, shape, dt=F32):
            return nc.alloc_sbuf_tensor_at(name, shape, dt, offset=addr)

        A0 = 16640
        cst = at("cst", A0, [P, C_W])
        par = at("par", A0 + 6144, [P, len(PARAMS) * KT])
        small = at("small", A0 + 7424, [P, 64])
        H_AT = A0 + 8192
        XB_AT = H_AT + 16384
        XA_AT = XB_AT + 32768
        RAW_AT = XA_AT + 32768
        WHI_AT = RAW_AT + 16384
        WORK = WHI_AT + 32768
        TOP = 229344
        LH_AT = TOP - 4096
        h = at("h", H_AT, [P, TT, D])
        xbh = at("xbh", XB_AT, [P, KT, T], F32R)
        xbl = at("xbl", XB_AT + 16384, [P, KT, T], F32R)
        xah = at("xah", XA_AT, [P, KT, T], F32R)
        xal = at("xal", XA_AT + 16384, [P, KT, T], F32R)
        raw = at("raw", RAW_AT, [P, RING, KC, SLAB])
        whi = at("whi", WHI_AT, [P, RING, KC, SLAB], F32R)
        wlo = at("wlo", WHI_AT + 16384, [P, RING, KC, SLAB], F32R)
        lora_h = at("lora_h", LH_AT, [P, 4, T])
        bank = [nc.alloc_psum_tensor(f"bank{i}", [P, 512], F32) for i in range(8)]
        rkv = nc.dram_tensor("rkv_scratch", [3, T, D], F32, kind="Internal").ap()

        ident = cst[:, C_ID:C_ID + P]

        def col(name, k):
            n = PARAMS.index(name) * KT + k
            return par[:, n:n + 1]

        raw_in = [sem(f"raw_in{i}") for i in range(RING)]
        hi_ready = sem("hi_ready")
        lo_ready = sem("lo_ready")
        w_used = sem("w_used")
        acc_free = sem("acc_free")
        stream = {'chunk': 0, 'slab': 0}

        def later(n, first):
            return not isinstance(n, int) or n > first

        def load_chunk(eng, w, G, c, k0, n0):
            if later(G, RING - 1):
                eng.wait_ge(lo_ready, G - (RING - 1))
            src = w[bass.ds(k0, KC * P), bass.ds(n0, SLAB)].rearrange("(k p) n -> p k n", p=P)
            eng.dma_start(raw[:, c % RING], src).then_inc(raw_in[c % RING], 16)

        def split_hi(act, G, uses, c):
            act.wait_ge(raw_in[c % RING], 16 * (uses + 1))
            if later(G, RING - 1):
                act.wait_ge(w_used, G - (RING - 1))
            nc.scalar.activation(whi[:, c % RING], raw[:, c % RING], ACT.Copy).then_inc(hi_ready, 1)

        def split_lo(dve, G, c):
            dve.wait_ge(hi_ready, G + 1)
            nc.vector.tensor_tensor(out=wlo[:, c % RING], in0=raw[:, c % RING],
                                    in1=whi[:, c % RING].bitcast(F32), op=ALU.subtract).then_inc(lo_ready, 1)

        def slab_matmuls(pe, G0, S, half, xh, xl, before=None):
            if later(S, 1):
                pe.wait_ge(acc_free, S - 1)
            for c in range(CPS):
                if before:
                    before(c)
                pe.wait_ge(lo_ready, G0 + c + 1)
                for j in range(KC):
                    k = c * KC + j
                    for tt in range(TT):
                        acc, tok = bank[2 * half + tt], slice(tt * P, (tt + 1) * P)
                        nc.tensor.matmul(acc[:], xh[:, k, tok], whi[:, c % RING, j], start=(k == 0), stop=False)
                        nc.tensor.matmul(acc[:], xh[:, k, tok], wlo[:, c % RING, j], start=False, stop=False)
                        last = nc.tensor.matmul(acc[:], xl[:, k, tok], whi[:, c % RING, j],
                                                start=False, stop=(k == KT - 1))
                last.then_inc(w_used, 1)

        def pe_unit(pe, unit, xh, xl, before=None):
            def step(i):
                for half in range(2):
                    slab_matmuls(pe, unit['chunk'] + 2 * CPS * i + CPS * half, unit['slab'] + 2 * i + half,
                                 half, xh, xl, before)
            n = unit['slabs'] // 2
            first = 1 if unit['slab'] == 0 else 0
            if first:
                step(0)
            if n > first:
                with pe.Fori(first, n) as i:
                    step(i)

        def sp_unit(sp, w, unit):
            def step(s):
                for c in range(CPS):
                    load_chunk(sp, w, unit['chunk'] + CPS * s + c, c, c * KC * P, s * SLAB)
            first = 1 if unit['slab'] == 0 else 0
            if first:
                step(0)
            with sp.Fori(first, unit['slabs']) as s:
                step(s)

        def new_unit(slabs):
            u = dict(stream, slabs=slabs)
            stream['chunk'] += slabs * CPS
            stream['slab'] += slabs
            return u

        xnT = at("xnT", WORK, [P, KT, T + 1])
        xs = at("xs", WORK + 16512, [P, TT, D])
        xx = at("xx", WORK + 16512, [P, KT, T])
        stage = at("stage", WORK + 32896, [P, 2, TT, SLAB])
        w1s = at("w1s", WORK + 41088, [P, KT, LW])
        a1s = at("a1s", WORK + 47232, [P, KT, LA])
        g1s = at("g1s", H_AT, [P, KT, LG])
        NMIX = 6
        mix = at("mix", WORK + 55424, [P, 2, NMIX, T])
        assert WORK + 55424 + 2 * NMIX * T * 4 <= LH_AT
        prow = at("prow", XA_AT, [PROW, 3, P])
        ss, rstd = small[:, 0:2], small[:, 2:4]
        eps_t = small[:, 4:5]

        consts_in = sem("consts_in")
        rows_in = sem("rows_in")
        x_in = sem("x_in")
        lora_in = sem("lora_in")
        par_T = sem("par_T")
        par_ready = sem("par_ready")
        eps_set = sem("eps_set")

        norm_ss, norm_var, norm_std, norm_r = sem("norm_ss"), sem("norm_var"), sem("norm_std"), sem("norm_r")
        norm_xs, norm_T = sem("norm_xs"), sem("norm_T")
        norms = {'n': 0}

        def act_norm_sum(act, n, ready, xs):
            ready(act)
            for tt in range(TT):
                last = nc.scalar.activation(xs[:, tt], h[:, tt], ACT.Square, accum_out=ss[:, tt:tt + 1])
                last.then_inc(norm_ss, 1)

        def act_norm_sqrt(act, n):
            act.wait_ge(norm_var, n + 1)
            nc.scalar.activation(rstd, rstd, ACT.Sqrt).then_inc(norm_std, 1)

        def dve_norm(dve, n, xs):
            dve.wait_ge(norm_ss, 2 * (n + 1))
            nc.vector.tensor_scalar(rstd, ss, 1.0 / D, NORM_EPS, ALU.mult, ALU.add).then_inc(norm_var, 1)
            dve.wait_ge(norm_std, n + 1)
            nc.vector.reciprocal(rstd, rstd).then_inc(norm_r, 1)
            dve.wait_ge(norm_r, n + 1)
            for tt in range(TT):
                nc.vector.tensor_scalar(xs[:, tt], h[:, tt], rstd[:, tt:tt + 1], None, ALU.mult).then_inc(norm_xs, 1)

        def pe_norm(pe, n, xs):
            pe.wait_ge(norm_xs, 2 * (n + 1))
            for b in range(8):
                for j in range(2):
                    for tt in range(TT):
                        k = 2 * b + j
                        last = nc.tensor.transpose(bank[b][:, j * T + tt * P:j * T + (tt + 1) * P],
                                                   xs[:, tt, k * P:(k + 1) * P], ident)
                last.then_inc(norm_T, 1)

        xn_ready = sem("xn_ready")
        pad_set = sem("pad_set")
        xx_ready = sem("xx_ready")
        mixed = sem("mixed")
        mix_hi = sem("mix_hi")
        mix_lo = sem("mix_lo")
        mix_used = sem("mix_used")
        lora_ready = sem("lora_ready")
        rkv_out = [sem(f"rkv_out{i}") for i in range(2)]
        units = [new_unit(NS) for _ in range(3)]
        order = ['rw_wr', 'rw_wk', 'rw_wv']
        MU = {'r': 'mu0', 'w': 'mu1', 'k': 'mu2', 'v': 'mu3', 'a': 'mu4', 'g': 'mu5'}

        with nc.Block() as block:
            @block.sync
            def _(sp):
                sp.dma_start(h[:], t['x'].rearrange("b (t p) d -> p (b t) d", p=P)).then_inc(x_in, 16)
                sp.dma_start(cst[:], t['consts']).then_inc(consts_in, 16)
                for u, name in zip(units, order):
                    sp_unit(sp, t[name][0], u)

            @block.gpsimd
            def _(pool):
                nc.gpsimd.memset(xnT[:, :, 0:1], 0.0).then_inc(pad_set, 1)
                pool.dma_start(prow[:, 0], t['par_rows'][0]).then_inc(rows_in, 16)
                pool.dma_start(prow[:, 1], t['par_rows'][1]).then_inc(rows_in, 16)
                pool.dma_start(prow[:, 2], t['par_rows'][2]).then_inc(rows_in, 16)
                pool.dma_start(w1s[:], t['rw_w1'][0].rearrange("(k p) n -> p k n", p=P)).then_inc(lora_in, 16)
                pool.dma_start(a1s[:], t['rw_a1'][0].rearrange("(k p) n -> p k n", p=P)).then_inc(lora_in, 16)
                pool.wait_ge(norm_xs, 2)
                pool.dma_start(g1s[:], t['rw_g1'][0].rearrange("(k p) n -> p k n", p=P)).then_inc(lora_in, 16)
                for n in range(3 * NS):
                    u, s = divmod(n, NS)
                    pool.wait_ge(acc_free, n + 1)
                    pool.dma_start(rkv[u].rearrange("(t p) d -> p t d", p=P)[:, :, s * SLAB:(s + 1) * SLAB],
                                   stage[:, n % 2]).then_inc(rkv_out[n % 2], 16)
                for i in range(2):
                    pool.wait_ge(rkv_out[i], 16 * (3 * NS // 2))

            def rkv_evac(act, n):
                act.wait_ge(w_used, CPS * (n + 1))
                if n >= 2:
                    act.wait_ge(rkv_out[n % 2], 16 * (n // 2))
                nc.scalar.activation(stage[:, n % 2, 0], bank[2 * (n % 2)][:], ACT.Copy)
                nc.scalar.activation(stage[:, n % 2, 1], bank[2 * (n % 2) + 1][:], ACT.Copy)\
                    .then_inc(acc_free, 1)

            @block.scalar
            def _(act):
                act_norm_sum(act, 0, lambda e: e.wait_ge(x_in, 16), xs)
                act_norm_sqrt(act, 0)
                act.wait_ge(par_ready, 1)
                for k in range(KT):
                    if k % 2 == 0:
                        act.wait_ge(norm_T, k // 2 + 1)
                    if k == 0:
                        act.wait_ge(pad_set, 1)
                    nc.scalar.activation(xnT[:, k, 1:T + 1], bank[k // 2][:, (k % 2) * T:(k % 2 + 1) * T], ACT.Copy,
                                         scale=col('a_norm_g', k)).then_inc(xn_ready, 1)
                split_hi(act, 0, 0, 0)
                for k in range(KT):
                    act.wait_ge(mixed, k + 1)
                    nc.scalar.activation(xah[:, k], mix[:, k % 2, 0], ACT.Copy).then_inc(mix_hi, 1)
                act.wait_ge(mix_used, KT)
                nc.scalar.activation(lora_h[0:LW, 0], bank[4][0:LW, 0:T], ACT.Tanh)
                nc.scalar.activation(lora_h[:, 1], bank[5][:, 0:T], ACT.Copy)
                for j in range(2):
                    last = nc.scalar.activation(lora_h[:, 2 + j], bank[6 + j][:, 0:T], ACT.Sigmoid)
                last.then_inc(lora_ready, 1)
                for G in range(1, 3 * NS * CPS):
                    c = G % CPS
                    split_hi(act, G, G // RING, c)
                    if c == 2 and G >= CPS:
                        rkv_evac(act, G // CPS - 1)
                    if G % 2 == 1 and 1 <= G // 32 + 1 <= 2:
                        n = KT * (G // 32 + 1) + (G % 32) // 2
                        act.wait_ge(mixed, n + 1)
                        xh = (xbh, xah)[G // 32]
                        nc.scalar.activation(xh[:, n % KT], mix[:, n % 2, 0], ACT.Copy).then_inc(mix_hi, 1)
                rkv_evac(act, 3 * NS - 1)

            @block.vector
            def _(dve):
                dve.wait_ge(par_T, 1)
                nc.vector.tensor_copy(par[:].rearrange("p (a n) -> p a n", a=3),
                                      bank[7][:, 0:3 * PROW].rearrange("p (a n) -> p a n", a=3)).then_inc(par_ready, 1)
                dve_norm(dve, 0, xs)
                dve.wait_ge(par_ready, 1)
                dve.wait_ge(norm_T, 8)
                for k in range(KT):
                    dve.wait_ge(xn_ready, k + 1)
                    nc.vector.tensor_tensor(out=xx[:, k], in0=xnT[:, k, 0:T], in1=xnT[:, k, 1:T + 1],
                                            op=ALU.subtract).then_inc(xx_ready, 1)

                def lo(k, n, xh, xl):
                    dve.wait_ge(mix_hi, n + 1)
                    nc.vector.tensor_tensor(out=xl[:, k], in0=mix[:, n % 2, 0], in1=xh[:, k].bitcast(F32),
                                            op=ALU.subtract).then_inc(mix_lo, 1)

                def blend(dst, k, name):
                    return nc.vector.scalar_tensor_tensor(out=dst, in0=xx[:, k], scalar=col(MU[name], k),
                                                          in1=xnT[:, k, 1:T + 1], op0=ALU.mult, op1=ALU.add)
                for k in range(KT):
                    dve.wait_ge(xx_ready, k + 1)
                    if k >= 2:
                        dve.wait_ge(mix_used, k - 1)
                    if k >= 2:
                        dve.wait_ge(mix_lo, k - 1)
                    for j, name in enumerate('rwag'):
                        last = blend(mix[:, k % 2, j], k, name)
                    last.then_inc(mixed, 1)
                    if k:
                        lo(k - 1, k - 1, xah, xal)
                lo(KT - 1, KT - 1, xah, xal)
                for G in range(3 * NS * CPS):
                    c = G % CPS
                    split_lo(dve, G, c)
                    if G % 2 == 0 and G // 32 < 2:
                        k = (G % 32) // 2
                        n = KT * (G // 32 + 1) + k
                        if n == KT:
                            dve.wait_ge(mix_used, KT)
                        dve.wait_ge(mix_lo, n - 1)
                        blend(mix[:, n % 2, 0], k, 'kv'[G // 32]).then_inc(mixed, 1)
                        if G // 32 == 1 and k == 0:
                            dve.wait_ge(w_used, NS * CPS)
                    if G % 2 == 1 and G // 32 < 2:
                        k = (G % 32) // 2
                        xh, xl = ((xbh, xbl), (xah, xal))[G // 32]
                        lo(k, KT * (G // 32 + 1) + k, xh, xl)

            @block.tensor
            def _(pe):
                pe.wait_ge(consts_in, 16)
                pe.wait_ge(rows_in, 48)
                for a in range(3):
                    last = nc.tensor.transpose(bank[7][:, a * PROW:(a + 1) * PROW], prow[:, a], ident[0:PROW, 0:PROW])
                last.then_inc(par_T, 1)
                pe.wait_ge(par_ready, 1)
                pe_norm(pe, 0, xs)
                pe.wait_ge(lora_in, 48)
                pe.wait_ge(xn_ready, KT)
                for k in range(KT):
                    pe.wait_ge(mixed, k + 1)
                    first, end = k == 0, k == KT - 1
                    nc.tensor.matmul(bank[4][0:LW, 0:T], w1s[:, k], mix[:, k % 2, 1], start=first, stop=end)
                    nc.tensor.matmul(bank[5][:, 0:T], a1s[:, k], mix[:, k % 2, 2], start=first, stop=end)
                    for j in range(2):
                        last = nc.tensor.matmul(bank[6 + j][:, 0:T], g1s[:, k, j * P:(j + 1) * P], mix[:, k % 2, 3],
                                                start=first, stop=end)
                    last.then_inc(mix_used, 1)
                for u, (xh, xl), n in zip(units, ((xah, xal), (xbh, xbl), (xah, xal)), (1, 2, 3)):
                    pe.wait_ge(mix_lo, KT * n)
                    pe_unit(pe, u, xh, xl)


        cursor = [XA_AT]

        def place(name, shape, dt=F32):
            n = 4 * math.prod(shape[1:])
            cursor[0] += n
            assert cursor[0] <= LH_AT
            return at(name, cursor[0] - n, shape, dt)

        UN = 2 * PAIRS * TT
        NCH = T // CH
        rkvg = at("rkvg", H_AT, [P, 3, TT, SLAB])
        vtok = at("vtok", H_AT + 12288, [P, TT, SLAB])
        gp = place("gp", [P, 8, PAIRS])
        gpe = place("gpe", [P, 2, PAIRS])
        pcb = place("pcb", [P, PAIRS * T // CH])
        zeros = place("zeros", [P, CH])
        rT, kT, vT, gT, dec, aT, nkk, tmp = (place(n, [P, PAIRS, T]) for n in
                                             ("rT", "kT", "vT", "gT", "dec", "aT", "nkk", "tmp"))
        prod = place("prod", [P, PAIRS * NCH, CH + 1])
        ipr = place("ipr", [P, PAIRS, T])
        ar = place("ar", [P, PAIRS, TT, 2, P])
        bt, kt_ = place("bt", [P, PAIRS, T]), place("kt_", [P, PAIRS, T])
        bh, kh = place("bh", [P, TT, SLAB]), place("kh", [P, TT, SLAB])
        Lm = place("Lm", [P, UN, P])
        X_AT = cursor[0]
        X, XT = place("X", [P, UN, P]), place("XT", [P, UN, P])
        Z_AT = cursor[0]
        Z = place("Z", [P, UN, P])
        mk = place("mk", [P, UN, 2, P])
        rbt = place("rbt", [P, UN, P])
        sd = place("sd", [P, PAIRS, 2, CH])
        sp_ = place("sp_", [P, PAIRS, CH])
        w1b, sab = place("w1b", [P, SLAB]), place("sab", [P, SLAB])
        w2g, a2g, g2g = place("w2g", [LW, SLAB]), place("a2g", [P, SLAB]), place("g2g", [P, 2, SLAB])
        yT, bvE, gE = (place(n, [P, PAIRS, T]) for n in ("yT", "bvE", "gE"))
        dT = at("dT", Z_AT, [P, PAIRS, T])
        etmp = at("etmp", Z_AT + 4096, [P, PAIRS, T])
        idec = at("idec", X_AT, [P, PAIRS, T])
        NPC = PAIRS * NCH
        NPRO, NACT, NDVE = 16, 12, 4

        def unit(h, pair, tt):
            return h * 8 + pair * 2 + tt

        rkvg_in = sem("rkvg_in")
        l2_in = sem("l2_in")
        vtok_ready = sem("vtok_ready")
        zero_set = sem("zero_set")
        pro_ps, pro_act, pro_dve = sem("pro_ps"), sem("pro_act"), sem("pro_dve")
        gp_copied, gp_ready, gpe_ready = sem("gp_copied"), sem("gp_ready"), sem("gpe_ready")
        kk_raw, kk_std, kk_rec, kkn_ready = sem("kk_raw"), sem("kk_std"), sem("kk_rec"), sem("kkn_ready")
        kfac, kmod_ready = sem("kfac"), sem("kmod_ready")
        idec_ready, dec_ready = sem("idec_ready"), sem("dec_ready")
        prod_ready, ipr_part = sem("prod_ready"), sem("ipr_part")
        bon_ready = sem("bon_ready")
        bt_raw, bk_ready = sem("bt_raw"), sem("bk_ready")
        factors_ready = sem("factors_ready")
        pcb_ready, sd_zero = sem("pcb_ready"), sem("sd_zero")
        s3_ps = sem("s3_ps")
        s3_read = sem("s3_read")
        l_ps, l_ready = sem("l_ps"), sem("l_ready")
        x0_ready = sem("x0_ready")
        z_ps, z_ready, x_ps, x_ready = sem("z_ps"), sem("z_ready"), sem("x_ps"), sem("x_ready")
        hat_ready, hat_ps, hat_read = sem("hat_ready"), sem("hat_ps"), sem("hat_read")
        kept = sem("kept")
        w1_ps, w1_ready, sa_ps, sa_ready = sem("w1_ps"), sem("w1_ready"), sem("sa_ps"), sem("sa_ready")
        sp_ready, s_ps, s_ready, y_ps, y_ready = (sem(n) for n in ("sp_ready", "s_ps", "s_ready", "y_ps", "y_ready"))
        mean_ps, d_ready, d_sq, var_ps, var_ready, std_ready, e_rec = (sem(n) for n in (
            "mean_ps", "d_ready", "d_sq", "var_ps", "var_ready", "std_ready", "e_rec"))
        d_normed, gn_ready, bonused, o_ready, o_hi = (sem(n) for n in (
            "d_normed", "gn_ready", "bonused", "o_ready", "o_hi"))
        grp_done = sem("grp_done")
        NLV = len(LEVELS)

        def bc(ap, n):
            return ap.unsqueeze(1).to_broadcast([ap.shape[0], n, ap.shape[-1]])

        with nc.Block() as block:
            @block.sync
            def _(sp):
                def load(n, first):
                    if not first:
                        sp.wait_ge(pro_ps, n * NPRO)
                        sp.wait_ge(vtok_ready, n)
                    cols = bass.ds(n * SLAB, SLAB)
                    for u in (1, 0, 2):
                        sp.dma_start(rkvg[:, u], rkv[u].rearrange("(t p) d -> p t d", p=P)[:, :, cols])\
                            .then_inc(rkvg_in, 16)
                    sp.dma_start(w2g[:], t['rw_w2'][0][:, cols]).then_inc(l2_in, 16)
                    sp.dma_start(a2g[:], t['rw_a2'][0][:, cols]).then_inc(l2_in, 16)
                    sp.dma_start(g2g[:], t['rw_g2'][0].rearrange("(k p) n -> p k n", p=P)[:, :, cols])\
                        .then_inc(l2_in, 16)
                load(0, True)
                with sp.Fori(1, NGRP) as n:
                    load(n, False)

            @block.gpsimd
            def _(pool):
                nc.gpsimd.memset(prod[:, :, 0:1], 1.0)
                nc.gpsimd.memset(sab[:], 0.0)
                nc.gpsimd.memset(w1b[:], 0.0)
                nc.gpsimd.memset(zeros[:], 0.0).then_inc(zero_set, 1)

                def factors(n):
                    pool.wait_ge(ipr_part, (n + 1) * NPC)
                    pool.wait_ge(kmod_ready, n + 1)
                    nc.gpsimd.tensor_tensor(out=kt_[:], in0=kT[:], in1=ipr[:], op=ALU.mult)
                    pool.wait_ge(kkn_ready, n + 1)
                    nc.gpsimd.tensor_tensor(out=bt[:], in0=aT[:], in1=nkk[:], op=ALU.mult).then_inc(bt_raw, 1)
                    pool.wait_ge(bt_raw, n + 1)
                    nc.gpsimd.tensor_tensor(out=bt[:], in0=bt[:], in1=ipr[:], op=ALU.mult).then_inc(bk_ready, 1)

                def epilogue(e):
                    pool.wait_ge(gn_ready, e + 1)
                    pool.wait_ge(kept, e + 1)
                    nc.gpsimd.tensor_tensor(out=dT[:], in0=dT[:], in1=bvE[:], op=ALU.add).then_inc(bonused, 1)
                    pool.wait_ge(bonused, e + 1)
                    nc.gpsimd.tensor_tensor(out=dT[:], in0=dT[:], in1=gE[:], op=ALU.mult).then_inc(o_ready, 1)

                def group(g, first, last):
                    if not first:
                        epilogue(g - 1)
                        pool.wait_ge(o_ready, g)
                    for q in range(4):
                        us = slice(4 * q, 4 * q + 4)
                        pool.wait_ge(l_ready, g * 4 + q + 1)
                        nc.gpsimd.tensor_tensor(out=X[:, us], in0=Lm[:, us], in1=bc(cst[:, C_L1:C_L1 + P], 4),
                                                op=ALU.mult).then_inc(x0_ready, 1)
                        pool.wait_ge(x0_ready, g * 8 + 2 * q + 1)
                        nc.gpsimd.tensor_tensor(out=XT[:, us], in0=XT[:, us], in1=bc(ident, 4), op=ALU.add)
                        nc.gpsimd.tensor_tensor(out=X[:, us], in0=X[:, us], in1=bc(ident, 4),
                                                op=ALU.add).then_inc(x0_ready, 1)
                    if not last:
                        pool.wait_ge(hat_ps, g * 2 + 2)
                        factors(g + 1)

                factors(0)
                group(0, True, False)
                with pool.Fori(1, NGRP - 1) as g:
                    group(g, False, False)
                group(NGRP - 1, False, True)
                epilogue(NGRP - 1)

            @block.scalar
            def _(act):
                def pro_bank(i):
                    return bank[1 + i % 3]

                def half(b, j):
                    return b[:, 2 * j:2 * j + 2].rearrange("p a n -> p (a n)")

                def pro_k(n):
                    act.wait_ge(gp_ready, n + 1)
                    for j in range(2):
                        act.wait_ge(pro_ps, n * NPRO + j + 1)
                        for p in range(2):
                            nc.scalar.activation(tmp[:, 2 * j + p], pro_bank(j)[:, p * T:(p + 1) * T], ACT.Square,
                                                 scale=gp[:, 2, 2 * j + p:2 * j + p + 1])
                        nc.scalar.activation(half(kT, j), pro_bank(j)[:], ACT.Copy).then_inc(pro_act, 1)

                def pro_sigmoid(n, i, dst, row, j):
                    act.wait_ge(pro_ps, n * NPRO + i + 1)
                    for p in range(2):
                        q = 2 * j + p
                        last = nc.scalar.activation(dst[:, q], pro_bank(i)[:, p * T:(p + 1) * T], ACT.Sigmoid,
                                                    bias=gp[:, row, q:q + 1])
                    last.then_inc(pro_act, 1)

                def pro_decay(n):
                    act.wait_ge(pro_act, n * NACT + 6)
                    nc.scalar.activation(idec[:], dec[:], ACT.Exp, scale=math.exp(-0.5)).then_inc(idec_ready, 1)
                    act.wait_ge(idec_ready, n + 1)
                    nc.scalar.activation(dec[:], dec[:], ACT.Exp, scale=-math.exp(-0.5)).then_inc(dec_ready, 1)

                def pro_copy(n, i, dst, j):
                    act.wait_ge(pro_ps, n * NPRO + i + 1)
                    nc.scalar.activation(half(dst, j), pro_bank(i)[:], ACT.Copy).then_inc(pro_act, 1)

                def pro_std(n):
                    act.wait_ge(pro_dve, n * NDVE + 2)
                    nc.scalar.activation(tmp[:], tmp[:], ACT.Sqrt).then_inc(kk_std, 1)

                def prologue(n, c):
                    if c == 0:
                        pro_k(n)
                        pro_sigmoid(n, 2, dec, 0, 0)
                    if c == 1:
                        pro_sigmoid(n, 3, dec, 0, 1)
                        pro_sigmoid(n, 4, aT, 1, 0)
                        pro_sigmoid(n, 5, aT, 1, 1)
                        pro_decay(n)
                    if c == 2:
                        pro_copy(n, 8, rT, 0)
                        pro_copy(n, 9, rT, 1)
                        pro_std(n)
                        pro_copy(n, 10, vT, 0)
                    if c == 3:
                        pro_copy(n, 11, vT, 1)
                        pro_copy(n, 12, gT, 0)
                        pro_copy(n, 13, gT, 1)

                def square(e):
                    act.wait_ge(d_ready, e + 1)
                    nc.scalar.activation(etmp[:], dT[:], ACT.Square).then_inc(d_sq, 1)

                def std(e):
                    act.wait_ge(var_ready, e + 1)
                    nc.scalar.activation(etmp[:], etmp[:], ACT.Sqrt).then_inc(std_ready, 1)

                def upper(e):
                    act.wait_ge(o_ready, e + 1)
                    nc.scalar.activation(xbh[:, bass.ds(e * PAIRS, PAIRS)], dT[:], ACT.Copy).then_inc(o_hi, 1)

                def group(g, first, last):
                    if not first:
                        act.wait_ge(y_ps, g * NCH)
                    act.wait_ge(rkvg_in, 16 * (g * 3 + 3))
                    nc.scalar.activation(vtok[:], rkvg[:, 2], ACT.Copy).then_inc(vtok_ready, 1)
                    if not first:
                        square(g - 1)
                        std(g - 1)
                        upper(g - 1)
                    act.wait_ge(pro_dve, (g + 1) * NDVE)
                    nc.scalar.activation(bvE[:], vT[:], ACT.Copy)
                    act.wait_ge(pro_act, (g + 1) * NACT)
                    nc.scalar.activation(gE[:], gT[:], ACT.Copy).then_inc(kept, 1)
                    for tt in range(TT):
                        act.wait_ge(hat_ps, g * 2 + tt + 1)
                        nc.scalar.activation(bh[:, tt], bank[tt][:], ACT.Copy)
                        nc.scalar.activation(kh[:, tt], bank[2 + tt][:], ACT.Copy).then_inc(hat_read, 1)
                    for c in range(NCH):
                        rows = slice(CH * (c % 2), CH * (c % 2) + CH)
                        act.wait_ge(w1_ps, g * NCH + c + 1)
                        nc.scalar.activation(w1b[rows], bank[4][rows], ACT.Copy).then_inc(w1_ready, 1)
                        if not last:
                            if c == 2:
                                act.wait_ge(kept, g + 1)
                            prologue(g + 1, c)
                        act.wait_ge(y_ps, g * NCH + c + 1)
                        nc.scalar.activation(yT[:, :, c * CH:(c + 1) * CH],
                                             bank[6 + c % 2][:, 0:PAIRS * CH].rearrange("p (a n) -> p a n", n=CH),
                                             ACT.Copy).then_inc(y_ready, 1)

                for c in range(NCH):
                    prologue(0, c)
                group(0, True, False)
                with act.Fori(1, NGRP - 1) as g:
                    group(g, False, False)
                group(NGRP - 1, False, True)
                square(NGRP - 1)
                std(NGRP - 1)
                upper(NGRP - 1)

            @block.vector
            def _(dve):
                flat = lambda b: b[:].rearrange("p a n -> p (a n)")
                halfof = lambda b, j: b[:, 2 * j:2 * j + 2].rearrange("p a n -> p (a n)")
                pro_bank = lambda i: bank[1 + i % 3]
                parv = par[:].rearrange("p (a k) -> p a k", k=KT)
                first_p = PARAMS.index('rw_w0')
                chunked = lambda b: b[:].rearrange("p a (c n) -> p (a c) n", n=CH)
                tiled = lambda x: ar[:, :, :, x].rearrange("p a t (c n) -> p (a t) c n", n=CH)
                tile3 = lambda b: b[:].rearrange("p a (t c n) -> p (a t) c n", t=TT, n=CH)
                pr3 = prod[:].rearrange("p (a c) n -> p a c n", c=2)

                def pro_params(n):
                    nc.vector.tensor_copy(gp[:, 0:5], parv[:, first_p:first_p + 5, bass.ds(n * PAIRS, PAIRS)])\
                        .then_inc(gp_copied, 1)
                    dve.wait_ge(gp_copied, n + 1)
                    nc.vector.tensor_scalar(gp[:, 5], gp[:, 3], -1.0, 1.0, ALU.mult, ALU.add).then_inc(gp_ready, 1)

                def pro_kk(n):
                    dve.wait_ge(pro_act, n * NACT + 2)
                    for p in range(PAIRS):
                        last = nc.vector.tensor_scalar(nkk[:, p], kT[:, p], gp[:, 2, p:p + 1], None, ALU.mult)
                    last.then_inc(kk_raw, 1)

                def pro_kmod(n):
                    dve.wait_ge(gp_ready, n + 1)
                    dve.wait_ge(pro_act, n * NACT + 6)
                    for p in range(PAIRS):
                        last = nc.vector.tensor_scalar(ipr[:, p], aT[:, p], gp[:, 3, p:p + 1], gp[:, 5, p:p + 1],
                                                       ALU.mult, ALU.add)
                    last.then_inc(kfac, 1)
                    dve.wait_ge(kfac, n + 1)
                    dve.wait_ge(kk_raw, n + 1)
                    nc.vector.tensor_tensor(out=kT[:], in0=kT[:], in1=ipr[:], op=ALU.mult).then_inc(kmod_ready, 1)
                    dve.wait_ge(kmod_ready, n + 1)

                def pro_scan(n, lo, hi):
                    dve.wait_ge(dec_ready, n + 1)
                    for m in range(lo, hi):
                        nc.vector.tensor_tensor_scan(prod[:, m, 1:CH + 1], chunked(dec)[:, m], zeros[:], 1.0,
                                                     ALU.mult, ALU.add).then_inc(prod_ready, 1)
                        nc.vector.tensor_tensor_scan(chunked(ipr)[:, m], chunked(idec)[:, m], zeros[:], 1.0,
                                                     ALU.mult, ALU.add).then_inc(ipr_part, 1)

                def pro_max(n, j):
                    dve.wait_ge(pro_ps, n * NPRO + 7 + j)
                    nc.vector.tensor_scalar(halfof(tmp, j), pro_bank(6 + j)[:], 1e-24, None, ALU.max)\
                        .then_inc(pro_dve, 1)

                def pro_recip(n, j):
                    dve.wait_ge(kk_std, n + 1)
                    nc.vector.reciprocal(halfof(tmp, j), halfof(tmp, j)).then_inc(kk_rec, 1)

                def pro_kkn(n):
                    dve.wait_ge(kk_rec, n * 2 + 2)
                    nc.vector.tensor_tensor(out=nkk[:], in0=nkk[:], in1=tmp[:], op=ALU.mult).then_inc(kkn_ready, 1)

                def pro_bonus(n):
                    dve.wait_ge(pro_act, n * NACT + 8)
                    dve.wait_ge(prod_ready, (n + 1) * NPC)
                    for p in range(PAIRS):
                        last = nc.vector.scalar_tensor_tensor(out=dec[:, p], in0=rT[:, p], scalar=gp[:, 4, p:p + 1],
                                                              in1=kT[:, p], op0=ALU.mult, op1=ALU.mult)
                    last.then_inc(bon_ready, 1)

                def pro_bv(n):
                    dve.wait_ge(pro_act, n * NACT + 10)
                    for j in range(2):
                        dve.wait_ge(pro_ps, n * NPRO + 15 + j)
                        last = nc.vector.tensor_tensor(out=halfof(vT, j), in0=halfof(vT, j), in1=pro_bank(14 + j)[:],
                                                       op=ALU.mult).then_inc(pro_dve, 1)
                    dve.wait_ge(pro_dve, (n + 1) * NDVE)

                def epi_d(e):
                    dve.wait_ge(y_ready, (e + 1) * NCH)
                    dve.wait_ge(mean_ps, e + 1)
                    nc.vector.tensor_copy(gpe[:], parv[:, first_p + 5:first_p + 7, bass.ds(e * PAIRS, PAIRS)])\
                        .then_inc(gpe_ready, 1)
                    for j in range(2):
                        last = nc.vector.scalar_tensor_tensor(out=halfof(dT, j), in0=bank[6 + j][:],
                                                              scalar=-1.0 / CH, in1=halfof(yT, j),
                                                              op0=ALU.mult, op1=ALU.add)
                    last.then_inc(d_ready, 1)

                def epi_var(e):
                    dve.wait_ge(var_ps, e + 1)
                    for j in range(2):
                        last = nc.vector.tensor_scalar(halfof(etmp, j), bank[6 + j][:], 1.0 / CH,
                                                       GN_EPS, ALU.mult, ALU.add)
                    last.then_inc(var_ready, 1)

                def epi_recip(e, j):
                    dve.wait_ge(std_ready, e + 1)
                    nc.vector.reciprocal(halfof(etmp, j), halfof(etmp, j)).then_inc(e_rec, 1)

                def epi_norm(e):
                    dve.wait_ge(e_rec, e * 2 + 2)
                    nc.vector.tensor_tensor(out=dT[:], in0=dT[:], in1=etmp[:], op=ALU.mult).then_inc(d_normed, 1)
                    dve.wait_ge(d_normed, e + 1)
                    dve.wait_ge(gpe_ready, e + 1)
                    for p in range(PAIRS):
                        last = nc.vector.tensor_scalar(dT[:, p], dT[:, p], gpe[:, 0, p:p + 1], gpe[:, 1, p:p + 1],
                                                       ALU.mult, ALU.add)
                    last.then_inc(gn_ready, 1)

                def epi_lower(e):
                    dve.wait_ge(o_hi, e + 1)
                    nc.vector.tensor_tensor(out=xbl[:, bass.ds(e * PAIRS, PAIRS)], in0=dT[:],
                                            in1=xbh[:, bass.ds(e * PAIRS, PAIRS)].bitcast(F32),
                                            op=ALU.subtract).then_inc(grp_done, 1)

                def group(g, first, last):
                    dve.wait_ge(prod_ready, (g + 1) * NPC)
                    dve.wait_ge(pro_act, (g + 1) * NACT)
                    dve.wait_ge(kkn_ready, g + 1)
                    if not first:
                        dve.wait_ge(y_ps, g * NCH)
                    nc.vector.tensor_tensor(out=tiled(1), in0=tile3(rT), in1=pr3[:, :, :, 1:CH + 1], op=ALU.mult)
                    nc.vector.scalar_tensor_tensor(out=tiled(0), in0=tile3(nkk), scalar=-1.0, in1=pr3[:, :, :, 0:CH],
                                                   op0=ALU.mult, op1=ALU.mult).then_inc(factors_ready, 1)
                    nc.vector.tensor_copy(pcb[:].unsqueeze(2), prod[:, :, CH:CH + 1]).then_inc(pcb_ready, 1)
                    nc.vector.memset(sd[:], 0.0).then_inc(sd_zero, 1)
                    if not first:
                        epi_d(g - 1)
                    for h_ in range(2):
                        for p in range(PAIRS):
                            j = h_ * PAIRS + p
                            dve.wait_ge(s3_ps, g * 8 + j + 1)
                            u = unit(h_, p, 0)
                            ps = bank[j % 2][:].rearrange("p (t n) -> p t n", t=2)
                            nc.vector.tensor_tensor(out=XT[:, u:u + 2], in0=ps[:, :, 0:P],
                                                    in1=bc(cst[:, C_T1:C_T1 + P], 2), op=ALU.mult)
                            nc.vector.tensor_tensor(out=rbt[:, u:u + 2], in0=ps[:, :, P:2 * P],
                                                    in1=bc(cst[:, C_CAUSAL + P:C_CAUSAL + 2 * P], 2), op=ALU.mult)
                            nc.vector.tensor_tensor(
                                out=mk[:, u:u + 2].rearrange("p t x n -> p t (x n)"),
                                in0=bank[2 + j % 2][:].rearrange("p (t n) -> p t n", t=2),
                                in1=bc(cst[:, C_CAUSAL:C_CAUSAL + 2 * P], 2), op=ALU.mult).then_inc(s3_read, 1)
                            if p % 2:
                                q = j // 2
                                dve.wait_ge(l_ps, g * 4 + q + 1)
                                nc.vector.tensor_tensor(out=Lm[:, 4 * q:4 * q + 4],
                                                        in0=bank[4 + q % 2][:].rearrange("p (t n) -> p t n", t=4),
                                                        in1=bc(cst[:, C_LOW:C_LOW + P], 4),
                                                        op=ALU.mult).then_inc(l_ready, 1)
                            if not first:
                                if j == 2:
                                    epi_var(g - 1)
                                if j in (3, 4):
                                    epi_recip(g - 1, j - 3)
                                if j == 5:
                                    epi_norm(g - 1)
                    dve.wait_ge(s3_ps, g * 8 + 8)
                    dve.wait_ge(pcb_ready, g + 1)
                    pc = pcb[:].unsqueeze(2).to_broadcast([P, NPC, CH])
                    nc.vector.tensor_tensor(out=chunked(kt_), in0=chunked(kt_), in1=pc, op=ALU.mult)
                    nc.vector.tensor_tensor(out=chunked(bt), in0=chunked(bt), in1=pc, op=ALU.mult)\
                        .then_inc(hat_ready, 1)
                    if not first:
                        epi_lower(g - 1)
                        dve.wait_ge(grp_done, g)
                    for n in range(NLV):
                        mask = cst[:, C_LV + P * n:C_LV + P * (n + 1)]
                        for q in range(4):
                            dve.wait_ge(z_ps, g * 4 * NLV + 4 * n + q + 1)
                            nc.vector.tensor_tensor(out=Z[:, 4 * q:4 * q + 4],
                                                    in0=bank[q][:].rearrange("p (t n) -> p t n", t=4),
                                                    in1=bc(mask, 4), op=ALU.mult).then_inc(z_ready, 1)
                        for q in range(4):
                            dve.wait_ge(x_ps, g * 4 * NLV + 4 * n + q + 1)
                            us = slice(4 * q, 4 * q + 4)
                            if n < NLV - 1:
                                nc.vector.tensor_tensor(out=X[:, us], in0=X[:, us], op=ALU.add,
                                                        in1=bank[6 + q % 2][:].rearrange("p (t n) -> p t n", t=4))
                            nc.vector.tensor_tensor(out=XT[:, us], in0=XT[:, us], op=ALU.add,
                                                    in1=bank[4 + q % 2][:].rearrange("p (t n) -> p t n", t=4))\
                                .then_inc(x_ready, 1)
                    if not last:
                        pro_params(g + 1)
                    for c in range(NCH):
                        rows = slice(CH * (c % 2), CH * (c % 2) + CH)
                        if c < NCH - 1:
                            if c == 0:
                                dve.wait_ge(sd_zero, g + 1)
                            for h_ in range(2):
                                hr = slice(CH * h_, CH * h_ + CH)
                                pr = pcb[hr].rearrange("p (a c) -> p a c", c=NCH)[:, :, c:c + 1]
                                ins = nc.vector.tensor_tensor(out=sp_[hr], in0=sd[hr, :, h_],
                                                              in1=pr.to_broadcast([CH, PAIRS, CH]), op=ALU.mult)
                            ins.then_inc(sp_ready, 1)
                            dve.wait_ge(sp_ready, g * (NCH - 1) + c + 1)
                        if not last:
                            if c == 1:
                                pro_kk(g + 1)
                            if c == 2:
                                pro_scan(g + 1, 0, NPC // 2)
                            if c == 3:
                                pro_recip(g + 1, 0)
                        dve.wait_ge(sa_ps, g * NCH + c + 1)
                        nc.vector.tensor_copy(sab[rows], bank[5][rows]).then_inc(sa_ready, 1)
                        if not last and c == 2:
                            pro_scan(g + 1, NPC // 2, 3 * NPC // 4)
                        if c < NCH - 1:
                            dve.wait_ge(s_ps, g * (NCH - 1) + c + 1)
                            for h_ in range(2):
                                hr = slice(CH * h_, CH * h_ + CH)
                                ins = nc.vector.tensor_tensor(
                                    out=sd[hr, :, h_], in0=sp_[hr],
                                    in1=bank[0][hr, 0:PAIRS * CH].rearrange("p (a n) -> p a n", n=CH), op=ALU.add)
                            ins.then_inc(s_ready, 1)
                            dve.wait_ge(s_ready, g * (NCH - 1) + c + 1)
                        if not last and c == 1:
                            pro_max(g + 1, 0)
                            pro_max(g + 1, 1)
                            pro_kmod(g + 1)
                    if not last:
                        pro_recip(g + 1, 1)
                        pro_kkn(g + 1)
                        pro_scan(g + 1, 3 * NPC // 4, NPC)
                        pro_bonus(g + 1)
                        pro_bv(g + 1)

                dve.wait_ge(zero_set, 1)
                pro_params(0)
                pro_kk(0)
                pro_max(0, 0)
                pro_max(0, 1)
                pro_kmod(0)
                pro_scan(0, 0, NPC)
                pro_recip(0, 0)
                pro_recip(0, 1)
                pro_kkn(0)
                pro_bonus(0)
                pro_bv(0)
                group(0, True, False)
                with dve.Fori(1, NGRP - 1) as g:
                    group(g, False, False)
                group(NGRP - 1, False, True)
                e = NGRP - 1
                epi_d(e)
                epi_var(e)
                epi_recip(e, 0)
                epi_recip(e, 1)
                epi_norm(e)
                epi_lower(e)

            @block.tensor
            def _(pe):
                ones = cst[:, C_ONES:C_ONES + P]
                halfof = lambda b, j: b[:, 2 * j:2 * j + 2].rearrange("p a n -> p (a n)")
                pro_bank = lambda i: bank[1 + i % 3]

                def turn(u, i, j):
                    for p in range(2):
                        for tt in range(TT):
                            last = nc.tensor.transpose(pro_bank(i)[:, p * T + tt * P:p * T + (tt + 1) * P],
                                                       rkvg[:, u, tt, (2 * j + p) * P:(2 * j + p + 1) * P], ident)
                    last.then_inc(pro_ps, 1)

                def lora(w, rows, x, i, j):
                    for p in range(2):
                        q = 2 * j + p
                        last = nc.tensor.matmul(pro_bank(i)[:, p * T:(p + 1) * T], w[:, q * P:(q + 1) * P],
                                                lora_h[rows, x], start=True, stop=True)
                    last.then_inc(pro_ps, 1)

                def lora_g(i, j):
                    for p in range(2):
                        q = 2 * j + p
                        for m in range(2):
                            last = nc.tensor.matmul(pro_bank(i)[:, p * T:(p + 1) * T], g2g[:, m, q * P:(q + 1) * P],
                                                    lora_h[:, 2 + m], start=(m == 0), stop=(m == 1))
                    last.then_inc(pro_ps, 1)

                def sums(x, i, j):
                    nc.tensor.matmul(pro_bank(i)[:], ones, halfof(x, j), start=True, stop=True).then_inc(pro_ps, 1)

                def pro_first(n):
                    pe.wait_ge(rkvg_in, 16 * (n * 3 + 3))
                    turn(1, 0, 0)
                    turn(1, 1, 1)
                    pe.wait_ge(l2_in, 16 * (n * 3 + 3))
                    lora(w2g, slice(0, LW), 0, 2, 0)

                def pro_wa(n):
                    pe.wait_ge(pro_act, n * NACT + 1)
                    lora(w2g, slice(0, LW), 0, 3, 1)
                    pe.wait_ge(pro_act, n * NACT + 2)
                    lora(a2g, slice(0, LA), 1, 4, 0)
                    pe.wait_ge(pro_act, n * NACT + 3)
                    lora(a2g, slice(0, LA), 1, 5, 1)

                def pro_sq(n, j):
                    pe.wait_ge(pro_act, n * NACT + 4 + j)
                    sums(tmp, 6 + j, j)

                def pro_r(n):
                    pe.wait_ge(pro_act, n * NACT + 6)
                    turn(0, 8, 0)
                    pe.wait_ge(pro_dve, n * NDVE + 1)
                    turn(0, 9, 1)

                def pro_v(n, j):
                    if j == 0:
                        pe.wait_ge(pro_dve, n * NDVE + 2)
                    else:
                        pe.wait_ge(pro_act, n * NACT + 7)
                    turn(2, 10 + j, j)

                def pro_g(n):
                    pe.wait_ge(pro_act, n * NACT + 8)
                    lora_g(12, 0)
                    pe.wait_ge(pro_act, n * NACT + 9)
                    lora_g(13, 1)

                def pro_bonus(n):
                    pe.wait_ge(bon_ready, n + 1)
                    pe.wait_ge(pro_act, n * NACT + 10)
                    sums(dec, 14, 0)
                    pe.wait_ge(pro_act, n * NACT + 11)
                    sums(dec, 15, 1)

                def epi_mean(e):
                    pe.wait_ge(y_ready, (e + 1) * NCH)
                    for j in range(2):
                        last = nc.tensor.matmul(bank[6 + j][:], ones, halfof(yT, j), start=True, stop=True)
                    last.then_inc(mean_ps, 1)

                def epi_var(e):
                    pe.wait_ge(d_sq, e + 1)
                    for j in range(2):
                        last = nc.tensor.matmul(bank[6 + j][:], ones, halfof(etmp, j), start=True, stop=True)
                    last.then_inc(var_ps, 1)

                def group(g, first, last_):
                    if not first:
                        epi_mean(g - 1)
                    pe.wait_ge(factors_ready, g + 1)
                    pe.wait_ge(bk_ready, g + 1)
                    pe.wait_ge(pro_dve, (g + 1) * NDVE)
                    pe.wait_ge(pro_act, (g + 1) * NACT)
                    for h_ in range(2):
                        hr = slice(CH * h_, CH * h_ + CH)
                        for p in range(PAIRS):
                            j = h_ * PAIRS + p
                            if j >= 2:
                                pe.wait_ge(s3_read, g * 8 + j - 1)
                            for x, b0 in ((bt, 0), (kt_, 2)):
                                for tt in range(TT):
                                    last = nc.tensor.matmul(bank[b0 + j % 2][:, tt * T:(tt + 1) * T],
                                                            x[hr, p, tt * P:(tt + 1) * P],
                                                            ar[hr, p, tt].rearrange("p x n -> p (x n)"),
                                                            start=True, stop=True)
                            last.then_inc(s3_ps, 1)
                            q = j // 2
                            if p % 2 == 0 and q >= 2:
                                pe.wait_ge(l_ready, g * 4 + q - 1)
                            for tt in range(TT):
                                last = nc.tensor.matmul(bank[4 + q % 2][:, (p % 2) * T + tt * P:(p % 2) * T + (tt + 1) * P],
                                                        ar[hr, p, tt, 0], bt[hr, p, tt * P:(tt + 1) * P],
                                                        start=True, stop=True)
                            if p % 2:
                                last.then_inc(l_ps, 1)
                            if j == 1 and not first:
                                epi_var(g - 1)
                    pe.wait_ge(s3_read, g * 8 + 8)
                    for n in range(NLV):
                        for q in range(4):
                            if n == 0:
                                pe.wait_ge(x0_ready, g * 8 + 2 * q + 2)
                            else:
                                pe.wait_ge(x_ready, g * 4 * NLV + 4 * (n - 1) + q + 1)
                            for k in range(4):
                                u = 4 * q + k
                                last = nc.tensor.matmul(bank[q][:, k * P:(k + 1) * P], Lm[:, u], XT[:, u],
                                                        start=True, stop=True)
                            last.then_inc(z_ps, 1)
                        for q in range(4):
                            pe.wait_ge(z_ready, g * 4 * NLV + 4 * n + q + 1)
                            if q >= 2:
                                pe.wait_ge(x_ready, g * 4 * NLV + 4 * n + q - 1)
                            for k in range(4):
                                u = 4 * q + k
                                last = nc.tensor.matmul(bank[4 + q % 2][:, k * P:(k + 1) * P], X[:, u], Z[:, u],
                                                        start=True, stop=True)
                                if n < NLV - 1:
                                    last = nc.tensor.matmul(bank[6 + q % 2][:, k * P:(k + 1) * P], Z[:, u], X[:, u],
                                                            start=True, stop=True)
                            last.then_inc(x_ps, 1)
                    pe.wait_ge(hat_ready, g + 1)
                    for tt in range(TT):
                        for p in range(PAIRS):
                            nc.tensor.transpose(bank[tt][:, p * P:(p + 1) * P], bt[:, p, tt * P:(tt + 1) * P], ident)
                        for p in range(PAIRS):
                            last = nc.tensor.transpose(bank[2 + tt][:, p * P:(p + 1) * P],
                                                       kt_[:, p, tt * P:(tt + 1) * P], ident)
                        last.then_inc(hat_ps, 1)
                    pe.wait_ge(x_ready, (g + 1) * 4 * NLV)
                    pe.wait_ge(sd_zero, g + 1)
                    pe.wait_ge(vtok_ready, g + 1)
                    pe.wait_ge(hat_read, g * 2 + 2)
                    if not last_:
                        pro_first(g + 1)
                    for c in range(NCH):
                        tt, half = divmod(c, 2)
                        rows = slice(CH * half, CH * half + CH)
                        v_of = lambda p, h_: vtok[:, tt, p * P + h_ * CH:p * P + (h_ + 1) * CH]
                        if c:
                            pe.wait_ge(s_ready, g * (NCH - 1) + c)
                        for p in range(PAIRS):
                            nc.tensor.matmul(bank[4][rows, p * P:(p + 1) * P], ar[:, p, tt, 0, rows],
                                             sd[:, p].rearrange("p x n -> p (x n)"), start=True, stop=False)
                            for h_ in range(2):
                                last = nc.tensor.matmul(bank[4][rows, p * P + h_ * CH:p * P + (h_ + 1) * CH],
                                                        mk[:, unit(h_, p, tt), 0, rows], v_of(p, h_),
                                                        start=False, stop=(h_ == 1))
                        last.then_inc(w1_ps, 1)
                        if c >= 2:
                            pe.wait_ge(y_ready, g * NCH + c - 1)
                        for p in range(PAIRS):
                            yb = bank[6 + c % 2]
                            nc.tensor.matmul(yb[:, p * CH:(p + 1) * CH], sd[:, p].rearrange("p x n -> p (x n)"),
                                             ar[:, p, tt, 1, rows], start=(p == 0), stop=False, skip_group_check=True)
                            for h_ in range(2):
                                nc.tensor.matmul(yb[h_ * CH:(h_ + 1) * CH, p * CH:(p + 1) * CH], v_of(p, h_),
                                                 mk[:, unit(h_, p, tt), 1, rows], start=False, stop=False,
                                                 skip_group_check=True)
                        if not last_:
                            if c == 1:
                                pro_sq(g + 1, 0)
                            if c == 2:
                                pro_v(g + 1, 0)
                        pe.wait_ge(w1_ready, g * NCH + c + 1)
                        for p in range(PAIRS):
                            for h_ in range(2):
                                cs = slice(p * P + h_ * CH, p * P + (h_ + 1) * CH)
                                last = nc.tensor.matmul(bank[5][rows, cs], XT[:, unit(h_, p, tt), rows],
                                                        w1b[:, cs], start=True, stop=True)
                        last.then_inc(sa_ps, 1)
                        pe.wait_ge(sa_ready, g * NCH + c + 1)
                        def y_sa(p, h_):
                            cs = slice(p * P + h_ * CH, p * P + (h_ + 1) * CH)
                            return nc.tensor.matmul(bank[6 + c % 2][h_ * CH:(h_ + 1) * CH, p * CH:(p + 1) * CH],
                                                    sab[:, cs], rbt[:, unit(h_, p, tt), rows], start=False,
                                                    stop=(p == PAIRS - 1), skip_group_check=True)
                        y_sa(0, 0)
                        if c < NCH - 1:
                            for p in range(PAIRS):
                                for h_ in range(2):
                                    cs = slice(p * P + h_ * CH, p * P + (h_ + 1) * CH)
                                    out = bank[0][h_ * CH:(h_ + 1) * CH, p * CH:(p + 1) * CH]
                                    nc.tensor.matmul(out, bh[rows, tt, cs], sab[rows, cs], start=True, stop=False)
                                    last = nc.tensor.matmul(out, kh[rows, tt, cs], vtok[rows, tt, cs],
                                                            start=False, stop=True)
                            last.then_inc(s_ps, 1)
                        for p in range(PAIRS):
                            for h_ in range(2):
                                if p or h_:
                                    last = y_sa(p, h_)
                        last.then_inc(y_ps, 1)
                        if not last_:
                            if c == 0:
                                pro_wa(g + 1)
                            if c == 1:
                                pro_sq(g + 1, 1)
                                pro_r(g + 1)
                            if c == 2:
                                pro_v(g + 1, 1)
                                pro_g(g + 1)
                            if c == 3:
                                pro_bonus(g + 1)

                pro_first(0)
                pro_wa(0)
                pro_sq(0, 0)
                pro_sq(0, 1)
                pro_r(0)
                pro_v(0, 0)
                pro_v(0, 1)
                pro_g(0)
                pro_bonus(0)
                group(0, True, False)
                with pe.Fori(1, NGRP - 1) as g:
                    group(g, False, False)
                group(NGRP - 1, False, True)
                epi_mean(NGRP - 1)
                epi_var(NGRP - 1)

        xs2 = at("xs2", WORK, [P, TT, D])
        u_ = at("u_", WORK + 16384, [P, 2, TT, SLAB])
        u2 = at("u2", WORK + 24576, [P, 2, TT, SLAB])
        kvs = at("kvs", WORK + 16384, [P, TT, 6, SLAB])
        qs = at("qs", WORK + 40960, [P, TT, D])
        gw = at("gw", WORK + 57344, [P, KT, 48])
        gwh = at("gwh", WORK + 60416, [P, KT, 48], F32R)
        gwl = at("gwl", WORK + 63488, [P, KT, 48], F32R)
        gates = at("gates", WORK + 66560, [P, TT, 48])

        h_in = sem("h_in")
        norm_hi, norm_lo = sem("norm_hi"), sem("norm_lo")
        sq_ready, hT_ps, hT_hi, hT_lo = sem("sq_ready"), sem("hT_ps"), sem("hT_hi"), sem("hT_lo")
        h_done = sem("h_done")
        gw_in, gw_hi, gw_lo, gate_ps = sem("gw_in"), sem("gw_hi"), sem("gw_lo"), sem("gate_ps")
        splits = {'n': 0}
        HPG = NS * 2
        CPG = HPG * CPS

        def act_split_norm(act, n, base, name, xh, again=False):
            for k in range(KT):
                act.wait_ge(norm_T, 8 * n + k // 2 + 1)
                if again:
                    act.wait_ge(norm_lo, base - KT + (k | 1) + 1)
                nc.scalar.activation(xh[:, k], bank[k // 2][:, (k % 2) * T:(k % 2 + 1) * T], ACT.Copy,
                                     scale=col(name, k)).then_inc(norm_hi, 1)

        def dve_split_norm(dve, base, name, xh, xl):
            for k in range(KT):
                dve.wait_ge(norm_hi, base + (k | 1) + 1)
                nc.vector.scalar_tensor_tensor(out=xl[:, k], in0=bank[k // 2][:, (k % 2) * T:(k % 2 + 1) * T],
                                               scalar=col(name, k), in1=xh[:, k].bitcast(F32),
                                               op0=ALU.mult, op1=ALU.subtract).then_inc(norm_lo, 1)

        def add_slab(dve, S, s, half):
            dve.wait_ge(w_used, CPS * S + CPS)
            for tt in range(TT):
                last = nc.vector.tensor_tensor(out=h[:, tt, s * SLAB:(s + 1) * SLAB],
                                               in0=h[:, tt, s * SLAB:(s + 1) * SLAB],
                                               in1=bank[2 * half + tt][:], op=ALU.add)
            last.then_inc(acc_free, 1)

        def act_mlp(act, layer, cb, sb):
            with act.Fori(0, NG) as g:
                for s in range(HPG):
                    for c in range(CPS):
                        split_hi(act, g * CPG + cb + s * CPS + c, g * (CPG // RING) + (cb + s * CPS + c) // RING, c)
                        if c == 2 and 1 <= s <= NS:
                            half = (s - 1) % 2
                            act.wait_ge(w_used, g * CPG + cb + s * CPS)
                            if s >= 3:
                                act.wait_ge(sq_ready, g * NS + layer * NG * NS + s - 2)
                            for tt in range(TT):
                                last = nc.scalar.activation(u_[:, half, tt], bank[2 * half + tt][:], ACT.Relu)
                            last.then_inc(acc_free, 1)
                        if c == CPS - 1 and 1 <= s <= NS:
                            n = g * NS + layer * NG * NS + s
                            act.wait_ge(hT_ps, n)
                            for j in range(2):
                                last = nc.scalar.activation(
                                    xbh[:, (s - 1) * 4 + 2 * j:(s - 1) * 4 + 2 * j + 2].rearrange("p a n -> p (a n)"),
                                    bank[4 + j][:], ACT.Copy)
                            last.then_inc(hT_hi, 1)

        def pool_mlp(pool, layer, cb, sb):
            with pool.Fori(0, NG) as g:
                for s in range(NS):
                    pool.wait_ge(acc_free, g * HPG + sb + s + 1)
                    if layer or s >= 2:
                        pool.wait_ge(hT_ps, g * NS + layer * NG * NS + s - 1)
                    nc.gpsimd.tensor_tensor(out=u2[:, s % 2], in0=u_[:, s % 2], in1=u_[:, s % 2],
                                            op=ALU.mult).then_inc(sq_ready, 1)

        def dve_mlp(dve, layer, cb, sb):
            with dve.Fori(0, NG) as g:
                for s in range(HPG):
                    for c in range(CPS):
                        split_lo(dve, g * CPG + cb + s * CPS + c, c)
                        if c == 2 and s > NS:
                            add_slab(dve, g * HPG + sb + s - 1, s - 1 - NS, (s - 1) % 2)
                        if c == CPS - 1 and 1 <= s <= NS:
                            n = g * NS + layer * NG * NS + s
                            dve.wait_ge(hT_hi, n)
                            for j in range(2):
                                kk = slice((s - 1) * 4 + 2 * j, (s - 1) * 4 + 2 * j + 2)
                                last = nc.vector.tensor_tensor(
                                    out=xbl[:, kk].rearrange("p a n -> p (a n)"), in0=bank[4 + j][:],
                                    in1=xbh[:, kk].bitcast(F32).rearrange("p a n -> p (a n)"), op=ALU.subtract)
                            last.then_inc(hT_lo, 1)
                add_slab(dve, g * HPG + sb + HPG - 1, NS - 1, 1)

        def pe_mlp(pe, layer, cb, sb, nlo):
            with pe.Fori(0, NG) as g:
                for s in range(HPG):
                    def before(c):
                        if s < NS:
                            pe.wait_ge(norm_lo, nlo + 2 * c + 2 if s == 0 and c >= 2 else nlo + 16 if s else nlo + 4)
                        if c == 4 and 1 <= s <= NS:
                            n = g * NS + layer * NG * NS + s
                            pe.wait_ge(sq_ready, n)
                            if layer or s > 1:
                                pe.wait_ge(hT_lo, n - 1)
                            for j in range(4):
                                for tt in range(TT):
                                    last = nc.tensor.transpose(
                                        bank[4 + j // 2][:, (j % 2) * T + tt * P:(j % 2) * T + (tt + 1) * P],
                                        u2[:, (s - 1) % 2, tt, j * P:(j + 1) * P], ident)
                            last.then_inc(hT_ps, 1)
                        if s >= NS:
                            pe.wait_ge(hT_lo, g * NS + layer * NG * NS + (NS - 1 if s == NS and c < 6 else NS))
                    xh, xl = (xah, xal) if s < NS else (xbh, xbl)
                    slab_matmuls(pe, g * CPG + cb + s * CPS, g * HPG + sb + s, s % 2, xh, xl, before)

        def sp_mlp(sp, layer, cb, sb):
            with sp.Fori(0, NG) as g:
                for s in range(HPG):
                    for c in range(CPS):
                        G = g * CPG + cb + s * CPS + c
                        if s < NS:
                            load_chunk(sp, t['mlp_up'][layer], G, c, c * KC * P, g * D + s * SLAB)
                        else:
                            load_chunk(sp, t['mlp_down'][layer], G, c, g * D + c * KC * P, (s - NS) * SLAB)

        def act_unit(act, unit, evac):
            for s in range(unit['slabs']):
                for c in range(CPS):
                    G = unit['chunk'] + s * CPS + c
                    split_hi(act, G, G // RING, c)
                    if c == 2 and s:
                        evac(s - 1)
            evac(unit['slabs'] - 1)

        def dve_unit(dve, unit, evac):
            for s in range(unit['slabs']):
                for c in range(CPS):
                    split_lo(dve, unit['chunk'] + s * CPS + c, c)
                    if c == 2 and s:
                        evac(s - 1)
            evac(unit['slabs'] - 1)

        def nothing(s):
            pass

        u_wo = new_unit(NS)
        mlp0 = dict(stream)
        new_unit(HPG * NG)
        u_kv = new_unit(6)
        u_q = new_unit(NS)

        with nc.Block() as block:
            @block.sync
            def _(sp):
                sp.dma_start(h[:], t['x'].rearrange("b (t p) d -> p (b t) d", p=P)).then_inc(h_in, 16)
                sp_unit(sp, t['rw_wo'][0], u_wo)
                sp_mlp(sp, 0, mlp0['chunk'], mlp0['slab'])
                sp_unit(sp, t['w_kv'], u_kv)
                sp_unit(sp, t['nsa_wq'][0], u_q)

            @block.gpsimd
            def _(pool):
                pool.dma_start(gw[:], t['nsa_wq'][0][:, D:D + 48].rearrange("(k p) n -> p k n", p=P))\
                    .then_inc(gw_in, 16)
                pool_mlp(pool, 0, mlp0['chunk'], mlp0['slab'])

            @block.scalar
            def _(act):
                act_unit(act, u_wo, nothing)
                act_norm_sum(act, 1, lambda e: e.wait_ge(acc_free, mlp0['slab']), xs2)
                act_norm_sqrt(act, 1)
                act_split_norm(act, 1, 0, 'm0', xah)
                act_mlp(act, 0, mlp0['chunk'], mlp0['slab'])
                act_norm_sum(act, 2, lambda e: e.wait_ge(acc_free, u_kv['slab']), xs2)
                act_norm_sqrt(act, 2)
                act_split_norm(act, 2, KT, 'kv_norm_g', xah)
                act_split_norm(act, 2, 2 * KT, 'b_norm_g', xbh, again=True)
                act.wait_ge(gw_in, 16)
                nc.scalar.activation(gwh[:], gw[:], ACT.Copy).then_inc(gw_hi, 1)

                def kv_evac(s):
                    act.wait_ge(w_used, u_kv['chunk'] + CPS * (s + 1))
                    for tt in range(TT):
                        last = nc.scalar.activation(kvs[:, tt, s], bank[2 * (s % 2) + tt][:], ACT.Copy)
                    last.then_inc(acc_free, 1)

                def q_evac(s):
                    act.wait_ge(w_used, u_q['chunk'] + CPS * (s + 1))
                    for tt in range(TT):
                        last = nc.scalar.activation(qs[:, tt, s * SLAB:(s + 1) * SLAB], bank[2 * (s % 2) + tt][:],
                                                    ACT.Copy, scale=HD ** -0.5)
                    last.then_inc(acc_free, 1)
                act_unit(act, u_kv, kv_evac)
                act_unit(act, u_q, q_evac)
                act.wait_ge(gate_ps, 1)
                for tt in range(TT):
                    nc.scalar.activation(gates[:, tt], bank[6 + tt][:, 0:48], ACT.Sigmoid)

            @block.vector
            def _(dve):
                dve.wait_ge(h_in, 16)
                dve_unit(dve, u_wo, lambda s: add_slab(dve, u_wo['slab'] + s, s, s % 2))
                dve_norm(dve, 1, xs2)
                dve_split_norm(dve, 0, 'm0', xah, xal)
                dve_mlp(dve, 0, mlp0['chunk'], mlp0['slab'])
                dve_norm(dve, 2, xs2)
                dve_split_norm(dve, KT, 'kv_norm_g', xah, xal)
                dve_split_norm(dve, 2 * KT, 'b_norm_g', xbh, xbl)
                dve.wait_ge(gw_hi, 1)
                nc.vector.tensor_tensor(out=gwl[:], in0=gw[:], in1=gwh[:].bitcast(F32),
                                        op=ALU.subtract).then_inc(gw_lo, 1)
                dve_unit(dve, u_kv, nothing)
                dve_unit(dve, u_q, nothing)

            @block.tensor
            def _(pe):
                pe_unit(pe, u_wo, xbh, xbl)
                pe_norm(pe, 1, xs2)
                pe_mlp(pe, 0, mlp0['chunk'], mlp0['slab'], 0)
                pe_norm(pe, 2, xs2)
                pe.wait_ge(norm_lo, 3 * KT)
                pe_unit(pe, u_kv, xah, xal)
                pe_unit(pe, u_q, xbh, xbl)
                pe.wait_ge(gw_lo, 1)
                for tt in range(TT):
                    for k in range(KT):
                        tok = slice(tt * P, (tt + 1) * P)
                        nc.tensor.matmul(bank[6 + tt][:, 0:48], xbh[:, k, tok], gwh[:, k], start=(k == 0), stop=False)
                        nc.tensor.matmul(bank[6 + tt][:, 0:48], xbh[:, k, tok], gwl[:, k], start=False, stop=False)
                        last = nc.tensor.matmul(bank[6 + tt][:, 0:48], xbl[:, k, tok], gwh[:, k], start=False,
                                                stop=(k == KT - 1))
                last.then_inc(gate_ps, 1)

        CP = (0, 1, 2, 4)
        kT4 = at("kT4", XA_AT, [P, 4, GB, T])
        xc = at("xc", XA_AT + 16384, [P, 2, 32, GB * NCB])
        cw1 = at("cw1", XA_AT + 31744, [P, 2, 32, P])
        tb = at("tb", XA_AT + 64512, [P, HB, T])
        tbr = at("tbr", XB_AT, [P, HB, T])
        qg = at("qg", XA_AT + 31744, [P, TT, SLAB])
        qT4 = at("qT4", XA_AT + 35840, [P, REP, T])
        vg = at("vg", XA_AT + 39936, [P, TT, 2, HD])
        vcg = at("vcg", XA_AT + 41984, [P, HD])
        s0 = at("s0", XA_AT + 42496, [P, 2, 2, P])
        s1 = at("s1", XA_AT + 44544, [P, 2, 2, T])
        sc = at("sc", XA_AT + 48640, [P, 2, TT, 16])
        pt1 = at("pt1", XA_AT + 48896, [P, 2, SLAB])
        pt2 = at("pt2", XA_AT + 52992, [P, 2, 256])
        ptc = at("ptc", XA_AT + 55040, [P, 2, T])
        mx = at("mx", XA_AT + 57088, [P, 2, 6])
        sm = at("sm", XA_AT + 57152, [P, 2, 6])
        cst2 = at("cst2", WORK, [P, 512 + TT])
        dist_of = cst2[0:BUCKETS + 1, 0:512]
        row_ok = cst2[:, 512:512 + TT]
        tabx = at("tabx", WORK + 4128, [BUCKETS + 1, HB])
        grow = at("grow", WORK + 4224, [HB, 512])
        tbc = at("tbc", WORK + 6272, [P, TT, HB, 16])
        cw2 = at("cw2", WORK + 8320, [P, 2, P])
        pebr = at("pebr", WORK + 9344, [66, P])
        peb = at("peb", WORK + 9856, [P, 66])
        hid = at("hid", WORK + 10144, [GB * NCB, 2, P])
        gel = at("gel", WORK + 11168, [P, 2, GB * NCB])
        kcT = at("kcT", WORK + 11680, [P, GB * NCB])
        vcs = at("vcs", WORK + 11936, [NCB, GB, HD])
        dist_scratch = nc.dram_tensor("dist_scratch", [HB, 512], F32, kind="Internal").ap()

        c2_in, cw_in, tab_in = sem("c2_in"), sem("cw_in"), sem("tab_in")
        tab_one, tb_ready = sem("tab_one"), sem("tb_ready")
        kT_ps, kT_act, kT_dve = sem("kT_ps"), sem("kT_act"), sem("kT_dve")
        peb_ps, peb_ready, dist_ps, dist_ready, dist_out, tb_in = (
            sem("peb_ps"), sem("peb_ready"), sem("dist_ps"), sem("dist_ready"), sem("dist_out"), sem("tb_in"))
        bc_ps, xc_ready, hid_ps, hid_ready, hidT_ps, gel_ready = (sem(n) for n in (
            "bc_ps", "xc_ready", "hid_ps", "hid_ready", "hidT_ps", "gel_ready"))
        kc_ps, kc_ready, gates_ok = sem("kc_ps"), sem("kc_ready"), sem("gates_ok")
        grp_in, qT_ps, qT_ready = sem("grp_in"), sem("qT_ps"), sem("qT_ready")
        pad0 = sem("pad0")
        sc_ps, biased, maxed, sums, weights, pT_ps, pT1, pT2, o_ps, oa_hi, oa_lo = (sem(n) for n in (
            "sc_ps", "biased", "maxed", "sums", "weights", "pT_ps", "pT1", "pT2", "o_ps", "oa_hi", "oa_lo"))
        alink = sem("alink")
        AL = 3 * REP

        with nc.Block() as block:
            @block.sync
            def _(sp):
                sp.dma_start(cst2[:], t['consts2']).then_inc(c2_in, 16)
                sp.dma_start(tabx[0:BUCKETS], t['rel_bias']).then_inc(tab_in, 16)
                sp.dma_start(pebr[0:64], t['cmp_pe'].rearrange("a l d -> (a l) d")).then_inc(c2_in, 16)
                sp.dma_start(pebr[64:66], t['cmp_b1']).then_inc(c2_in, 16)
                sp.dma_start(cw2[:], t['cmp_w2'].rearrange("a k n -> k a n")).then_inc(cw_in, 16)
                for a in range(2):
                    sp.dma_start(cw1[:, a], t['cmp_w1'][a].rearrange("(l d) n -> d l n", d=P)).then_inc(cw_in, 16)
                sp.wait_ge(dist_ready, 1)
                sp.dma_start(dist_scratch, grow[:]).then_inc(dist_out, 16)
                sp.wait_ge(dist_out, 16)
                for a in range(HB):
                    skew = bass.AP(tensor=dist_scratch.tensor, offset=512 * a + P + 1, ap=[[1, P], [1, T]])
                    sp.dma_start(tbr[:, a], skew).then_inc(tb_in, 16)

            @block.gpsimd
            def _(pool):
                nc.gpsimd.memset(tabx[BUCKETS:BUCKETS + 1], 1.0).then_inc(tab_one, 1)
                pool.wait_ge(kc_ready, 1)
                nc.gpsimd.memset(vcg[:], 0.0)
                nc.gpsimd.memset(ptc[:], 0.0).then_inc(pad0, 1)
                pool.wait_ge(pad0, 1)
                with pool.Fori(0, GB) as g:
                    pool.wait_ge(oa_lo, g * REP + 1)
                    nc.gpsimd.tensor_copy(qg[:], qs[:, :, bass.ds(g * SLAB, SLAB)])
                    for b in range(2):
                        nc.gpsimd.tensor_copy(vg[:, :, b], kvs[:, :, 3 + 2 * b, bass.ds(g * HD, HD)])
                    nc.gpsimd.tensor_copy(vcg[0:NCB], vcs[:, bass.ds(g, 1)].rearrange("p a n -> p (a n)"))\
                        .then_inc(grp_in, 1)

            @block.scalar
            def _(act):
                for j in range(0, 8, 2):
                    act.wait_ge(kT_ps, j + 1)
                    nc.scalar.activation(kT4[:, j // 2, (j % 2) * 2:(j % 2) * 2 + 2].rearrange("p a n -> p (a n)"),
                                         bank[j][:], ACT.Copy).then_inc(kT_act, 1)
                act.wait_ge(dist_ps, 1)
                nc.scalar.activation(grow[:], bank[1][0:HB], ACT.Copy).then_inc(dist_ready, 1)
                act.wait_ge(hid_ps, 1)
                for a in range(2):
                    last = nc.scalar.activation(hid[:, a], bank[4 + a][0:GB * NCB, 0:P], ACT.Copy)
                last.then_inc(hid_ready, 1)
                act.wait_ge(hidT_ps, 1)
                for a in range(2):
                    last = nc.scalar.activation(gel[:, a], bank[6][:, a * 64:a * 64 + GB * NCB], ACT.Gelu_apprx_tanh,
                                                bias=peb[:, 64 + a:65 + a])
                last.then_inc(gel_ready, 1)
                with act.Fori(0, GB) as g:
                    act.wait_ge(qT_ps, g + 1)
                    for j in range(2):
                        last = nc.scalar.activation(qT4[:, 2 * j:2 * j + 2].rearrange("p a n -> p (a n)"),
                                                    bank[6 + j][:], ACT.Copy)
                    last.then_inc(qT_ready, 1)

                    def exps(r):
                        b = r % 2
                        act.wait_ge(maxed, g * REP + r + 1)
                        for tt in range(TT):
                            nc.scalar.activation(sc[:, b, tt, 0:NCB], sc[:, b, tt, 0:NCB], ACT.Exp,
                                                 bias=mx[:, b, 3 * tt:3 * tt + 1], accum_out=sm[:, b, 3 * tt:3 * tt + 1])
                            for br in range(2):
                                s = (s0, s1)[tt][:, b, br]
                                n = 3 * tt + 1 + br
                                last = nc.scalar.activation(s, s, ACT.Exp, bias=mx[:, b, n:n + 1],
                                                            accum_out=sm[:, b, n:n + 1])
                        last.then_inc(sums, 1)
                    exps(0)
                    for r in range(REP):
                        if r < REP - 1:
                            exps(r + 1)
                        act.wait_ge(pT_ps, g * REP + r + 1)
                        nc.scalar.activation(pt1[:, r % 2], bank[4][:], ACT.Copy).then_inc(pT1, 1)
                        act.wait_ge(o_ps, g * REP + r + 1)
                        nc.scalar.activation(xbh[:, bass.ds(g * REP + r, 1)].rearrange("p a n -> p (a n)"),
                                             bank[6 + r % 2][:, 0:T], ACT.Copy).then_inc(oa_hi, 1)

            @block.vector
            def _(dve):
                for j in range(1, 8, 2):
                    dve.wait_ge(kT_ps, j + 1)
                    nc.vector.tensor_copy(kT4[:, j // 2, (j % 2) * 2:(j % 2) * 2 + 2].rearrange("p a n -> p (a n)"),
                                          bank[j][:]).then_inc(kT_dve, 1)
                dve.wait_ge(peb_ps, 1)
                nc.vector.tensor_copy(peb[:], bank[0][:, 0:66]).then_inc(peb_ready, 1)
                dve.wait_ge(bc_ps, 1)
                for tt in range(TT):
                    nc.vector.tensor_copy(tbc[:, tt, :, 0:NCB].rearrange("p h c -> p c h"),
                                          bank[2 + tt][:, 0:NCB * HB].rearrange("p (c h) -> p c h", h=HB))
                dve.wait_ge(c2_in, 16)
                for tt in range(TT):
                    last = nc.vector.tensor_scalar(gates[:, tt].rearrange("p (h b) -> p h b", b=3)[:, :, 0],
                                                   gates[:, tt].rearrange("p (h b) -> p h b", b=3)[:, :, 0],
                                                   row_ok[:, tt:tt + 1], None, ALU.mult)
                last.then_inc(gates_ok, 1)
                dve.wait_ge(peb_ready, 1)
                dve.wait_ge(kT_act, 4)
                dve.wait_ge(kT_dve, 4)
                for a in range(2):
                    for gg in range(GB):
                        for hf in range(2):
                            src = kT4[:, a, gg, hf * 16:hf * 16 + NCB * 16].rearrange("p (c l) -> p c l", l=16)
                            dst = xc[:, a, hf * 16:hf * 16 + 16, gg * NCB:(gg + 1) * NCB].rearrange("p l c -> p c l")
                            pe_ = peb[:, a * 32 + hf * 16:a * 32 + hf * 16 + 16]
                            last = nc.vector.tensor_tensor(out=dst, in0=src, in1=bc(pe_, NCB), op=ALU.add)
                last.then_inc(xc_ready, 1)
                dve.wait_ge(kc_ps, 1)
                nc.vector.tensor_copy(kcT[:], bank[7][:, 0:GB * NCB])
                nc.vector.tensor_copy(vcs[:].rearrange("p a n -> p (a n)"), bank[0][0:NCB]).then_inc(kc_ready, 1)
                dve.wait_ge(tb_in, 16 * (HB))
                nc.vector.tensor_copy(tb[:], tbr[:, :, ::-1]).then_inc(tb_ready, 1)
                nc.vector.memset(mx[:, 0, 0:1], 0.0).then_inc(oa_lo, 1)
                dve.wait_ge(tb_ready, 1)
                dve.wait_ge(gates_ok, 1)
                links = [0]
                with dve.Fori(0, GB) as g:
                    def link(ins):
                        links[0] += 1
                        ins.then_inc(alink, 1)
                        dve.wait_ge(alink, g * AL + links[0])

                    def bias(r):
                        b = r % 2
                        a = bass.ds(g * REP + r, 1)
                        A, B = bank[b], bank[2 + b]
                        dve.wait_ge(sc_ps, g * REP + r + 1)
                        if r >= 2:
                            dve.wait_ge(pT_ps, g * REP + r - 1)
                        nc.vector.tensor_tensor(out=s0[:, b], in0=A[:, 0:256].rearrange("p (a n) -> p a n", a=2),
                                                in1=tb[:, a, P:T].to_broadcast([P, 2, P]), op=ALU.add)
                        nc.vector.tensor_tensor(out=s1[:, b], in0=B[:].rearrange("p (a n) -> p a n", a=2),
                                                in1=tb[:, a].to_broadcast([P, 2, T]), op=ALU.add)
                        nc.vector.tensor_tensor(out=sc[:, b, :, 0:NCB],
                                                in0=A[:, 256:288].rearrange("p (a n) -> p a n", n=16)[:, :, 0:NCB],
                                                in1=tbc[:, :, a, 0:NCB].rearrange("p t a n -> p (t a) n"),
                                                op=ALU.add).then_inc(biased, 1)
                        dve.wait_ge(biased, g * REP + r + 1)
                        m3 = mx[:, b].rearrange("p (t n) -> p t n", t=2)
                        nc.vector.reduce_max(m3[:, 0, 1:3], s0[:, b], AX.X)
                        nc.vector.reduce_max(m3[:, 1, 1:3], s1[:, b], AX.X)
                        link(nc.vector.reduce_max(m3[:, :, 0], sc[:, b, :, 0:NCB], AX.X))
                        nc.vector.tensor_scalar(mx[:, b], mx[:, b], -1.0, None, ALU.mult).then_inc(maxed, 1)
                    bias(0)
                    for r in range(REP):
                        b = r % 2
                        if r < REP - 1:
                            bias(r + 1)
                        dve.wait_ge(sums, g * REP + r + 1)
                        link(nc.vector.reciprocal(sm[:, b], sm[:, b]))
                        s3 = sm[:, b].rearrange("p (t n) -> p t n", t=2)
                        link(nc.vector.tensor_tensor(out=s3, in0=s3, in1=gates[:, :, bass.ds((g * REP + r) * 3, 3)],
                                                     op=ALU.mult))
                        nc.vector.tensor_tensor(out=s0[:, b], in0=s0[:, b], op=ALU.mult,
                                                in1=sm[:, b, 1:3].unsqueeze(2).to_broadcast([P, 2, P]))
                        nc.vector.tensor_tensor(out=s1[:, b], in0=s1[:, b], op=ALU.mult,
                                                in1=sm[:, b, 4:6].unsqueeze(2).to_broadcast([P, 2, T]))
                        nc.vector.tensor_tensor(out=sc[:, b, :, 0:NCB], in0=sc[:, b, :, 0:NCB], op=ALU.mult,
                                                in1=s3[:, :, 0:1].to_broadcast([P, 2, NCB])).then_inc(weights, 1)
                        dve.wait_ge(pT_ps, g * REP + r + 1)
                        nc.vector.tensor_copy(pt2[:, b], bank[5][:, 0:256])
                        nc.vector.tensor_copy(ptc[0:NCB, b], bank[5][0:NCB, 256:512]).then_inc(pT2, 1)
                        dve.wait_ge(oa_hi, g * REP + r + 1)
                        a = bass.ds(g * REP + r, 1)
                        nc.vector.tensor_tensor(out=xbl[:, a].rearrange("p a n -> p (a n)"), in0=bank[6 + b][:, 0:T],
                                                in1=xbh[:, a].bitcast(F32).rearrange("p a n -> p (a n)"),
                                                op=ALU.subtract).then_inc(oa_lo, 1)
                assert links[0] == AL, links[0]

            @block.tensor
            def _(pe):
                for n, part in enumerate(CP):
                    for j in range(2):
                        for k in range(2):
                            gg = 2 * j + k
                            for tt in range(TT):
                                last = nc.tensor.transpose(bank[2 * n + j][:, k * T + tt * P:k * T + (tt + 1) * P],
                                                           kvs[:, tt, part, gg * HD:(gg + 1) * HD], ident)
                        last.then_inc(kT_ps, 1)
                pe.wait_ge(c2_in, 48)
                pe.wait_ge(kT_act, 1)
                nc.tensor.transpose(bank[0][:, 0:66], pebr[:], ident[0:66, 0:66]).then_inc(peb_ps, 1)
                pe.wait_ge(tab_in, 16)
                pe.wait_ge(tab_one, 1)
                pe.wait_ge(kT_dve, 1)
                nc.tensor.matmul(bank[1][0:HB], tabx[:], dist_of, start=True, stop=True).then_inc(dist_ps, 1)
                pe.wait_ge(kT_act, 2)
                pe.wait_ge(kT_dve, 2)
                for tt in range(TT):
                    for c in range(NCB):
                        i0 = T + P * tt - (31 + 16 * c)
                        last = nc.tensor.matmul(bank[2 + tt][:, c * HB:(c + 1) * HB], dist_of[:, i0:i0 + P], tabx[:],
                                                start=True, stop=True)
                last.then_inc(bc_ps, 1)
                pe.wait_ge(cw_in, 48)
                pe.wait_ge(xc_ready, 1)
                pe.wait_ge(kT_act, 4)
                pe.wait_ge(kT_dve, 4)
                for a in range(2):
                    for l in range(32):
                        last = nc.tensor.matmul(bank[4 + a][0:GB * NCB, 0:P], xc[:, a, l], cw1[:, a, l],
                                                start=(l == 0), stop=(l == 31))
                last.then_inc(hid_ps, 1)
                pe.wait_ge(hid_ready, 1)
                for a in range(2):
                    last = nc.tensor.transpose(bank[6][:, a * 64:a * 64 + GB * NCB], hid[:, a],
                                               ident[0:GB * NCB, 0:GB * NCB])
                last.then_inc(hidT_ps, 1)
                pe.wait_ge(gel_ready, 1)
                nc.tensor.matmul(bank[7][:, 0:GB * NCB], cw2[:, 0], gel[:, 0], start=True, stop=True)
                for gg in range(GB):
                    last = nc.tensor.matmul(bank[0][0:NCB, gg * HD:(gg + 1) * HD],
                                            gel[:, 1, gg * NCB:(gg + 1) * NCB], cw2[:, 1], start=True, stop=True)
                last.then_inc(kc_ps, 1)
                pe.wait_ge(dist_ready, 1)
                pe.wait_ge(kc_ready, 1)
                with pe.Fori(0, GB) as g:
                    pe.wait_ge(grp_in, g + 1)
                    pe.wait_ge(oa_lo, g * REP + 1)
                    for r in range(REP):
                        for tt in range(TT):
                            last = nc.tensor.transpose(bank[6 + r // 2][:, (r % 2) * T + tt * P:(r % 2) * T + (tt + 1) * P],
                                                       qg[:, tt, r * HD:(r + 1) * HD], ident)
                    last.then_inc(qT_ps, 1)
                    pe.wait_ge(qT_ready, g + 1)

                    def scores(r):
                        b = r % 2
                        A, B = bank[b], bank[2 + b]
                        if r >= 2:
                            pe.wait_ge(biased, g * REP + r - 1)
                        nc.tensor.matmul(A[:, 0:256].rearrange("p (a n) -> p a n", a=2), qT4[:, r, 0:P],
                                         kT4[:, 2:4, bass.ds(g, 1), 0:P].rearrange("p a b n -> p (a b) n"),
                                         start=True, stop=True)
                        nc.tensor.matmul(B[:].rearrange("p (a n) -> p a n", a=2), qT4[:, r, P:T],
                                         kT4[:, 2:4, bass.ds(g, 1)].rearrange("p a b n -> p (a b) n"),
                                         start=True, stop=True)
                        for tt in range(TT):
                            last = nc.tensor.matmul(A[:, 256 + 16 * tt:256 + 16 * tt + NCB], qT4[:, r, tt * P:(tt + 1) * P],
                                                    kcT[:, bass.ds(g * NCB, NCB)], start=True, stop=True)
                        last.then_inc(sc_ps, 1)
                    scores(0)
                    for r in range(REP):
                        b = r % 2
                        if r < REP - 1:
                            scores(r + 1)
                        pe.wait_ge(weights, g * REP + r + 1)
                        if r:
                            pe.wait_ge(pT1, g * REP + r)
                            pe.wait_ge(pT2, g * REP + r)
                        for br in range(2):
                            nc.tensor.transpose(bank[4][:, br * 256:br * 256 + P], s0[:, b, br], ident)
                            nc.tensor.transpose(bank[4][:, br * 256 + P:br * 256 + 2 * P], s1[:, b, br, 0:P], ident)
                            nc.tensor.transpose(bank[5][:, br * P:(br + 1) * P], s1[:, b, br, P:T], ident)
                        for tt in range(TT):
                            last = nc.tensor.transpose(bank[5][0:NCB, 256 + tt * P:256 + (tt + 1) * P],
                                                       sc[:, b, tt, 0:NCB], ident)
                        last.then_inc(pT_ps, 1)
                        pe.wait_ge(pT1, g * REP + r + 1)
                        pe.wait_ge(pT2, g * REP + r + 1)
                        if r >= 2:
                            pe.wait_ge(oa_lo, g * REP + r)
                        O = bank[6 + b]
                        for br in range(2):
                            nc.tensor.matmul(O[:, 0:T], vg[:, 0, br], pt1[:, b, br * T:(br + 1) * T],
                                             start=(br == 0), stop=False)
                        for br in range(2):
                            nc.tensor.matmul(O[:, P:T], vg[:, 1, br], pt2[:, b, br * P:(br + 1) * P],
                                             start=False, stop=False)
                        nc.tensor.matmul(O[:, 0:T], vcg[:], ptc[:, b], start=False, stop=True).then_inc(o_ps, 1)

        u_wo2 = new_unit(NS)
        mlp1 = dict(stream)
        new_unit(HPG * NG)
        fg = at("fg", WORK + 32768, [P, D])
        fg_in, y_out, out_ready = sem("fg_in"), sem("y_out"), sem("out_ready")

        with nc.Block() as block:
            @block.sync
            def _(sp):
                sp_unit(sp, t['nsa_wo'][0], u_wo2)
                sp_mlp(sp, 1, mlp1['chunk'], mlp1['slab'])
                for tt in range(TT):
                    sp.wait_ge(out_ready, tt + 1)
                    sp.dma_start(t['y'][0].rearrange("(t p) d -> p t d", p=P)[:, tt], xs2[:, tt])\
                        .then_inc(y_out, 16)
                sp.wait_ge(y_out, 16 * (TT))

            @block.gpsimd
            def _(pool):
                pool.dma_start(fg[:], t['final_norm_g'].partition_broadcast(P)).then_inc(fg_in, 16)
                pool_mlp(pool, 1, mlp1['chunk'], mlp1['slab'])

            @block.scalar
            def _(act):
                act_unit(act, u_wo2, nothing)
                act_norm_sum(act, 3, lambda e: e.wait_ge(acc_free, mlp1['slab']), xs2)
                act_norm_sqrt(act, 3)
                act_split_norm(act, 3, 3 * KT, 'm1', xah)
                act_mlp(act, 1, mlp1['chunk'], mlp1['slab'])
                act_norm_sum(act, 4, lambda e: e.wait_ge(acc_free, stream['slab']), xs2)
                act_norm_sqrt(act, 4)

            @block.vector
            def _(dve):
                dve_unit(dve, u_wo2, lambda s: add_slab(dve, u_wo2['slab'] + s, s, s % 2))
                dve_norm(dve, 3, xs2)
                dve_split_norm(dve, 3 * KT, 'm1', xah, xal)
                dve_mlp(dve, 1, mlp1['chunk'], mlp1['slab'])
                dve.wait_ge(norm_ss, 10)
                nc.vector.tensor_scalar(rstd, ss, 1.0 / D, NORM_EPS, ALU.mult, ALU.add).then_inc(norm_var, 1)
                dve.wait_ge(norm_std, 5)
                nc.vector.reciprocal(rstd, rstd).then_inc(norm_r, 1)
                dve.wait_ge(norm_r, 5)
                dve.wait_ge(fg_in, 16)
                for tt in range(TT):
                    nc.vector.scalar_tensor_tensor(out=xs2[:, tt], in0=h[:, tt], scalar=rstd[:, tt:tt + 1], in1=fg[:],
                                                   op0=ALU.mult, op1=ALU.mult).then_inc(out_ready, 1)

            @block.tensor
            def _(pe):
                pe_unit(pe, u_wo2, xbh, xbl)
                pe_norm(pe, 3, xs2)
                pe_mlp(pe, 1, mlp1['chunk'], mlp1['slab'], 3 * KT)

INS = ['x', 'consts', 'consts2', 'par_rows', 'rw_w1', 'rw_a1', 'rw_g1', 'rw_wr', 'rw_wk', 'rw_wv', 'rw_w2', 'rw_a2',
       'rw_g2', 'rw_wo', 'mlp_up', 'mlp_down', 'w_kv', 'nsa_wq', 'nsa_wo', 'rel_bias', 'cmp_pe', 'cmp_w1', 'cmp_b1',
       'cmp_w2', 'final_norm_g']
OUTS = {'y': (1, T, D)}


def kernel(**inputs):
    import numpy as _np
    import concourse.bacc as _bacc
    from concourse import mybir as _mybir
    from concourse.bass_utils import run_bass_kernel_spmd as _run
    nc = _bacc.Bacc("TRN2", target_bir_lowering=False, num_devices=1)
    ins = {k: _np.asarray(v) for k, v in inputs.items()}
    rows = {n: ins[n] for n in PARAMS if n in ins}
    for j in range(6):
        rows[f'mu{j}'] = ins['rw_mu'][0, j]
    for j in range(2):
        rows[f'm{j}'] = ins['m_norm_g'][j]
    ins['par_rows'] = _np.concatenate([_np.reshape(rows[n], (KT, P)) for n in PARAMS]).reshape(3, PROW, P)
    ins['consts'], ins['consts2'] = constants(), constants2()
    arrays, args = {}, {}
    for name in INS:
        a = _np.ascontiguousarray(ins[name])
        arrays[f"in_{name}"] = a
        args[name] = nc.dram_tensor(f"in_{name}", a.shape, _mybir.dt.from_np(a.dtype), kind="ExternalInput").ap()
    for name, shape in OUTS.items():
        args[name] = nc.dram_tensor(f"out_{name}", shape, _mybir.dt.float32, kind="ExternalOutput").ap()
    build(nc, **args)
    r = _run(nc, [arrays], core_ids=[0])
    got = tuple(r.results[0][f"out_{n}"] for n in OUTS)
    return got[0]
```

```python
import math
from contextlib import ExitStack

import numpy as np
import concourse.bass as bass
from concourse import mybir

F32 = mybir.dt.float32
F32R = mybir.dt.float32r
ALU = mybir.AluOpType
ACT = mybir.ActivationFunctionType
AX = mybir.AxisListType

P = 128
D = 2048
T = 256
TT = T // P
KT = D // P
SLAB = 512
NS = D // SLAB
KC = 2
CPS = KT // KC
RING = 4
FF = 4 * D
NG = FF // D
LW, LA, LG = 96, 128, 256
NORM_EPS = 1e-6
GN_EPS = 64e-5
CH = 64
HEADS_A = 32
PAIRS = 4
NGRP = KT // PAIRS
HB, GB, HD = 16, 4, 128
REP = HB // GB
KVW = 6 * GB * HD
NCB = T // 16 - 1
BUCKETS, MAXDIST = 32, 128
NEG = -1e30
LEVELS = (2, 4, 8, 16, 32)

PARAMS = ['a_norm_g', 'mu0', 'mu1', 'mu2', 'mu3', 'mu4', 'mu5', 'rw_w0', 'rw_a0', 'rw_kk', 'rw_ka',
          'rw_rk', 'rw_lnx_w', 'rw_lnx_b', 'kv_norm_g', 'b_norm_g', 'm0', 'm1']
PROW = 6 * KT

C_ID, C_ONES, C_CAUSAL, C_LOW, C_T1, C_LV = 0, 128, 256, 512, 640, 768
C_W = C_LV + 128 * len(LEVELS)


def constants():
    c = np.zeros((P, C_W), np.float32)
    s, t = np.arange(P)[:, None], np.arange(P)[None, :]
    same = s // CH == t // CH
    c[:, C_ID:C_ID + P] = s == t
    c[:, C_ONES:C_ONES + P] = same
    c[:, C_CAUSAL:C_CAUSAL + P] = same & (s < t)
    c[:, C_CAUSAL + P:C_CAUSAL + 2 * P] = same & (s <= t)
    c[:, C_LOW:C_LOW + P] = same & (s > t)

    def level(m):
        return (s // (2 * m) == t // (2 * m)) & (s % (2 * m) < m) & (t % (2 * m) >= m)
    c[:, C_T1:C_T1 + P] = level(1)
    for n, m in enumerate(LEVELS):
        c[:, C_LV + P * n:C_LV + P * (n + 1)] = level(m)
    return c


def constants2():
    c = np.zeros((P, 512 + TT), np.float32)
    exact = BUCKETS // 2
    for dist in range(-T + 1, T):
        n = max(dist, 0)
        if n < exact:
            b = n
        else:
            b = min(BUCKETS - 1, exact + int(np.log(np.float32(n / exact)) / math.log(MAXDIST / exact) * (BUCKETS - exact)))
        c[b, T + dist] = dist >= 0
        c[BUCKETS, T + dist] = NEG if dist < 0 else 0.0
    for tt in range(TT):
        c[:, 512 + tt] = tt * P + np.arange(P) >= 31
    return c


def build(nc, **t):
    ctx = ExitStack()
    with ctx:
        def sem(name):
            return ctx.enter_context(nc.semaphore(name))

        def at(name, addr, shape, dt=F32):
            return nc.alloc_sbuf_tensor_at(name, shape, dt, offset=addr)

        A0 = 16640
        cst = at("cst", A0, [P, C_W])
        par = at("par", A0 + 6144, [P, len(PARAMS) * KT])
        small = at("small", A0 + 7424, [P, 64])
        H_AT = A0 + 8192
        XB_AT = H_AT + 16384
        XA_AT = XB_AT + 32768
        RAW_AT = XA_AT + 32768
        WHI_AT = RAW_AT + 16384
        WORK = WHI_AT + 32768
        TOP = 229344
        LH_AT = TOP - 4096
        h = at("h", H_AT, [P, TT, D])
        xbh = at("xbh", XB_AT, [P, KT, T], F32R)
        xbl = at("xbl", XB_AT + 16384, [P, KT, T], F32R)
        xah = at("xah", XA_AT, [P, KT, T], F32R)
        xal = at("xal", XA_AT + 16384, [P, KT, T], F32R)
        raw = at("raw", RAW_AT, [P, RING, KC, SLAB])
        whi = at("whi", WHI_AT, [P, RING, KC, SLAB], F32R)
        wlo = at("wlo", WHI_AT + 16384, [P, RING, KC, SLAB], F32R)
        lora_h = at("lora_h", LH_AT, [P, 4, T])
        bank = [nc.alloc_psum_tensor(f"bank{i}", [P, 512], F32) for i in range(8)]
        rkv = nc.dram_tensor("rkv_scratch", [3, T, D], F32, kind="Internal").ap()

        ident = cst[:, C_ID:C_ID + P]

        def col(name, k):
            n = PARAMS.index(name) * KT + k
            return par[:, n:n + 1]

        raw_in = [sem(f"raw_in{i}") for i in range(RING)]
        hi_ready = sem("hi_ready")
        lo_ready = sem("lo_ready")
        w_used = sem("w_used")
        acc_free = sem("acc_free")
        stream = {'chunk': 0, 'slab': 0}

        def later(n, first):
            return not isinstance(n, int) or n > first

        def load_chunk(eng, w, G, c, k0, n0):
            if later(G, RING - 1):
                eng.wait_ge(lo_ready, G - (RING - 1))
            src = w[bass.ds(k0, KC * P), bass.ds(n0, SLAB)].rearrange("(k p) n -> p k n", p=P)
            eng.dma_start(raw[:, c % RING], src).then_inc(raw_in[c % RING], 16)

        def split_hi(act, G, uses, c):
            act.wait_ge(raw_in[c % RING], 16 * (uses + 1))
            if later(G, RING - 1):
                act.wait_ge(w_used, G - (RING - 1))
            nc.scalar.activation(whi[:, c % RING], raw[:, c % RING], ACT.Copy).then_inc(hi_ready, 1)

        def split_lo(dve, G, c):
            dve.wait_ge(hi_ready, G + 1)
            nc.vector.tensor_tensor(out=wlo[:, c % RING], in0=raw[:, c % RING],
                                    in1=whi[:, c % RING].bitcast(F32), op=ALU.subtract).then_inc(lo_ready, 1)

        def slab_matmuls(pe, G0, S, half, xh, xl, before=None):
            if later(S, 1):
                pe.wait_ge(acc_free, S - 1)
            for c in range(CPS):
                if before:
                    before(c)
                pe.wait_ge(lo_ready, G0 + c + 1)
                for j in range(KC):
                    k = c * KC + j
                    for tt in range(TT):
                        acc, tok = bank[2 * half + tt], slice(tt * P, (tt + 1) * P)
                        nc.tensor.matmul(acc[:], xh[:, k, tok], whi[:, c % RING, j], start=(k == 0), stop=False)
                        nc.tensor.matmul(acc[:], xh[:, k, tok], wlo[:, c % RING, j], start=False, stop=False)
                        last = nc.tensor.matmul(acc[:], xl[:, k, tok], whi[:, c % RING, j],
                                                start=False, stop=(k == KT - 1))
                last.then_inc(w_used, 1)

        def pe_unit(pe, unit, xh, xl, before=None):
            def step(i):
                for half in range(2):
                    slab_matmuls(pe, unit['chunk'] + 2 * CPS * i + CPS * half, unit['slab'] + 2 * i + half,
                                 half, xh, xl, before)
            n = unit['slabs'] // 2
            first = 1 if unit['slab'] == 0 else 0
            if first:
                step(0)
            if n > first:
                with pe.Fori(first, n) as i:
                    step(i)

        def sp_unit(sp, w, unit):
            def step(s):
                for c in range(CPS):
                    load_chunk(sp, w, unit['chunk'] + CPS * s + c, c, c * KC * P, s * SLAB)
            first = 1 if unit['slab'] == 0 else 0
            if first:
                step(0)
            with sp.Fori(first, unit['slabs']) as s:
                step(s)

        def new_unit(slabs):
            u = dict(stream, slabs=slabs)
            stream['chunk'] += slabs * CPS
            stream['slab'] += slabs
            return u

        xnT = at("xnT", WORK, [P, KT, T + 1])
        xs = at("xs", WORK + 16512, [P, TT, D])
        xx = at("xx", WORK + 16512, [P, KT, T])
        stage = at("stage", WORK + 32896, [P, 2, TT, SLAB])
        w1s = at("w1s", WORK + 41088, [P, KT, LW])
        a1s = at("a1s", WORK + 47232, [P, KT, LA])
        g1s = at("g1s", H_AT, [P, KT, LG])
        NMIX = 6
        mix = at("mix", WORK + 55424, [P, 2, NMIX, T])
        assert WORK + 55424 + 2 * NMIX * T * 4 <= LH_AT
        prow = at("prow", XA_AT, [PROW, 3, P])
        ss, rstd = small[:, 0:2], small[:, 2:4]
        part_ss = small[:, 8:8 + TT * NS].rearrange("p (t s) -> p t s", s=NS)

        consts_in = sem("consts_in")
        rows_in = sem("rows_in")
        x_in = [sem(f"x_in{s}") for s in range(NS)]
        lora_in = sem("lora_in")
        par_T = sem("par_T")
        par_ready = sem("par_ready")

        norm_ss, norm_var, norm_std, norm_r = sem("norm_ss"), sem("norm_var"), sem("norm_std"), sem("norm_r")
        norm_sum, norm_xs, norm_T = sem("norm_sum"), sem("norm_xs"), sem("norm_T")

        def act_norm_sum(act, n, ready, xs):
            for s in range(NS):
                ready(s)
                cols = slice(s * SLAB, (s + 1) * SLAB)
                for tt in range(TT):
                    last = nc.scalar.activation(xs[:, tt, cols], h[:, tt, cols], ACT.Square,
                                                accum_out=part_ss[:, tt, s:s + 1])
                last.then_inc(norm_ss, 1)

        def act_norm_sqrt(act, n):
            act.wait_ge(norm_var, n + 1)
            nc.scalar.activation(rstd, rstd, ACT.Sqrt).then_inc(norm_std, 1)

        def dve_rstd(dve, n):
            dve.wait_ge(norm_ss, NS * (n + 1))
            nc.vector.reduce_sum(ss, part_ss, AX.X).then_inc(norm_sum, 1)
            dve.wait_ge(norm_sum, n + 1)
            nc.vector.tensor_scalar(rstd, ss, 1.0 / D, NORM_EPS, ALU.mult, ALU.add).then_inc(norm_var, 1)
            dve.wait_ge(norm_std, n + 1)
            nc.vector.reciprocal(rstd, rstd).then_inc(norm_r, 1)
            dve.wait_ge(norm_r, n + 1)

        def dve_norm(dve, n, xs):
            dve_rstd(dve, n)
            for s in range(NS):
                cols = slice(s * SLAB, (s + 1) * SLAB)
                for tt in range(TT):
                    last = nc.vector.tensor_scalar(xs[:, tt, cols], h[:, tt, cols], rstd[:, tt:tt + 1], None, ALU.mult)
                last.then_inc(norm_xs, 1)

        def pe_norm(pe, n, xs):
            for b in range(8):
                if b % 2 == 0:
                    pe.wait_ge(norm_xs, NS * n + b // 2 + 1)
                for j in range(2):
                    for tt in range(TT):
                        k = 2 * b + j
                        last = nc.tensor.transpose(bank[b][:, j * T + tt * P:j * T + (tt + 1) * P],
                                                   xs[:, tt, k * P:(k + 1) * P], ident)
                last.then_inc(norm_T, 1)

        xn_ready = sem("xn_ready")
        pad_set = sem("pad_set")
        xx_ready = sem("xx_ready")
        mixed = sem("mixed")
        mix_hi = sem("mix_hi")
        mix_lo = sem("mix_lo")
        mix_used = sem("mix_used")
        lora_ready = sem("lora_ready")
        rkv_out = [sem(f"rkv_out{i}") for i in range(2)]
        units = [new_unit(NS) for _ in range(3)]
        order = ['rw_wr', 'rw_wk', 'rw_wv']
        MU = {'r': 'mu0', 'w': 'mu1', 'k': 'mu2', 'v': 'mu3', 'a': 'mu4', 'g': 'mu5'}

        cursor = [XA_AT]

        def place(name, shape, dt=F32):
            n = 4 * math.prod(shape[1:])
            cursor[0] += n
            assert cursor[0] <= LH_AT
            return at(name, cursor[0] - n, shape, dt)

        UN = 2 * PAIRS * TT
        NCH = T // CH
        rkvg = at("rkvg", H_AT, [P, 3, TT, SLAB])
        vtok = at("vtok", H_AT + 12288, [P, TT, SLAB])
        rT, kT, vT, gT = (place(n, [P, PAIRS, T]) for n in ("rT", "kT", "vT", "gT"))
        bt, kt_ = place("bt", [P, PAIRS, T]), place("kt_", [P, PAIRS, T])
        bh, kh = place("bh", [P, TT, SLAB]), place("kh", [P, TT, SLAB])
        assert cursor[0] == RAW_AT
        dec, aT, nkk, tmp = (place(n, [P, PAIRS, T]) for n in ("dec", "aT", "nkk", "tmp"))
        assert cursor[0] == WHI_AT
        gp = place("gp", [P, 8, PAIRS])
        gpe = small[:, 16:16 + PAIRS]
        pcb = place("pcb", [P, PAIRS * T // CH])
        zeros = place("zeros", [P, CH])
        gn_eps = small[:, 24:25]
        prod = place("prod", [P, PAIRS * NCH, CH + 1])
        ipr = place("ipr", [P, PAIRS, T])
        ar = place("ar", [P, PAIRS, TT, 2, P])
        Lm = place("Lm", [P, UN, P])
        X_AT = cursor[0]
        X, XT = place("X", [P, UN, P]), place("XT", [P, UN, P])
        mk = place("mk", [P, UN, 2, P])
        rbt = place("rbt", [P, UN, P])
        sd = place("sd", [P, PAIRS, 2, CH])
        sp_ = place("sp_", [P, PAIRS, CH])
        w1b, sab = place("w1b", [P, SLAB]), place("sab", [P, SLAB])
        gE = place("gE", [P, PAIRS, T])
        w2g, a2g, g2g = place("w2g", [LW, SLAB]), place("a2g", [P, SLAB]), place("g2g", [P, 2, SLAB])
        Z_AT = cursor[0]
        assert cursor[0] - 8192 >= WORK + 41088 and cursor[0] <= WORK + 55424
        Z = place("Z", [P, UN, P])
        yT, bvE = (place(n, [P, PAIRS, T]) for n in ("yT", "bvE"))
        dT = at("dT", Z_AT, [P, PAIRS, T])
        etmp = at("etmp", Z_AT + 4096, [P, PAIRS, T])
        idec = at("idec", X_AT, [P, PAIRS, T])
        NPC = PAIRS * NCH
        NPRO, NACT, NDVE = 16, 12, 4

        def unit(h, pair, tt):
            return h * 8 + pair * 2 + tt

        rkvg_in = sem("rkvg_in")
        l2_in = sem("l2_in")
        vtok_ready = sem("vtok_ready")
        zero_set = sem("zero_set")
        pro_ps, pro_act, pro_dve = sem("pro_ps"), sem("pro_act"), sem("pro_dve")
        gp_copied, gp_ready, gpe_ready = sem("gp_copied"), sem("gp_ready"), sem("gpe_ready")
        kk_raw, kk_std, kk_rec, kkn_ready = sem("kk_raw"), sem("kk_std"), sem("kk_rec"), sem("kkn_ready")
        kfac, kmod_ready = sem("kfac"), sem("kmod_ready")
        idec_ready, dec_ready = sem("idec_ready"), sem("dec_ready")
        prod_ready, ipr_part = sem("prod_ready"), sem("ipr_part")
        bon_ready = sem("bon_ready")
        bt_raw, bk_ready = sem("bt_raw"), sem("bk_ready")
        factors_ready = sem("factors_ready")
        pcb_ready, sd_zero = sem("pcb_ready"), sem("sd_zero")
        s3_ps = sem("s3_ps")
        s3_read = sem("s3_read")
        l_ps, l_ready = sem("l_ps"), sem("l_ready")
        x0_ready = sem("x0_ready")
        xt_ps, xt_read = sem("xt_ps"), sem("xt_read")
        z_ps, z_ready, x_ps, x_ready = sem("z_ps"), sem("z_ready"), sem("x_ps"), sem("x_ready")
        hat_ready, hat_ps, hat_read = sem("hat_ready"), sem("hat_ps"), sem("hat_read")
        kept = sem("kept")
        w1_ps, w1_ready, sa_ps, sa_ready = sem("w1_ps"), sem("w1_ready"), sem("sa_ps"), sem("sa_ready")
        sp_ready, s_ps, s_ready, y_ps, y_ready = (sem(n) for n in ("sp_ready", "s_ps", "s_ready", "y_ps", "y_ready"))
        mean_ps, d_ready, d_sq, var_ps, std_ready, e_rec = (sem(n) for n in (
            "mean_ps", "d_ready", "d_sq", "var_ps", "std_ready", "e_rec"))
        gn_ready, bonused, o_ready, o_hi = (sem(n) for n in (
            "gn_ready", "bonused", "o_ready", "o_hi"))
        grp_done = sem("grp_done")
        NLV = len(LEVELS)

        def bc(ap, n):
            return ap.unsqueeze(1).to_broadcast([ap.shape[0], n, ap.shape[-1]])

        def load_group(sp, n):
            cols = bass.ds(n * SLAB, SLAB)
            for u in (1, 0, 2):
                sp.dma_start(rkvg[:, u], rkv[u].rearrange("(t p) d -> p t d", p=P)[:, :, cols]).then_inc(rkvg_in, 16)
            sp.dma_start(w2g[:], t['rw_w2'][0][:, cols]).then_inc(l2_in, 16)
            sp.dma_start(a2g[:], t['rw_a2'][0][:, cols]).then_inc(l2_in, 16)
            sp.dma_start(g2g[:], t['rw_g2'][0].rearrange("(k p) n -> p k n", p=P)[:, :, cols]).then_inc(l2_in, 16)

        u_wo = new_unit(NS)

        with nc.Block() as block:
            @block.sync
            def _(sp):
                for s in range(NS):
                    cols = slice(s * SLAB, (s + 1) * SLAB)
                    sp.dma_start(h[:, :, cols], t['x'].rearrange("b (t p) d -> p (b t) d", p=P)[:, :, cols])\
                        .then_inc(x_in[s], 16)
                sp.dma_start(cst[:], t['consts']).then_inc(consts_in, 16)
                for u, name in zip(units, order):
                    sp_unit(sp, t[name][0], u)
                sp.wait_ge(mix_used, KT)
                sp.wait_ge(rkv_out[0], 16 * (NS + 1))
                load_group(sp, 0)

            @block.gpsimd
            def _(pool):
                nc.gpsimd.memset(xnT[:, :, 0:1], 0.0).then_inc(pad_set, 1)
                pool.dma_start(prow[:, 0], t['par_rows'][0]).then_inc(rows_in, 16)
                pool.dma_start(prow[:, 1], t['par_rows'][1]).then_inc(rows_in, 16)
                pool.dma_start(prow[:, 2], t['par_rows'][2]).then_inc(rows_in, 16)
                pool.dma_start(w1s[:], t['rw_w1'][0].rearrange("(k p) n -> p k n", p=P)).then_inc(lora_in, 16)
                pool.dma_start(a1s[:], t['rw_a1'][0].rearrange("(k p) n -> p k n", p=P)).then_inc(lora_in, 16)
                pool.wait_ge(norm_xs, NS)
                pool.dma_start(g1s[:], t['rw_g1'][0].rearrange("(k p) n -> p k n", p=P)).then_inc(lora_in, 16)
                for n in range(3 * NS):
                    u, s = divmod(n, NS)
                    pool.wait_ge(acc_free, n + 1)
                    pool.dma_start(rkv[u].rearrange("(t p) d -> p t d", p=P)[:, :, s * SLAB:(s + 1) * SLAB],
                                   stage[:, n % 2]).then_inc(rkv_out[n % 2], 16)
                for i in range(2):
                    pool.wait_ge(rkv_out[i], 16 * (3 * NS // 2))

            def rkv_evac(act, n):
                act.wait_ge(w_used, CPS * (n + 1))
                if n >= 2:
                    act.wait_ge(rkv_out[n % 2], 16 * (n // 2))
                nc.scalar.activation(stage[:, n % 2, 0], bank[2 * (n % 2)][:], ACT.Copy)
                nc.scalar.activation(stage[:, n % 2, 1], bank[2 * (n % 2) + 1][:], ACT.Copy)\
                    .then_inc(acc_free, 1)

            @block.scalar
            def _(act):
                act_norm_sum(act, 0, lambda s: act.wait_ge(x_in[s], 16), xs)
                act_norm_sqrt(act, 0)
                act.wait_ge(par_ready, 1)
                for k in range(KT):
                    if k % 2 == 0:
                        act.wait_ge(norm_T, k // 2 + 1)
                    if k == 0:
                        act.wait_ge(pad_set, 1)
                    nc.scalar.activation(xnT[:, k, 1:T + 1], bank[k // 2][:, (k % 2) * T:(k % 2 + 1) * T], ACT.Copy,
                                         scale=col('a_norm_g', k)).then_inc(xn_ready, 1)
                split_hi(act, 0, 0, 0)
                for k in range(KT):
                    act.wait_ge(mixed, k + 1)
                    nc.scalar.activation(xah[:, k], mix[:, k % 2, 0], ACT.Copy).then_inc(mix_hi, 1)
                act.wait_ge(mix_used, KT)
                nc.scalar.activation(lora_h[0:LW, 0], bank[4][0:LW, 0:T], ACT.Tanh)
                nc.scalar.activation(lora_h[:, 1], bank[5][:, 0:T], ACT.Copy)
                for j in range(2):
                    last = nc.scalar.activation(lora_h[:, 2 + j], bank[6 + j][:, 0:T], ACT.Sigmoid)
                last.then_inc(lora_ready, 1)
                for G in range(1, 3 * NS * CPS):
                    c = G % CPS
                    split_hi(act, G, G // RING, c)
                    if c == 2 and G >= CPS:
                        rkv_evac(act, G // CPS - 1)
                    if G % 2 == 1 and 1 <= G // 32 + 1 <= 2:
                        n = KT * (G // 32 + 1) + (G % 32) // 2
                        act.wait_ge(mixed, n + 1)
                        xh = (xbh, xah)[G // 32]
                        nc.scalar.activation(xh[:, n % KT], mix[:, n % 2, 0], ACT.Copy).then_inc(mix_hi, 1)
                rkv_evac(act, 3 * NS - 1)

            @block.vector
            def _(dve):
                dve.wait_ge(par_T, 1)
                nc.vector.tensor_copy(par[:].rearrange("p (a n) -> p a n", a=3),
                                      bank[7][:, 0:3 * PROW].rearrange("p (a n) -> p a n", a=3)).then_inc(par_ready, 1)
                dve_norm(dve, 0, xs)
                dve.wait_ge(par_ready, 1)
                dve.wait_ge(norm_T, 8)
                for k in range(KT):
                    dve.wait_ge(xn_ready, k + 1)
                    nc.vector.tensor_tensor(out=xx[:, k], in0=xnT[:, k, 0:T], in1=xnT[:, k, 1:T + 1],
                                            op=ALU.subtract).then_inc(xx_ready, 1)

                def lo(k, n, xh, xl):
                    dve.wait_ge(mix_hi, n + 1)
                    nc.vector.tensor_tensor(out=xl[:, k], in0=mix[:, n % 2, 0], in1=xh[:, k].bitcast(F32),
                                            op=ALU.subtract).then_inc(mix_lo, 1)

                def blend(dst, k, name):
                    return nc.vector.scalar_tensor_tensor(out=dst, in0=xx[:, k], scalar=col(MU[name], k),
                                                          in1=xnT[:, k, 1:T + 1], op0=ALU.mult, op1=ALU.add)
                for k in range(KT):
                    dve.wait_ge(xx_ready, k + 1)
                    if k >= 2:
                        dve.wait_ge(mix_used, k - 1)
                    if k >= 2:
                        dve.wait_ge(mix_lo, k - 1)
                    for j, name in enumerate('rwag'):
                        last = blend(mix[:, k % 2, j], k, name)
                    last.then_inc(mixed, 1)
                    if k:
                        lo(k - 1, k - 1, xah, xal)
                lo(KT - 1, KT - 1, xah, xal)
                for G in range(3 * NS * CPS):
                    c = G % CPS
                    split_lo(dve, G, c)
                    if G % 2 == 0 and G // 32 < 2:
                        k = (G % 32) // 2
                        n = KT * (G // 32 + 1) + k
                        if n == KT:
                            dve.wait_ge(mix_used, KT)
                        dve.wait_ge(mix_lo, n - 1)
                        blend(mix[:, n % 2, 0], k, 'kv'[G // 32]).then_inc(mixed, 1)
                        if G // 32 == 1 and k == 0:
                            dve.wait_ge(w_used, NS * CPS)
                    if G % 2 == 1 and G // 32 < 2:
                        k = (G % 32) // 2
                        xh, xl = ((xbh, xbl), (xah, xal))[G // 32]
                        lo(k, KT * (G // 32 + 1) + k, xh, xl)

            @block.tensor
            def _(pe):
                pe.wait_ge(consts_in, 16)
                pe.wait_ge(rows_in, 48)
                for a in range(3):
                    last = nc.tensor.transpose(bank[7][:, a * PROW:(a + 1) * PROW], prow[:, a], ident[0:PROW, 0:PROW])
                last.then_inc(par_T, 1)
                pe.wait_ge(par_ready, 1)
                pe_norm(pe, 0, xs)
                pe.wait_ge(lora_in, 48)
                pe.wait_ge(xn_ready, KT)
                for k in range(KT):
                    pe.wait_ge(mixed, k + 1)
                    first, end = k == 0, k == KT - 1
                    nc.tensor.matmul(bank[4][0:LW, 0:T], w1s[:, k], mix[:, k % 2, 1], start=first, stop=end)
                    nc.tensor.matmul(bank[5][:, 0:T], a1s[:, k], mix[:, k % 2, 2], start=first, stop=end)
                    for j in range(2):
                        last = nc.tensor.matmul(bank[6 + j][:, 0:T], g1s[:, k, j * P:(j + 1) * P], mix[:, k % 2, 3],
                                                start=first, stop=end)
                    last.then_inc(mix_used, 1)
                for u, (xh, xl), n in zip(units, ((xah, xal), (xbh, xbl), (xah, xal)), (1, 2, 3)):
                    pe.wait_ge(mix_lo, KT * n)
                    pe_unit(pe, u, xh, xl)


        def halfof(b, j):
            return b[:, 2 * j:2 * j + 2].rearrange("p a n -> p (a n)")

        parv = par[:].rearrange("p (a k) -> p a k", k=KT)
        first_p = PARAMS.index('rw_w0')

        def pe_mean(pe, e):
            pe.wait_ge(y_ready, (e + 1) * NCH)
            for j in range(2):
                last = nc.tensor.matmul(bank[6 + j][:], cst[:, C_ONES:C_ONES + P], halfof(yT, j), start=True, stop=True)
            last.then_inc(mean_ps, 1)

        def pe_var(pe, e):
            pe.wait_ge(d_sq, e + 1)
            for j in range(2):
                last = nc.tensor.matmul(bank[6 + j][:], cst[:, C_ONES:C_ONES + P], halfof(etmp, j), start=True, stop=True)
            last.then_inc(var_ps, 1)

        def act_square(act, e):
            act.wait_ge(d_ready, e + 1)
            nc.scalar.activation(etmp[:], dT[:], ACT.Square).then_inc(d_sq, 1)

        def act_std(act, e):
            act.wait_ge(var_ps, e + 1)
            for j in range(2):
                last = nc.scalar.activation(etmp[:, 2 * j:2 * j + 2].rearrange("p a n -> p (a n)"),
                                            bank[6 + j][:], ACT.Sqrt, scale=1.0 / CH, bias=gn_eps)
            last.then_inc(std_ready, 1)

        def act_upper(act, e):
            act.wait_ge(o_ready, e + 1)
            nc.scalar.activation(xbh[:, bass.ds(e * PAIRS, PAIRS)], dT[:], ACT.Copy).then_inc(o_hi, 1)

        def dve_epi_d(dve, e):
            dve.wait_ge(y_ready, (e + 1) * NCH)
            dve.wait_ge(mean_ps, e + 1)
            nc.vector.tensor_copy(gpe, parv[:, first_p + 5, bass.ds(e * PAIRS, PAIRS)])\
                .then_inc(gpe_ready, 1)
            for j in range(2):
                last = nc.vector.scalar_tensor_tensor(out=halfof(dT, j), in0=bank[6 + j][:],
                                                      scalar=-1.0 / CH, in1=halfof(yT, j),
                                                      op0=ALU.mult, op1=ALU.add)
            last.then_inc(d_ready, 1)

        def dve_recip(dve, e, j):
            dve.wait_ge(std_ready, e + 1)
            nc.vector.reciprocal(halfof(etmp, j), halfof(etmp, j)).then_inc(e_rec, 1)

        def dve_epi_norm(dve, e):
            dve.wait_ge(e_rec, e * 2 + 2)
            dve.wait_ge(gpe_ready, e + 1)
            for p in range(PAIRS):
                last = nc.vector.scalar_tensor_tensor(out=dT[:, p], in0=dT[:, p], scalar=gpe[:, p:p + 1],
                                                      in1=etmp[:, p], op0=ALU.mult, op1=ALU.mult)
            last.then_inc(gn_ready, 1)

        def dve_lower(dve, e):
            dve.wait_ge(o_hi, e + 1)
            nc.vector.tensor_tensor(out=xbl[:, bass.ds(e * PAIRS, PAIRS)], in0=dT[:],
                                    in1=xbh[:, bass.ds(e * PAIRS, PAIRS)].bitcast(F32),
                                    op=ALU.subtract).then_inc(grp_done, 1)

        def pool_epilogue(pool, e):
            pool.wait_ge(gn_ready, e + 1)
            pool.wait_ge(kept, e + 1)
            nc.gpsimd.tensor_tensor(out=dT[:], in0=dT[:], in1=bvE[:], op=ALU.add).then_inc(bonused, 1)
            pool.wait_ge(bonused, e + 1)
            nc.gpsimd.tensor_tensor(out=dT[:], in0=dT[:], in1=gE[:], op=ALU.mult).then_inc(o_ready, 1)

        with nc.Block() as block:
            @block.sync
            def _(sp):
                with sp.Fori(1, NGRP) as n:
                    sp.wait_ge(pro_ps, n * NPRO)
                    sp.wait_ge(vtok_ready, n)
                    load_group(sp, n)
                sp.wait_ge(hat_ready, NGRP)
                for c in range(RING):
                    load_chunk(sp, t['rw_wo'][0], u_wo['chunk'] + c, c, c * KC * P, 0)

            @block.gpsimd
            def _(pool):
                nc.gpsimd.memset(prod[:, :, 0:1], 1.0)
                nc.gpsimd.memset(sab[:], 0.0)
                nc.gpsimd.memset(w1b[:], 0.0)
                nc.gpsimd.memset(gn_eps, GN_EPS)
                nc.gpsimd.memset(zeros[:], 0.0).then_inc(zero_set, 1)

                def factors(n):
                    pool.wait_ge(ipr_part, (n + 1) * NPC)
                    pool.wait_ge(kmod_ready, n + 1)
                    nc.gpsimd.tensor_tensor(out=kt_[:], in0=kT[:], in1=ipr[:], op=ALU.mult)
                    pool.wait_ge(kkn_ready, n + 1)
                    nc.gpsimd.tensor_tensor(out=bt[:], in0=aT[:], in1=nkk[:], op=ALU.mult).then_inc(bt_raw, 1)
                    pool.wait_ge(bt_raw, n + 1)
                    nc.gpsimd.tensor_tensor(out=bt[:], in0=bt[:], in1=ipr[:], op=ALU.mult).then_inc(bk_ready, 1)

                def group(g, first, last):
                    if not first:
                        pool_epilogue(pool, g - 1)
                        pool.wait_ge(o_ready, g)
                    for q in range(4):
                        us = slice(4 * q, 4 * q + 4)
                        pool.wait_ge(l_ready, g * 4 + q + 1)
                        nc.gpsimd.tensor_tensor(out=XT[:, us], in0=XT[:, us], in1=bc(ident, 4),
                                                op=ALU.add).then_inc(x0_ready, 1)
                    if not last:
                        pool.wait_ge(hat_ps, g * 2 + 2)
                        factors(g + 1)

                factors(0)
                group(0, True, False)
                with pool.Fori(1, NGRP - 1) as g:
                    group(g, False, False)
                group(NGRP - 1, False, True)

            @block.scalar
            def _(act):
                def pro_bank(i):
                    return bank[1 + i % 3]

                def half(b, j):
                    return b[:, 2 * j:2 * j + 2].rearrange("p a n -> p (a n)")

                def pro_k(n):
                    act.wait_ge(gp_ready, n + 1)
                    for j in range(2):
                        act.wait_ge(pro_ps, n * NPRO + j + 1)
                        for p in range(2):
                            nc.scalar.activation(tmp[:, 2 * j + p], pro_bank(j)[:, p * T:(p + 1) * T], ACT.Square,
                                                 scale=gp[:, 2, 2 * j + p:2 * j + p + 1])
                        nc.scalar.activation(half(kT, j), pro_bank(j)[:], ACT.Copy).then_inc(pro_act, 1)

                def pro_sigmoid(n, i, dst, row, j):
                    act.wait_ge(pro_ps, n * NPRO + i + 1)
                    for p in range(2):
                        q = 2 * j + p
                        last = nc.scalar.activation(dst[:, q], pro_bank(i)[:, p * T:(p + 1) * T], ACT.Sigmoid,
                                                    bias=gp[:, row, q:q + 1])
                    last.then_inc(pro_act, 1)

                def pro_decay(n):
                    act.wait_ge(pro_act, n * NACT + 5)
                    nc.scalar.activation(idec[:], dec[:], ACT.Exp, scale=math.exp(-0.5)).then_inc(idec_ready, 1)
                    act.wait_ge(idec_ready, n + 1)
                    nc.scalar.activation(dec[:], dec[:], ACT.Exp, scale=-math.exp(-0.5)).then_inc(dec_ready, 1)

                def pro_copy(n, i, dst, j):
                    act.wait_ge(pro_ps, n * NPRO + i + 1)
                    nc.scalar.activation(half(dst, j), pro_bank(i)[:], ACT.Copy).then_inc(pro_act, 1)

                def pro_std(n):
                    act.wait_ge(pro_dve, n * NDVE + 2)
                    nc.scalar.activation(tmp[:], tmp[:], ACT.Sqrt).then_inc(kk_std, 1)

                def prologue(n, c):
                    if c == 0:
                        pro_k(n)
                        pro_sigmoid(n, 2, dec, 0, 0)
                    if c == 1:
                        pro_sigmoid(n, 5, dec, 0, 1)
                        pro_sigmoid(n, 6, aT, 1, 0)
                        pro_decay(n)
                        pro_std(n)
                    if c == 2:
                        pro_sigmoid(n, 7, aT, 1, 1)
                        pro_copy(n, 8, rT, 0)
                        pro_copy(n, 9, rT, 1)
                        pro_copy(n, 10, vT, 0)
                    if c == 3:
                        pro_copy(n, 11, vT, 1)
                        pro_copy(n, 12, gT, 0)
                        pro_copy(n, 13, gT, 1)

                def group(g, first, last):
                    if not first:
                        act.wait_ge(y_ps, g * NCH)
                    act.wait_ge(rkvg_in, 16 * (g * 3 + 3))
                    nc.scalar.activation(vtok[:], rkvg[:, 2], ACT.Copy).then_inc(vtok_ready, 1)
                    if not first:
                        act_square(act, g - 1)
                        act_std(act, g - 1)
                        act_upper(act, g - 1)
                    act.wait_ge(pro_dve, (g + 1) * NDVE)
                    for p in range(PAIRS):
                        nc.scalar.activation(bvE[:, p], vT[:, p], ACT.Identity, bias=gp[:, 6, p:p + 1])
                    act.wait_ge(pro_act, (g + 1) * NACT)
                    nc.scalar.activation(gE[:], gT[:], ACT.Copy).then_inc(kept, 1)
                    for i in range(4 * NLV):
                        act.wait_ge(xt_ps, g * 4 * NLV + i + 1)
                        nc.scalar.activation(X[:, 4 * (i % 4):4 * (i % 4) + 4].rearrange("p a n -> p (a n)"),
                                             bank[6 + i % 2][:], ACT.Copy).then_inc(xt_read, 1)
                    for tt in range(TT):
                        act.wait_ge(hat_ps, g * 2 + tt + 1)
                        nc.scalar.activation(bh[:, tt], bank[tt][:], ACT.Copy)
                        nc.scalar.activation(kh[:, tt], bank[2 + tt][:], ACT.Copy).then_inc(hat_read, 1)
                    for c in range(NCH):
                        rows = slice(CH * (c % 2), CH * (c % 2) + CH)
                        act.wait_ge(w1_ps, g * NCH + c + 1)
                        nc.scalar.activation(w1b[rows], bank[4][rows], ACT.Copy).then_inc(w1_ready, 1)
                        if not last:
                            if c == 2:
                                act.wait_ge(kept, g + 1)
                            prologue(g + 1, c)
                        act.wait_ge(y_ps, g * NCH + c + 1)
                        nc.scalar.activation(yT[:, :, c * CH:(c + 1) * CH],
                                             bank[6 + c % 2][:, 0:PAIRS * CH].rearrange("p (a n) -> p a n", n=CH),
                                             ACT.Copy).then_inc(y_ready, 1)

                for c in range(NCH):
                    prologue(0, c)
                group(0, True, False)
                with act.Fori(1, NGRP - 1) as g:
                    group(g, False, False)
                group(NGRP - 1, False, True)

            @block.vector
            def _(dve):
                pro_bank = lambda i: bank[1 + i % 3]
                chunked = lambda b: b[:].rearrange("p a (c n) -> p (a c) n", n=CH)
                tiled = lambda x: ar[:, :, :, x].rearrange("p a t (c n) -> p (a t) c n", n=CH)
                tile3 = lambda b: b[:].rearrange("p a (t c n) -> p (a t) c n", t=TT, n=CH)
                pr3 = prod[:].rearrange("p (a c) n -> p a c n", c=2)

                def pro_params(n):
                    nc.vector.tensor_copy(gp[:, 0:7], parv[:, first_p:first_p + 7, bass.ds(n * PAIRS, PAIRS)])\
                        .then_inc(gp_copied, 1)
                    dve.wait_ge(gp_copied, n + 1)
                    nc.vector.tensor_scalar(gp[:, 7], gp[:, 3], -1.0, 1.0, ALU.mult, ALU.add).then_inc(gp_ready, 1)

                def pro_kk(n):
                    dve.wait_ge(pro_act, n * NACT + 2)
                    for p in range(PAIRS):
                        last = nc.vector.tensor_scalar(nkk[:, p], kT[:, p], gp[:, 2, p:p + 1], None, ALU.mult)
                    last.then_inc(kk_raw, 1)

                def pro_kmod(n):
                    dve.wait_ge(pro_act, n * NACT + 6)
                    dve.wait_ge(kkn_ready, n + 1)
                    for p in range(PAIRS):
                        last = nc.vector.tensor_scalar(tmp[:, p], aT[:, p], gp[:, 3, p:p + 1], gp[:, 7, p:p + 1],
                                                       ALU.mult, ALU.add)
                    last.then_inc(kfac, 1)
                    dve.wait_ge(kfac, n + 1)
                    dve.wait_ge(kk_raw, n + 1)
                    nc.vector.tensor_tensor(out=kT[:], in0=kT[:], in1=tmp[:], op=ALU.mult).then_inc(kmod_ready, 1)
                    dve.wait_ge(kmod_ready, n + 1)

                def pro_scan(n, lo, hi):
                    dve.wait_ge(dec_ready, n + 1)
                    for m in range(lo, hi):
                        nc.vector.tensor_tensor_scan(prod[:, m, 1:CH + 1], chunked(dec)[:, m], zeros[:], 1.0,
                                                     ALU.mult, ALU.add).then_inc(prod_ready, 1)
                        nc.vector.tensor_tensor_scan(chunked(ipr)[:, m], chunked(idec)[:, m], zeros[:], 1.0,
                                                     ALU.mult, ALU.add).then_inc(ipr_part, 1)

                def pro_max(n, j):
                    dve.wait_ge(pro_ps, n * NPRO + 4 + j)
                    nc.vector.tensor_scalar(halfof(tmp, j), pro_bank(3 + j)[:], 1e-24, None, ALU.max)\
                        .then_inc(pro_dve, 1)

                def pro_recip(n, j):
                    dve.wait_ge(kk_std, n + 1)
                    nc.vector.reciprocal(halfof(tmp, j), halfof(tmp, j)).then_inc(kk_rec, 1)

                def pro_kkn(n):
                    dve.wait_ge(kk_rec, n * 2 + 2)
                    nc.vector.tensor_tensor(out=nkk[:], in0=nkk[:], in1=tmp[:], op=ALU.mult).then_inc(kkn_ready, 1)

                def pro_bonus(n):
                    dve.wait_ge(pro_act, n * NACT + 8)
                    dve.wait_ge(prod_ready, (n + 1) * NPC)
                    for p in range(PAIRS):
                        last = nc.vector.scalar_tensor_tensor(out=dec[:, p], in0=rT[:, p], scalar=gp[:, 4, p:p + 1],
                                                              in1=kT[:, p], op0=ALU.mult, op1=ALU.mult)
                    last.then_inc(bon_ready, 1)

                def pro_bv(n):
                    dve.wait_ge(pro_act, n * NACT + 10)
                    for j in range(2):
                        dve.wait_ge(pro_ps, n * NPRO + 15 + j)
                        last = nc.vector.tensor_tensor(out=halfof(vT, j), in0=halfof(vT, j), in1=pro_bank(14 + j)[:],
                                                       op=ALU.mult).then_inc(pro_dve, 1)
                    dve.wait_ge(pro_dve, (n + 1) * NDVE)

                def group(g, first, last):
                    dve.wait_ge(prod_ready, (g + 1) * NPC)
                    dve.wait_ge(pro_act, (g + 1) * NACT)
                    dve.wait_ge(kkn_ready, g + 1)
                    if not first:
                        dve.wait_ge(y_ps, g * NCH)
                    nc.vector.tensor_tensor(out=tiled(1), in0=tile3(rT), in1=pr3[:, :, :, 1:CH + 1], op=ALU.mult)
                    nc.vector.scalar_tensor_tensor(out=tiled(0), in0=tile3(nkk), scalar=-1.0, in1=pr3[:, :, :, 0:CH],
                                                   op0=ALU.mult, op1=ALU.mult).then_inc(factors_ready, 1)
                    nc.vector.tensor_copy(pcb[:].unsqueeze(2), prod[:, :, CH:CH + 1]).then_inc(pcb_ready, 1)
                    nc.vector.memset(sd[:], 0.0).then_inc(sd_zero, 1)
                    if not first:
                        dve_epi_d(dve, g - 1)
                    for h_ in range(2):
                        for p in range(PAIRS):
                            j = h_ * PAIRS + p
                            dve.wait_ge(s3_ps, g * 8 + j + 1)
                            u = unit(h_, p, 0)
                            ps = bank[j % 2][:].rearrange("p (t n) -> p t n", t=2)
                            nc.vector.tensor_tensor(out=XT[:, u:u + 2], in0=ps[:, :, 0:P],
                                                    in1=bc(cst[:, C_T1:C_T1 + P], 2), op=ALU.mult)
                            nc.vector.tensor_tensor(out=rbt[:, u:u + 2], in0=ps[:, :, P:2 * P],
                                                    in1=bc(cst[:, C_CAUSAL + P:C_CAUSAL + 2 * P], 2), op=ALU.mult)
                            nc.vector.tensor_tensor(
                                out=mk[:, u:u + 2].rearrange("p t x n -> p t (x n)"),
                                in0=bank[2 + j % 2][:].rearrange("p (t n) -> p t n", t=2),
                                in1=bc(cst[:, C_CAUSAL:C_CAUSAL + 2 * P], 2), op=ALU.mult).then_inc(s3_read, 1)
                            if p % 2:
                                q = j // 2
                                dve.wait_ge(l_ps, g * 4 + q + 1)
                                nc.vector.tensor_tensor(out=Lm[:, 4 * q:4 * q + 4],
                                                        in0=bank[4 + q % 2][:].rearrange("p (t n) -> p t n", t=4),
                                                        in1=bc(cst[:, C_LOW:C_LOW + P], 4),
                                                        op=ALU.mult).then_inc(l_ready, 1)
                            if not first:
                                if j in (3, 4):
                                    dve_recip(dve, g - 1, j - 3)
                                if j == 5:
                                    dve_epi_norm(dve, g - 1)
                    dve.wait_ge(s3_ps, g * 8 + 8)
                    dve.wait_ge(pcb_ready, g + 1)
                    pc = pcb[:].unsqueeze(2).to_broadcast([P, NPC, CH])
                    nc.vector.tensor_tensor(out=chunked(kt_), in0=chunked(kt_), in1=pc, op=ALU.mult)
                    nc.vector.tensor_tensor(out=chunked(bt), in0=chunked(bt), in1=pc, op=ALU.mult)\
                        .then_inc(hat_ready, 1)
                    if not first:
                        dve_lower(dve, g - 1)
                        dve.wait_ge(grp_done, g)
                    for n in range(NLV):
                        mask = cst[:, C_LV + P * n:C_LV + P * (n + 1)]
                        for q in range(4):
                            dve.wait_ge(z_ps, g * 4 * NLV + 4 * n + q + 1)
                            nc.vector.tensor_tensor(out=Z[:, 4 * q:4 * q + 4],
                                                    in0=bank[q][:].rearrange("p (t n) -> p t n", t=4),
                                                    in1=bc(mask, 4), op=ALU.mult).then_inc(z_ready, 1)
                        for q in range(4):
                            dve.wait_ge(x_ps, g * 4 * NLV + 4 * n + q + 1)
                            us = slice(4 * q, 4 * q + 4)
                            nc.vector.tensor_tensor(out=XT[:, us], in0=XT[:, us], op=ALU.add,
                                                    in1=bank[4 + q % 2][:].rearrange("p (t n) -> p t n", t=4))\
                                .then_inc(x_ready, 1)
                    if not last:
                        pro_params(g + 1)
                    for c in range(NCH):
                        rows = slice(CH * (c % 2), CH * (c % 2) + CH)
                        if c < NCH - 1:
                            if c == 0:
                                dve.wait_ge(sd_zero, g + 1)
                            for h_ in range(2):
                                hr = slice(CH * h_, CH * h_ + CH)
                                pr = pcb[hr].rearrange("p (a c) -> p a c", c=NCH)[:, :, c:c + 1]
                                ins = nc.vector.tensor_tensor(out=sp_[hr], in0=sd[hr, :, h_],
                                                              in1=pr.to_broadcast([CH, PAIRS, CH]), op=ALU.mult)
                            ins.then_inc(sp_ready, 1)
                            dve.wait_ge(sp_ready, g * (NCH - 1) + c + 1)
                        if not last:
                            if c == 1:
                                pro_kk(g + 1)
                            if c == 2:
                                pro_recip(g + 1, 0)
                            if c == 3:
                                pro_recip(g + 1, 1)
                        dve.wait_ge(sa_ps, g * NCH + c + 1)
                        nc.vector.tensor_copy(sab[rows], bank[5][rows]).then_inc(sa_ready, 1)
                        if not last and c == 2:
                            pro_scan(g + 1, NPC // 2, 3 * NPC // 4)
                        if c < NCH - 1:
                            dve.wait_ge(s_ps, g * (NCH - 1) + c + 1)
                            for h_ in range(2):
                                hr = slice(CH * h_, CH * h_ + CH)
                                ins = nc.vector.tensor_tensor(
                                    out=sd[hr, :, h_], in0=sp_[hr],
                                    in1=bank[0][hr, 0:PAIRS * CH].rearrange("p (a n) -> p a n", n=CH), op=ALU.add)
                            ins.then_inc(s_ready, 1)
                            dve.wait_ge(s_ready, g * (NCH - 1) + c + 1)
                        if not last and c == 0:
                            pro_max(g + 1, 0)
                            pro_max(g + 1, 1)
                        if not last and c == 1:
                            pro_scan(g + 1, 0, NPC // 2)
                    if not last:
                        pro_kkn(g + 1)
                        pro_scan(g + 1, 3 * NPC // 4, NPC)
                        pro_kmod(g + 1)
                        pro_bonus(g + 1)
                        pro_bv(g + 1)

                dve.wait_ge(zero_set, 1)
                pro_params(0)
                pro_kk(0)
                pro_max(0, 0)
                pro_max(0, 1)
                pro_scan(0, 0, NPC)
                pro_recip(0, 0)
                pro_recip(0, 1)
                pro_kkn(0)
                pro_kmod(0)
                pro_bonus(0)
                pro_bv(0)
                group(0, True, False)
                with dve.Fori(1, NGRP - 1) as g:
                    group(g, False, False)
                group(NGRP - 1, False, True)

            @block.tensor
            def _(pe):
                ones = cst[:, C_ONES:C_ONES + P]
                pro_bank = lambda i: bank[1 + i % 3]

                def turn(u, i, j):
                    for p in range(2):
                        for tt in range(TT):
                            last = nc.tensor.transpose(pro_bank(i)[:, p * T + tt * P:p * T + (tt + 1) * P],
                                                       rkvg[:, u, tt, (2 * j + p) * P:(2 * j + p + 1) * P], ident)
                    last.then_inc(pro_ps, 1)

                def lora(w, rows, x, i, j):
                    for p in range(2):
                        q = 2 * j + p
                        last = nc.tensor.matmul(pro_bank(i)[:, p * T:(p + 1) * T], w[:, q * P:(q + 1) * P],
                                                lora_h[rows, x], start=True, stop=True)
                    last.then_inc(pro_ps, 1)

                def lora_g(i, j):
                    for p in range(2):
                        q = 2 * j + p
                        for m in range(2):
                            last = nc.tensor.matmul(pro_bank(i)[:, p * T:(p + 1) * T], g2g[:, m, q * P:(q + 1) * P],
                                                    lora_h[:, 2 + m], start=(m == 0), stop=(m == 1))
                    last.then_inc(pro_ps, 1)

                def sums(x, i, j):
                    nc.tensor.matmul(pro_bank(i)[:], ones, halfof(x, j), start=True, stop=True).then_inc(pro_ps, 1)

                def pro_first(n):
                    pe.wait_ge(rkvg_in, 16 * (n * 3 + 3))
                    turn(1, 0, 0)
                    turn(1, 1, 1)
                    pe.wait_ge(l2_in, 16 * (n * 3 + 3))
                    lora(w2g, slice(0, LW), 0, 2, 0)

                def pro_sq(n):
                    pe.wait_ge(pro_act, n * NACT + 1)
                    sums(tmp, 3, 0)
                    pe.wait_ge(pro_act, n * NACT + 2)
                    sums(tmp, 4, 1)
                    pe.wait_ge(pro_act, n * NACT + 3)
                    lora(w2g, slice(0, LW), 0, 5, 1)

                def pro_a(n, j):
                    pe.wait_ge(pro_dve, n * NDVE + 1 + j)
                    lora(a2g, slice(0, LA), 1, 6 + j, j)

                def pro_r(n):
                    pe.wait_ge(pro_act, n * NACT + 4)
                    turn(0, 8, 0)
                    pe.wait_ge(pro_act, n * NACT + 5)
                    turn(0, 9, 1)

                def pro_v(n, j):
                    pe.wait_ge(pro_act, n * NACT + 6 + j)
                    turn(2, 10 + j, j)

                def pro_g(n):
                    pe.wait_ge(pro_act, n * NACT + 8)
                    lora_g(12, 0)
                    pe.wait_ge(pro_act, n * NACT + 9)
                    lora_g(13, 1)

                def pro_bonus(n):
                    pe.wait_ge(bon_ready, n + 1)
                    pe.wait_ge(pro_act, n * NACT + 10)
                    sums(dec, 14, 0)
                    pe.wait_ge(pro_act, n * NACT + 11)
                    sums(dec, 15, 1)

                def group(g, first, last_):
                    if not first:
                        pe_mean(pe, g - 1)
                    pe.wait_ge(factors_ready, g + 1)
                    pe.wait_ge(bk_ready, g + 1)
                    pe.wait_ge(pro_dve, (g + 1) * NDVE)
                    pe.wait_ge(pro_act, (g + 1) * NACT)
                    for h_ in range(2):
                        hr = slice(CH * h_, CH * h_ + CH)
                        for p in range(PAIRS):
                            j = h_ * PAIRS + p
                            if j >= 2:
                                pe.wait_ge(s3_read, g * 8 + j - 1)
                            for x, b0 in ((bt, 0), (kt_, 2)):
                                for tt in range(TT):
                                    last = nc.tensor.matmul(bank[b0 + j % 2][:, tt * T:(tt + 1) * T],
                                                            x[hr, p, tt * P:(tt + 1) * P],
                                                            ar[hr, p, tt].rearrange("p x n -> p (x n)"),
                                                            start=True, stop=True)
                            last.then_inc(s3_ps, 1)
                            q = j // 2
                            if p % 2 == 0 and q >= 2:
                                pe.wait_ge(l_ready, g * 4 + q - 1)
                            for tt in range(TT):
                                last = nc.tensor.matmul(bank[4 + q % 2][:, (p % 2) * T + tt * P:(p % 2) * T + (tt + 1) * P],
                                                        ar[hr, p, tt, 0], bt[hr, p, tt * P:(tt + 1) * P],
                                                        start=True, stop=True)
                            if p % 2:
                                last.then_inc(l_ps, 1)
                            if j == 1 and not first:
                                pe_var(pe, g - 1)
                    pe.wait_ge(s3_read, g * 8 + 8)
                    for n in range(NLV):
                        for q in range(4):
                            if n == 0:
                                pe.wait_ge(x0_ready, g * 4 + q + 1)
                            else:
                                pe.wait_ge(x_ready, g * 4 * NLV + 4 * (n - 1) + q + 1)
                            for k in range(4):
                                u = 4 * q + k
                                last = nc.tensor.matmul(bank[q][:, k * P:(k + 1) * P], Lm[:, u], XT[:, u],
                                                        start=True, stop=True)
                            last.then_inc(z_ps, 1)
                        for q in range(4):
                            if 4 * n + q >= 2:
                                pe.wait_ge(xt_read, g * 4 * NLV + 4 * n + q - 1)
                            for k in range(4):
                                last = nc.tensor.transpose(bank[6 + q % 2][:, k * P:(k + 1) * P], XT[:, 4 * q + k],
                                                           ident)
                            last.then_inc(xt_ps, 1)
                        for q in range(4):
                            pe.wait_ge(z_ready, g * 4 * NLV + 4 * n + q + 1)
                            pe.wait_ge(xt_read, g * 4 * NLV + 4 * n + q + 1)
                            if q >= 2:
                                pe.wait_ge(x_ready, g * 4 * NLV + 4 * n + q - 1)
                            for k in range(4):
                                u = 4 * q + k
                                last = nc.tensor.matmul(bank[4 + q % 2][:, k * P:(k + 1) * P], X[:, u], Z[:, u],
                                                        start=True, stop=True)
                            last.then_inc(x_ps, 1)
                    pe.wait_ge(hat_ready, g + 1)
                    for tt in range(TT):
                        for p in range(PAIRS):
                            nc.tensor.transpose(bank[tt][:, p * P:(p + 1) * P], bt[:, p, tt * P:(tt + 1) * P], ident)
                        for p in range(PAIRS):
                            last = nc.tensor.transpose(bank[2 + tt][:, p * P:(p + 1) * P],
                                                       kt_[:, p, tt * P:(tt + 1) * P], ident)
                        last.then_inc(hat_ps, 1)
                    pe.wait_ge(x_ready, (g + 1) * 4 * NLV)
                    pe.wait_ge(sd_zero, g + 1)
                    pe.wait_ge(vtok_ready, g + 1)
                    pe.wait_ge(hat_read, g * 2 + 2)
                    if not last_:
                        pro_first(g + 1)
                    for c in range(NCH):
                        tt, half = divmod(c, 2)
                        rows = slice(CH * half, CH * half + CH)
                        v_of = lambda p, h_: vtok[:, tt, p * P + h_ * CH:p * P + (h_ + 1) * CH]
                        if c:
                            pe.wait_ge(s_ready, g * (NCH - 1) + c)
                        for p in range(PAIRS):
                            nc.tensor.matmul(bank[4][rows, p * P:(p + 1) * P], ar[:, p, tt, 0, rows],
                                             sd[:, p].rearrange("p x n -> p (x n)"), start=True, stop=False)
                            for h_ in range(2):
                                last = nc.tensor.matmul(bank[4][rows, p * P + h_ * CH:p * P + (h_ + 1) * CH],
                                                        mk[:, unit(h_, p, tt), 0, rows], v_of(p, h_),
                                                        start=False, stop=(h_ == 1))
                        last.then_inc(w1_ps, 1)
                        if c >= 2:
                            pe.wait_ge(y_ready, g * NCH + c - 1)
                        for p in range(PAIRS):
                            yb = bank[6 + c % 2]
                            nc.tensor.matmul(yb[:, p * CH:(p + 1) * CH], sd[:, p].rearrange("p x n -> p (x n)"),
                                             ar[:, p, tt, 1, rows], start=(p == 0), stop=False, skip_group_check=True)
                            for h_ in range(2):
                                nc.tensor.matmul(yb[h_ * CH:(h_ + 1) * CH, p * CH:(p + 1) * CH], v_of(p, h_),
                                                 mk[:, unit(h_, p, tt), 1, rows], start=False, stop=False,
                                                 skip_group_check=True)
                        if not last_:
                            if c == 1:
                                pro_a(g + 1, 0)
                            if c == 2:
                                pro_v(g + 1, 0)
                        pe.wait_ge(w1_ready, g * NCH + c + 1)
                        for p in range(PAIRS):
                            for h_ in range(2):
                                cs = slice(p * P + h_ * CH, p * P + (h_ + 1) * CH)
                                last = nc.tensor.matmul(bank[5][rows, cs], XT[:, unit(h_, p, tt), rows],
                                                        w1b[:, cs], start=True, stop=True)
                        last.then_inc(sa_ps, 1)
                        pe.wait_ge(sa_ready, g * NCH + c + 1)
                        def y_sa(p, h_):
                            cs = slice(p * P + h_ * CH, p * P + (h_ + 1) * CH)
                            return nc.tensor.matmul(bank[6 + c % 2][h_ * CH:(h_ + 1) * CH, p * CH:(p + 1) * CH],
                                                    sab[:, cs], rbt[:, unit(h_, p, tt), rows], start=False,
                                                    stop=(p == PAIRS - 1), skip_group_check=True)
                        y_sa(0, 0)
                        if c < NCH - 1:
                            for p in range(PAIRS):
                                for h_ in range(2):
                                    cs = slice(p * P + h_ * CH, p * P + (h_ + 1) * CH)
                                    out = bank[0][h_ * CH:(h_ + 1) * CH, p * CH:(p + 1) * CH]
                                    nc.tensor.matmul(out, bh[rows, tt, cs], sab[rows, cs], start=True, stop=False)
                                    last = nc.tensor.matmul(out, kh[rows, tt, cs], vtok[rows, tt, cs],
                                                            start=False, stop=True)
                            last.then_inc(s_ps, 1)
                        for p in range(PAIRS):
                            for h_ in range(2):
                                if p or h_:
                                    last = y_sa(p, h_)
                        last.then_inc(y_ps, 1)
                        if not last_:
                            if c == 0:
                                pro_sq(g + 1)
                            if c == 1:
                                pro_a(g + 1, 1)
                                pro_r(g + 1)
                            if c == 2:
                                pro_v(g + 1, 1)
                                pro_g(g + 1)
                            if c == 3:
                                pro_bonus(g + 1)

                pro_first(0)
                pro_sq(0)
                pro_a(0, 0)
                pro_a(0, 1)
                pro_r(0)
                pro_v(0, 0)
                pro_v(0, 1)
                pro_g(0)
                pro_bonus(0)
                group(0, True, False)
                with pe.Fori(1, NGRP - 1) as g:
                    group(g, False, False)
                group(NGRP - 1, False, True)

        xs2 = at("xs2", WORK, [P, TT, D])
        u_ = at("u_", WORK + 16384, [P, 2, TT, SLAB])
        u2 = at("u2", WORK + 24576, [P, 2, TT, SLAB])
        kvs = at("kvs", WORK + 16384, [P, TT, 6, SLAB])
        qs = at("qs", WORK + 40960, [P, TT, D])
        NG3 = 3 * HB
        gw = at("gw", WORK + 57344, [P, KT, NG3])
        gwh = at("gwh", WORK + 60416, [P, KT, NG3], F32R)
        gwl = at("gwl", WORK + 63488, [P, KT, NG3], F32R)
        gates = at("gates", WORK + 66560, [P, TT, NG3])
        gatesT = at("gatesT", WORK + 66944, [NG3, T])

        h_in = sem("h_in")
        norm_hi, norm_lo = sem("norm_hi"), sem("norm_lo")
        sq_ready, hT_ps, hT_hi, hT_lo = sem("sq_ready"), sem("hT_ps"), sem("hT_hi"), sem("hT_lo")
        gw_in, gw_hi, gw_lo, gate_ps, gate_sig = (sem(n) for n in ("gw_in", "gw_hi", "gw_lo", "gate_ps", "gate_sig"))
        HPG = NS * 2
        CPG = HPG * CPS

        def act_split(act, k, name, xh):
            nc.scalar.activation(xh[:, k], bank[k // 2][:, (k % 2) * T:(k % 2 + 1) * T], ACT.Copy,
                                 scale=col(name, k)).then_inc(norm_hi, 1)

        def act_split_norm(act, n, name, xh):
            for k in range(KT):
                act.wait_ge(norm_T, 8 * n + k // 2 + 1)
                act_split(act, k, name, xh)

        def dve_split(dve, k, name, xh, xl):
            nc.vector.scalar_tensor_tensor(out=xl[:, k], in0=bank[k // 2][:, (k % 2) * T:(k % 2 + 1) * T],
                                           scalar=col(name, k), in1=xh[:, k].bitcast(F32),
                                           op0=ALU.mult, op1=ALU.subtract).then_inc(norm_lo, 1)

        def dve_split_norm(dve, base, name, xh, xl):
            for k in range(KT):
                dve.wait_ge(norm_hi, base + (k | 1) + 1)
                dve_split(dve, k, name, xh, xl)

        NB = KT // 2

        def first_at(b):
            return max(0, 2 * b - 1)

        def second_at(b):
            return min(2 * b + 2, 2 * NB - 1)

        def add_slab(dve, S, s, half):
            dve.wait_ge(w_used, CPS * S + CPS)
            for tt in range(TT):
                last = nc.vector.tensor_tensor(out=h[:, tt, s * SLAB:(s + 1) * SLAB],
                                               in0=h[:, tt, s * SLAB:(s + 1) * SLAB],
                                               in1=bank[2 * half + tt][:], op=ALU.add)
            last.then_inc(acc_free, 1)

        def act_mlp(act, layer, cb, sb):
            with act.Fori(0, NG) as g:
                for s in range(HPG):
                    for c in range(CPS):
                        split_hi(act, g * CPG + cb + s * CPS + c, g * (CPG // RING) + (cb + s * CPS + c) // RING, c)
                        if c == 2 and 1 <= s <= NS:
                            half = (s - 1) % 2
                            act.wait_ge(w_used, g * CPG + cb + s * CPS)
                            if s >= 3:
                                act.wait_ge(sq_ready, g * NS + layer * NG * NS + s - 2)
                            for tt in range(TT):
                                last = nc.scalar.activation(u_[:, half, tt], bank[2 * half + tt][:], ACT.Relu)
                            last.then_inc(acc_free, 1)
                        if c == CPS - 1 and 1 <= s <= NS:
                            n = g * NS + layer * NG * NS + s
                            act.wait_ge(hT_ps, n)
                            for j in range(2):
                                last = nc.scalar.activation(
                                    xbh[:, (s - 1) * 4 + 2 * j:(s - 1) * 4 + 2 * j + 2].rearrange("p a n -> p (a n)"),
                                    bank[4 + j][:], ACT.Copy)
                            last.then_inc(hT_hi, 1)

        def pool_mlp(pool, layer, cb, sb):
            with pool.Fori(0, NG) as g:
                for s in range(NS):
                    pool.wait_ge(acc_free, g * HPG + sb + s + 1)
                    if layer or s >= 2:
                        pool.wait_ge(hT_ps, g * NS + layer * NG * NS + s - 1)
                    nc.gpsimd.tensor_tensor(out=u2[:, s % 2], in0=u_[:, s % 2], in1=u_[:, s % 2],
                                            op=ALU.mult).then_inc(sq_ready, 1)

        def dve_mlp(dve, layer, cb, sb):
            with dve.Fori(0, NG) as g:
                for s in range(HPG):
                    for c in range(CPS):
                        split_lo(dve, g * CPG + cb + s * CPS + c, c)
                        if c == 2 and s > NS:
                            add_slab(dve, g * HPG + sb + s - 1, s - 1 - NS, (s - 1) % 2)
                        if c == CPS - 1 and 1 <= s <= NS:
                            n = g * NS + layer * NG * NS + s
                            dve.wait_ge(hT_hi, n)
                            for j in range(2):
                                kk = slice((s - 1) * 4 + 2 * j, (s - 1) * 4 + 2 * j + 2)
                                last = nc.vector.tensor_tensor(
                                    out=xbl[:, kk].rearrange("p a n -> p (a n)"), in0=bank[4 + j][:],
                                    in1=xbh[:, kk].bitcast(F32).rearrange("p a n -> p (a n)"), op=ALU.subtract)
                            last.then_inc(hT_lo, 1)
                add_slab(dve, g * HPG + sb + HPG - 1, NS - 1, 1)

        def pe_mlp(pe, layer, cb, sb, nlo):
            with pe.Fori(0, NG) as g:
                for s in range(HPG):
                    def before(c):
                        if s < NS:
                            pe.wait_ge(norm_lo, nlo + 2 * c + 2 if s == 0 and c >= 2 else nlo + 16 if s else nlo + 4)
                        if c == 4 and 1 <= s <= NS:
                            n = g * NS + layer * NG * NS + s
                            pe.wait_ge(sq_ready, n)
                            if layer or s > 1:
                                pe.wait_ge(hT_lo, n - 1)
                            for j in range(4):
                                for tt in range(TT):
                                    last = nc.tensor.transpose(
                                        bank[4 + j // 2][:, (j % 2) * T + tt * P:(j % 2) * T + (tt + 1) * P],
                                        u2[:, (s - 1) % 2, tt, j * P:(j + 1) * P], ident)
                            last.then_inc(hT_ps, 1)
                        if s >= NS:
                            pe.wait_ge(hT_lo, g * NS + layer * NG * NS + (NS - 1 if s == NS and c < 6 else NS))
                    xh, xl = (xah, xal) if s < NS else (xbh, xbl)
                    slab_matmuls(pe, g * CPG + cb + s * CPS, g * HPG + sb + s, s % 2, xh, xl, before)

        def sp_mlp(sp, layer, cb, sb):
            with sp.Fori(0, NG) as g:
                for s in range(HPG):
                    for c in range(CPS):
                        G = g * CPG + cb + s * CPS + c
                        if s < NS:
                            load_chunk(sp, t['mlp_up'][layer], G, c, c * KC * P, g * D + s * SLAB)
                        else:
                            load_chunk(sp, t['mlp_down'][layer], G, c, g * D + c * KC * P, (s - NS) * SLAB)

        AHEAD = 3

        def act_unit(act, unit, evac, done=0):
            for s in range(unit['slabs']):
                for c in range(CPS):
                    G = unit['chunk'] + s * CPS + c
                    if s * CPS + c >= done:
                        split_hi(act, G, G // RING, c)
                    if c == 2 and s:
                        evac(s - 1)
            evac(unit['slabs'] - 1)

        def dve_unit(dve, unit, evac, done=0):
            for s in range(unit['slabs']):
                for c in range(CPS):
                    if s * CPS + c >= done:
                        split_lo(dve, unit['chunk'] + s * CPS + c, c)
                    if c == 2 and s:
                        evac(s - 1)
            evac(unit['slabs'] - 1)

        def nothing(s):
            pass

        mlp0 = dict(stream)
        new_unit(HPG * NG)
        u_kv = new_unit(6)
        u_q = new_unit(NS)

        with nc.Block() as block:
            @block.sync
            def _(sp):
                sp.dma_start(h[:], t['x'].rearrange("b (t p) d -> p (b t) d", p=P)).then_inc(h_in, 16)
                for c in range(RING, CPS):
                    load_chunk(sp, t['rw_wo'][0], u_wo['chunk'] + c, c, c * KC * P, 0)
                with sp.Fori(1, NS) as s:
                    for c in range(CPS):
                        load_chunk(sp, t['rw_wo'][0], u_wo['chunk'] + CPS * s + c, c, c * KC * P, s * SLAB)
                sp_mlp(sp, 0, mlp0['chunk'], mlp0['slab'])
                sp_unit(sp, t['w_kv'], u_kv)
                sp_unit(sp, t['nsa_wq'][0], u_q)

            @block.gpsimd
            def _(pool):
                pool_epilogue(pool, NGRP - 1)
                pool.wait_ge(grp_done, NGRP)
                pool.dma_start(gw[:], t['nsa_wq'][0][:, D:D + NG3].rearrange("(k p) n -> p k n", p=P))\
                    .then_inc(gw_in, 16)
                pool_mlp(pool, 0, mlp0['chunk'], mlp0['slab'])

            @block.scalar
            def _(act):
                e = NGRP - 1
                for s in range(NS):
                    for c in range(CPS):
                        G = u_wo['chunk'] + s * CPS + c
                        split_hi(act, G, G // RING, c)
                        if s == 0:
                            if c == 0:
                                act_square(act, e)
                            if c == 2:
                                act_std(act, e)
                            if c == 5:
                                act_upper(act, e)
                act_norm_sum(act, 1, lambda s: act.wait_ge(acc_free, mlp0['slab'] - (NS - 1 - s)), xs2)
                act_norm_sqrt(act, 1)
                act_split_norm(act, 1, 'm0', xah)
                act_mlp(act, 0, mlp0['chunk'], mlp0['slab'])

                def slab_added(s):
                    if s == NS - 1:
                        for c in range(AHEAD):
                            G = u_kv['chunk'] + c
                            split_hi(act, G, G // RING, c)
                    act.wait_ge(acc_free, u_kv['slab'] - (NS - 1 - s))
                act_norm_sum(act, 2, slab_added, xs2)
                act_norm_sqrt(act, 2)
                for b in range(NB + 1):
                    if b < NB:
                        act.wait_ge(norm_T, 8 * 2 + b + 1)
                        act_split(act, 2 * b, 'kv_norm_g', xah)
                        act_split(act, 2 * b + 1, 'kv_norm_g', xah)
                    if b:
                        act.wait_ge(norm_lo, KT + 2 * first_at(b - 1) + 2)
                        act_split(act, 2 * b - 2, 'b_norm_g', xbh)
                        act_split(act, 2 * b - 1, 'b_norm_g', xbh)

                def kv_evac(s):
                    if s == 1:
                        act.wait_ge(gw_in, 16)
                        nc.scalar.activation(gwh[:], gw[:], ACT.Copy).then_inc(gw_hi, 1)
                    act.wait_ge(w_used, u_kv['chunk'] + CPS * (s + 1))
                    for tt in range(TT):
                        last = nc.scalar.activation(kvs[:, tt, s], bank[2 * (s % 2) + tt][:], ACT.Copy)
                    last.then_inc(acc_free, 1)

                def q_evac(s):
                    if s == 1:
                        act.wait_ge(gate_ps, 1)
                        nc.scalar.activation(gatesT[:], bank[6][0:NG3, 0:T], ACT.Sigmoid).then_inc(gate_sig, 1)
                    act.wait_ge(w_used, u_q['chunk'] + CPS * (s + 1))
                    for tt in range(TT):
                        last = nc.scalar.activation(qs[:, tt, s * SLAB:(s + 1) * SLAB], bank[2 * (s % 2) + tt][:],
                                                    ACT.Copy, scale=HD ** -0.5)
                    last.then_inc(acc_free, 1)
                act_unit(act, u_kv, kv_evac, AHEAD)
                act_unit(act, u_q, q_evac)
                act.wait_ge(gate_ps, 2)
                for tt in range(TT):
                    nc.scalar.activation(gates[:, tt], bank[7][:, tt * NG3:(tt + 1) * NG3], ACT.Copy)

            @block.vector
            def _(dve):
                e = NGRP - 1
                dve_epi_d(dve, e)
                for s in range(NS):
                    for c in range(CPS):
                        split_lo(dve, u_wo['chunk'] + s * CPS + c, c)
                        if s == 0:
                            if c in (2, 3):
                                dve_recip(dve, e, c - 2)
                            if c == 4:
                                dve_epi_norm(dve, e)
                            if c == 5:
                                dve_lower(dve, e)
                        if c == 2 and s:
                            if s == 1:
                                dve.wait_ge(h_in, 16)
                            add_slab(dve, u_wo['slab'] + s - 1, s - 1, (s - 1) % 2)
                add_slab(dve, u_wo['slab'] + NS - 1, NS - 1, (NS - 1) % 2)
                dve_norm(dve, 1, xs2)
                dve_split_norm(dve, 0, 'm0', xah, xal)
                dve_mlp(dve, 0, mlp0['chunk'], mlp0['slab'])
                split_lo(dve, u_kv['chunk'], 0)
                dve_norm(dve, 2, xs2)
                for c in range(1, AHEAD):
                    split_lo(dve, u_kv['chunk'] + c, c)
                for b in range(NB + 1):
                    if b < NB:
                        dve.wait_ge(norm_hi, KT + 2 * first_at(b) + 2)
                        dve_split(dve, 2 * b, 'kv_norm_g', xah, xal)
                        dve_split(dve, 2 * b + 1, 'kv_norm_g', xah, xal)
                    if b:
                        dve.wait_ge(norm_hi, KT + 2 * second_at(b - 1) + 2)
                        dve_split(dve, 2 * b - 2, 'b_norm_g', xbh, xbl)
                        dve_split(dve, 2 * b - 1, 'b_norm_g', xbh, xbl)

                def gate_weights(s):
                    if s == 2:
                        dve.wait_ge(gw_hi, 1)
                        nc.vector.tensor_tensor(out=gwl[:], in0=gw[:], in1=gwh[:].bitcast(F32),
                                                op=ALU.subtract).then_inc(gw_lo, 1)
                dve_unit(dve, u_kv, gate_weights, AHEAD)
                dve_unit(dve, u_q, nothing)

            @block.tensor
            def _(pe):
                pe_mean(pe, NGRP - 1)

                def before(c):
                    if c == 1:
                        pe_var(pe, NGRP - 1)
                    if c == KT * 3 // 4 // KC:
                        pe.wait_ge(grp_done, NGRP)
                for s in range(NS):
                    slab_matmuls(pe, u_wo['chunk'] + CPS * s, u_wo['slab'] + s, s % 2, xbh, xbl,
                                 None if s else before)
                pe_norm(pe, 1, xs2)
                pe_mlp(pe, 0, mlp0['chunk'], mlp0['slab'], 0)
                pe_norm(pe, 2, xs2)

                def split_done(c):
                    pe.wait_ge(norm_lo, KT + 2 * max(first_at(c), second_at(1)) + 2)
                pe_unit(pe, u_kv, xah, xal, split_done)
                pe.wait_ge(norm_lo, 3 * KT)
                pe.wait_ge(gw_lo, 1)
                for k in range(KT):
                    first, end = k == 0, k == KT - 1
                    nc.tensor.matmul(bank[6][0:NG3, 0:T], gwh[:, k], xbh[:, k], start=first, stop=False)
                    nc.tensor.matmul(bank[6][0:NG3, 0:T], gwl[:, k], xbh[:, k], start=False, stop=False)
                    last = nc.tensor.matmul(bank[6][0:NG3, 0:T], gwh[:, k], xbl[:, k], start=False, stop=end)
                last.then_inc(gate_ps, 1)
                pe_unit(pe, u_q, xbh, xbl)
                pe.wait_ge(gate_sig, 1)
                for tt in range(TT):
                    last = nc.tensor.transpose(bank[7][:, tt * NG3:(tt + 1) * NG3], gatesT[:, tt * P:(tt + 1) * P],
                                               ident[0:NG3, 0:NG3])
                last.then_inc(gate_ps, 1)

        CP = (0, 1, 2, 4)
        kT4 = at("kT4", XA_AT, [P, 4, GB, T])
        xc = at("xc", XA_AT + 16384, [P, 2, 32, GB * NCB])
        cw1 = at("cw1", XA_AT + 31744, [P, 2, 32, P])
        tb = at("tb", XA_AT + 64512, [P, HB, T])
        tbr = at("tbr", XB_AT, [P, HB, T])
        qg = at("qg", WORK + 57344, [P, TT, SLAB])
        qT4 = at("qT4", XA_AT + 35840, [P, REP, T])
        vg = at("vg", WORK + 61440, [P, TT, 2, HD])
        vcg = at("vcg", WORK + 63488, [P, HD])
        s0 = at("s0", XA_AT + 42496, [P, 2, 2, P])
        s1 = at("s1", XA_AT + 44544, [P, 2, 2, T])
        sc = at("sc", XA_AT + 48640, [P, 2, TT, 16])
        pt1 = at("pt1", XA_AT + 48896, [P, 2, SLAB])
        pt2 = at("pt2", XA_AT + 52992, [P, 2, 256])
        ptc = at("ptc", XA_AT + 55040, [P, 2, T])
        mx = at("mx", XA_AT + 57088, [P, 2, 6])
        sm = at("sm", XA_AT + 57152, [P, 2, 6])
        cst2 = at("cst2", WORK, [P, 512 + TT])
        dist_of = cst2[0:BUCKETS + 1, 0:512]
        row_ok = cst2[:, 512:512 + TT]
        tabx = at("tabx", WORK + 4128, [BUCKETS + 1, HB])
        grow = at("grow", WORK + 4224, [HB, 512])
        tbc = at("tbc", WORK + 6272, [P, TT, HB, 16])
        cw2 = at("cw2", WORK + 8320, [P, 2, P])
        pebr = at("pebr", WORK + 9344, [66, P])
        peb = at("peb", WORK + 9856, [P, 66])
        hid = at("hid", WORK + 10144, [GB * NCB, 2, P])
        gel = at("gel", WORK + 11168, [P, 2, GB * NCB])
        kcT = at("kcT", WORK + 11680, [P, GB * NCB])
        vcs = at("vcs", WORK + 11936, [NCB, GB, HD])
        dist_scratch = nc.dram_tensor("dist_scratch", [HB, 512], F32, kind="Internal").ap()

        c2_in, cw_in, tab_in = sem("c2_in"), sem("cw_in"), sem("tab_in")
        tab_one, tb_ready = sem("tab_one"), sem("tb_ready")
        kT_ps, kT_act, kT_dve = sem("kT_ps"), sem("kT_act"), sem("kT_dve")
        peb_ps, peb_ready, dist_ps, dist_ready, dist_out, tb_in = (
            sem("peb_ps"), sem("peb_ready"), sem("dist_ps"), sem("dist_ready"), sem("dist_out"), sem("tb_in"))
        bc_ps, xc_ready, hid_ps, hid_ready, hidT_ps, gel_ready = (sem(n) for n in (
            "bc_ps", "xc_ready", "hid_ps", "hid_ready", "hidT_ps", "gel_ready"))
        kc_ps, kc_ready, gates_ok = sem("kc_ps"), sem("kc_ready"), sem("gates_ok")
        q_in, v_in, qT_ps, qT_ready = sem("q_in"), sem("v_in"), sem("qT_ps"), sem("qT_ready")
        pad0 = sem("pad0")
        sc_ps, biased, maxed, sums, weights, pT_ps, pT1, pT2, o_ps, oa_hi, oa_lo = (sem(n) for n in (
            "sc_ps", "biased", "maxed", "sums", "weights", "pT_ps", "pT1", "pT2", "o_ps", "oa_hi", "oa_lo"))
        mx_raw, sm_rec, sm_gated = sem("mx_raw"), sem("sm_rec"), sem("sm_gated")

        with nc.Block() as block:
            @block.sync
            def _(sp):
                sp.dma_start(cst2[:], t['consts2']).then_inc(c2_in, 16)
                sp.dma_start(tabx[0:BUCKETS], t['rel_bias']).then_inc(tab_in, 16)
                sp.dma_start(pebr[0:64], t['cmp_pe'].rearrange("a l d -> (a l) d")).then_inc(c2_in, 16)
                sp.dma_start(pebr[64:66], t['cmp_b1']).then_inc(c2_in, 16)
                sp.dma_start(cw2[:], t['cmp_w2'].rearrange("a k n -> k a n")).then_inc(cw_in, 16)
                for a in range(2):
                    sp.dma_start(cw1[:, a], t['cmp_w1'][a].rearrange("(l d) n -> d l n", d=P)).then_inc(cw_in, 16)
                sp.wait_ge(dist_ready, 1)
                sp.dma_start(dist_scratch, grow[:]).then_inc(dist_out, 16)
                sp.wait_ge(dist_out, 16)
                for a in range(HB):
                    skew = bass.AP(tensor=dist_scratch.tensor, offset=512 * a + P + 1, ap=[[1, P], [1, T]])
                    sp.dma_start(tbr[:, a], skew).then_inc(tb_in, 16)

            @block.gpsimd
            def _(pool):
                nc.gpsimd.memset(tabx[BUCKETS:BUCKETS + 1], 1.0).then_inc(tab_one, 1)
                def queries(g):
                    nc.gpsimd.tensor_copy(qg[:], qs[:, :, bass.ds(g * SLAB, SLAB)]).then_inc(q_in, 1)

                def values(g):
                    for b in range(2):
                        nc.gpsimd.tensor_copy(vg[:, :, b], kvs[:, :, 3 + 2 * b, bass.ds(g * HD, HD)])
                    nc.gpsimd.tensor_copy(vcg[0:NCB], vcs[:, bass.ds(g, 1)].rearrange("p a n -> p (a n)"))\
                        .then_inc(v_in, 1)
                pool.wait_ge(tab_one, 1)
                queries(0)
                pool.wait_ge(q_in, 1)
                pool.wait_ge(kc_ready, 1)
                nc.gpsimd.memset(vcg[:], 0.0)
                nc.gpsimd.memset(ptc[:], 0.0).then_inc(pad0, 1)
                pool.wait_ge(pad0, 1)
                values(0)
                with pool.Fori(1, GB) as g:
                    pool.wait_ge(qT_ps, g)
                    queries(g)
                    pool.wait_ge(o_ps, g * REP)
                    values(g)

            @block.scalar
            def _(act):
                for j in range(0, 8, 2):
                    act.wait_ge(kT_ps, j + 1)
                    nc.scalar.activation(kT4[:, j // 2, (j % 2) * 2:(j % 2) * 2 + 2].rearrange("p a n -> p (a n)"),
                                         bank[j][:], ACT.Copy).then_inc(kT_act, 1)
                act.wait_ge(dist_ps, 1)
                nc.scalar.activation(grow[:], bank[1][0:HB], ACT.Copy).then_inc(dist_ready, 1)
                act.wait_ge(hid_ps, 1)
                for a in range(2):
                    last = nc.scalar.activation(hid[:, a], bank[4 + a][0:GB * NCB, 0:P], ACT.Copy)
                last.then_inc(hid_ready, 1)
                act.wait_ge(hidT_ps, 1)
                for a in range(2):
                    last = nc.scalar.activation(gel[:, a], bank[6][:, a * 64:a * 64 + GB * NCB], ACT.Gelu_apprx_tanh,
                                                bias=peb[:, 64 + a:65 + a])
                last.then_inc(gel_ready, 1)
                def queries(g):
                    act.wait_ge(qT_ps, g + 1)
                    for j in range(2):
                        last = nc.scalar.activation(qT4[:, 2 * j:2 * j + 2].rearrange("p a n -> p (a n)"),
                                                    bank[j][:], ACT.Copy)
                    last.then_inc(qT_ready, 1)

                def exps(g, r):
                    b = r % 2
                    act.wait_ge(maxed, g * REP + r + 1)
                    for tt in range(TT):
                        nc.scalar.activation(sc[:, b, tt, 0:NCB], sc[:, b, tt, 0:NCB], ACT.Exp,
                                             bias=mx[:, b, 3 * tt:3 * tt + 1], accum_out=sm[:, b, 3 * tt:3 * tt + 1])
                        for br in range(2):
                            s = (s0, s1)[tt][:, b, br]
                            n = 3 * tt + 1 + br
                            last = nc.scalar.activation(s, s, ACT.Exp, bias=mx[:, b, n:n + 1],
                                                        accum_out=sm[:, b, n:n + 1])
                    last.then_inc(sums, 1)

                def group(g, last_group):
                    for r in range(REP):
                        act.wait_ge(pT_ps, g * REP + r + 1)
                        nc.scalar.activation(pt1[:, r % 2], bank[4][:], ACT.Copy).then_inc(pT1, 1)
                        if r == REP - 2 and not last_group:
                            queries(g + 1)
                        if r < REP - 2 or (r == REP - 1 and not last_group):
                            exps(g, r + 2 if r < REP - 2 else REP)
                        act.wait_ge(o_ps, g * REP + r + 1)
                        nc.scalar.activation(xbh[:, bass.ds(g * REP + r, 1)].rearrange("p a n -> p (a n)"),
                                             bank[6 + r % 2][:, 0:T], ACT.Copy).then_inc(oa_hi, 1)
                    if not last_group:
                        exps(g, REP + 1)

                queries(0)
                exps(0, 0)
                exps(0, 1)
                with act.Fori(0, GB - 1) as g:
                    group(g, False)
                group(GB - 1, True)

            @block.vector
            def _(dve):
                for j in range(1, 8, 2):
                    dve.wait_ge(kT_ps, j + 1)
                    nc.vector.tensor_copy(kT4[:, j // 2, (j % 2) * 2:(j % 2) * 2 + 2].rearrange("p a n -> p (a n)"),
                                          bank[j][:]).then_inc(kT_dve, 1)
                dve.wait_ge(peb_ps, 1)
                nc.vector.tensor_copy(peb[:], bank[0][:, 0:66]).then_inc(peb_ready, 1)
                dve.wait_ge(bc_ps, 1)
                for tt in range(TT):
                    nc.vector.tensor_copy(tbc[:, tt, :, 0:NCB].rearrange("p h c -> p c h"),
                                          bank[2 + tt][:, 0:NCB * HB].rearrange("p (c h) -> p c h", h=HB))
                dve.wait_ge(c2_in, 16)
                for tt in range(TT):
                    last = nc.vector.tensor_scalar(gates[:, tt].rearrange("p (h b) -> p h b", b=3)[:, :, 0],
                                                   gates[:, tt].rearrange("p (h b) -> p h b", b=3)[:, :, 0],
                                                   row_ok[:, tt:tt + 1], None, ALU.mult)
                last.then_inc(gates_ok, 1)
                dve.wait_ge(peb_ready, 1)
                dve.wait_ge(kT_act, 4)
                dve.wait_ge(kT_dve, 4)
                for a in range(2):
                    for gg in range(GB):
                        for hf in range(2):
                            src = kT4[:, a, gg, hf * 16:hf * 16 + NCB * 16].rearrange("p (c l) -> p c l", l=16)
                            dst = xc[:, a, hf * 16:hf * 16 + 16, gg * NCB:(gg + 1) * NCB].rearrange("p l c -> p c l")
                            pe_ = peb[:, a * 32 + hf * 16:a * 32 + hf * 16 + 16]
                            last = nc.vector.tensor_tensor(out=dst, in0=src, in1=bc(pe_, NCB), op=ALU.add)
                last.then_inc(xc_ready, 1)
                dve.wait_ge(kc_ps, 1)
                nc.vector.tensor_copy(kcT[:], bank[7][:, 0:GB * NCB])
                nc.vector.tensor_copy(vcs[:].rearrange("p a n -> p (a n)"), bank[0][0:NCB]).then_inc(kc_ready, 1)
                dve.wait_ge(tb_in, 16 * (HB))
                nc.vector.tensor_copy(tb[:], tbr[:, :, ::-1]).then_inc(tb_ready, 1)
                dve.wait_ge(tb_ready, 1)
                dve.wait_ge(gates_ok, 1)
                def bias(g, r):
                    b = r % 2
                    n = g * REP + r
                    a = bass.ds(n, 1)
                    A, B = bank[b], bank[2 + b]
                    dve.wait_ge(sc_ps, n + 1)
                    if later(n, 1):
                        dve.wait_ge(pT_ps, n - 1)
                    nc.vector.tensor_tensor(out=s0[:, b], in0=A[:, 0:256].rearrange("p (a n) -> p a n", a=2),
                                            in1=tb[:, a, P:T].to_broadcast([P, 2, P]), op=ALU.add)
                    nc.vector.tensor_tensor(out=s1[:, b], in0=B[:].rearrange("p (a n) -> p a n", a=2),
                                            in1=tb[:, a].to_broadcast([P, 2, T]), op=ALU.add)
                    nc.vector.tensor_tensor(out=sc[:, b, :, 0:NCB],
                                            in0=A[:, 256:288].rearrange("p (a n) -> p a n", n=16)[:, :, 0:NCB],
                                            in1=tbc[:, :, a, 0:NCB].rearrange("p t a n -> p (t a) n"),
                                            op=ALU.add).then_inc(biased, 1)
                    dve.wait_ge(biased, n + 1)
                    m3 = mx[:, b].rearrange("p (t n) -> p t n", t=2)
                    nc.vector.reduce_max(m3[:, 0, 1:3], s0[:, b], AX.X)
                    nc.vector.reduce_max(m3[:, 1, 1:3], s1[:, b], AX.X)
                    nc.vector.reduce_max(m3[:, :, 0], sc[:, b, :, 0:NCB], AX.X).then_inc(mx_raw, 1)
                    dve.wait_ge(mx_raw, n + 1)
                    nc.vector.tensor_scalar(mx[:, b], mx[:, b], -1.0, None, ALU.mult).then_inc(maxed, 1)

                def lower(g, r):
                    dve.wait_ge(oa_hi, g * REP + r + 1)
                    a = bass.ds(g * REP + r, 1)
                    nc.vector.tensor_tensor(out=xbl[:, a].rearrange("p a n -> p (a n)"), in0=bank[6 + r % 2][:, 0:T],
                                            in1=xbh[:, a].bitcast(F32).rearrange("p a n -> p (a n)"),
                                            op=ALU.subtract).then_inc(oa_lo, 1)

                def group(g, last_group):
                    for r in range(REP):
                        b = r % 2
                        n = g * REP + r
                        dve.wait_ge(sums, n + 1)
                        nc.vector.reciprocal(sm[:, b], sm[:, b]).then_inc(sm_rec, 1)
                        dve.wait_ge(sm_rec, n + 1)
                        s3 = sm[:, b].rearrange("p (t n) -> p t n", t=2)
                        nc.vector.tensor_tensor(out=s3, in0=s3, in1=gates[:, :, bass.ds(n * 3, 3)],
                                                op=ALU.mult).then_inc(sm_gated, 1)
                        dve.wait_ge(sm_gated, n + 1)
                        nc.vector.tensor_tensor(out=s0[:, b], in0=s0[:, b], op=ALU.mult,
                                                in1=sm[:, b, 1:3].unsqueeze(2).to_broadcast([P, 2, P]))
                        nc.vector.tensor_tensor(out=s1[:, b], in0=s1[:, b], op=ALU.mult,
                                                in1=sm[:, b, 4:6].unsqueeze(2).to_broadcast([P, 2, T]))
                        nc.vector.tensor_tensor(out=sc[:, b, :, 0:NCB], in0=sc[:, b, :, 0:NCB], op=ALU.mult,
                                                in1=s3[:, :, 0:1].to_broadcast([P, 2, NCB])).then_inc(weights, 1)
                        if r:
                            lower(g, r - 1)
                        dve.wait_ge(pT_ps, n + 1)
                        nc.vector.tensor_copy(pt2[:, b], bank[5][:, 0:256])
                        nc.vector.tensor_copy(ptc[0:NCB, b], bank[5][0:NCB, 256:512]).then_inc(pT2, 1)
                        if r < REP - 2:
                            bias(g, r + 2)
                        if r == REP - 1 and not last_group:
                            bias(g, REP)
                    if not last_group:
                        bias(g, REP + 1)
                    lower(g, REP - 1)

                dve.wait_ge(pad0, 1)
                bias(0, 0)
                bias(0, 1)
                with dve.Fori(0, GB - 1) as g:
                    group(g, False)
                group(GB - 1, True)

            @block.tensor
            def _(pe):
                for n, part in enumerate(CP):
                    for j in range(2):
                        for k in range(2):
                            gg = 2 * j + k
                            for tt in range(TT):
                                last = nc.tensor.transpose(bank[2 * n + j][:, k * T + tt * P:k * T + (tt + 1) * P],
                                                           kvs[:, tt, part, gg * HD:(gg + 1) * HD], ident)
                        last.then_inc(kT_ps, 1)
                pe.wait_ge(c2_in, 48)
                pe.wait_ge(kT_act, 1)
                nc.tensor.transpose(bank[0][:, 0:66], pebr[:], ident[0:66, 0:66]).then_inc(peb_ps, 1)
                pe.wait_ge(tab_in, 16)
                pe.wait_ge(tab_one, 1)
                pe.wait_ge(kT_dve, 1)
                nc.tensor.matmul(bank[1][0:HB], tabx[:], dist_of, start=True, stop=True).then_inc(dist_ps, 1)
                pe.wait_ge(kT_act, 2)
                pe.wait_ge(kT_dve, 2)
                for tt in range(TT):
                    for c in range(NCB):
                        i0 = T + P * tt - (31 + 16 * c)
                        last = nc.tensor.matmul(bank[2 + tt][:, c * HB:(c + 1) * HB], dist_of[:, i0:i0 + P], tabx[:],
                                                start=True, stop=True)
                last.then_inc(bc_ps, 1)
                pe.wait_ge(cw_in, 48)
                pe.wait_ge(xc_ready, 1)
                pe.wait_ge(kT_act, 4)
                pe.wait_ge(kT_dve, 4)
                for a in range(2):
                    for l in range(32):
                        last = nc.tensor.matmul(bank[4 + a][0:GB * NCB, 0:P], xc[:, a, l], cw1[:, a, l],
                                                start=(l == 0), stop=(l == 31))
                last.then_inc(hid_ps, 1)
                pe.wait_ge(hid_ready, 1)
                for a in range(2):
                    last = nc.tensor.transpose(bank[6][:, a * 64:a * 64 + GB * NCB], hid[:, a],
                                               ident[0:GB * NCB, 0:GB * NCB])
                last.then_inc(hidT_ps, 1)
                pe.wait_ge(gel_ready, 1)
                nc.tensor.matmul(bank[7][:, 0:GB * NCB], cw2[:, 0], gel[:, 0], start=True, stop=True)
                for gg in range(GB):
                    last = nc.tensor.matmul(bank[0][0:NCB, gg * HD:(gg + 1) * HD],
                                            gel[:, 1, gg * NCB:(gg + 1) * NCB], cw2[:, 1], start=True, stop=True)
                last.then_inc(kc_ps, 1)
                pe.wait_ge(dist_ready, 1)
                pe.wait_ge(kc_ready, 1)
                def queries(g):
                    pe.wait_ge(q_in, g + 1)
                    for r in range(REP):
                        for tt in range(TT):
                            last = nc.tensor.transpose(bank[r // 2][:, (r % 2) * T + tt * P:(r % 2) * T + (tt + 1) * P],
                                                       qg[:, tt, r * HD:(r + 1) * HD], ident)
                    last.then_inc(qT_ps, 1)

                def scores(g, r):
                    b = r % 2
                    A, B = bank[b], bank[2 + b]
                    if later(g, 0) or r >= 2:
                        pe.wait_ge(biased, g * REP + r - 1)
                    nc.tensor.matmul(A[:, 0:256].rearrange("p (a n) -> p a n", a=2), qT4[:, r, 0:P],
                                     kT4[:, 2:4, bass.ds(g, 1), 0:P].rearrange("p a b n -> p (a b) n"),
                                     start=True, stop=True)
                    nc.tensor.matmul(B[:].rearrange("p (a n) -> p a n", a=2), qT4[:, r, P:T],
                                     kT4[:, 2:4, bass.ds(g, 1)].rearrange("p a b n -> p (a b) n"),
                                     start=True, stop=True)
                    for tt in range(TT):
                        last = nc.tensor.matmul(A[:, 256 + 16 * tt:256 + 16 * tt + NCB], qT4[:, r, tt * P:(tt + 1) * P],
                                                kcT[:, bass.ds(g * NCB, NCB)], start=True, stop=True)
                    last.then_inc(sc_ps, 1)

                def group(g, last_group):
                    for r in range(REP):
                        b = r % 2
                        n = g * REP + r
                        pe.wait_ge(weights, n + 1)
                        for br in range(2):
                            nc.tensor.transpose(bank[4][:, br * 256:br * 256 + P], s0[:, b, br], ident)
                            nc.tensor.transpose(bank[4][:, br * 256 + P:br * 256 + 2 * P], s1[:, b, br, 0:P], ident)
                            nc.tensor.transpose(bank[5][:, br * P:(br + 1) * P], s1[:, b, br, P:T], ident)
                        for tt in range(TT):
                            last = nc.tensor.transpose(bank[5][0:NCB, 256 + tt * P:256 + (tt + 1) * P],
                                                       sc[:, b, tt, 0:NCB], ident)
                        last.then_inc(pT_ps, 1)
                        if r < REP - 2:
                            scores(g, r + 2)
                        if not last_group:
                            if r == REP - 2:
                                pe.wait_ge(biased, g * REP + REP)
                                queries(g + 1)
                            if r == REP - 1:
                                pe.wait_ge(qT_ready, g + 2)
                                scores(g + 1, 0)
                                scores(g + 1, 1)
                        if r == 0:
                            pe.wait_ge(v_in, g + 1)
                        pe.wait_ge(pT1, n + 1)
                        pe.wait_ge(pT2, n + 1)
                        if later(n, 1):
                            pe.wait_ge(oa_lo, n - 1)
                        O = bank[6 + b]
                        for br in range(2):
                            nc.tensor.matmul(O[:, 0:T], vg[:, 0, br], pt1[:, b, br * T:(br + 1) * T],
                                             start=(br == 0), stop=False)
                        for br in range(2):
                            nc.tensor.matmul(O[:, P:T], vg[:, 1, br], pt2[:, b, br * P:(br + 1) * P],
                                             start=False, stop=False)
                        nc.tensor.matmul(O[:, 0:T], vcg[:], ptc[:, b], start=False, stop=True).then_inc(o_ps, 1)

                queries(0)
                pe.wait_ge(qT_ready, 1)
                scores(0, 0)
                scores(0, 1)
                group(0, False)
                with pe.Fori(1, GB - 1) as g:
                    group(g, False)
                group(GB - 1, True)

        u_wo2 = new_unit(NS)
        mlp1 = dict(stream)
        new_unit(HPG * NG)
        fg = at("fg", WORK + 32768, [P, D])
        fg_in, y_out, out_ready = sem("fg_in"), sem("y_out"), sem("out_ready")

        with nc.Block() as block:
            @block.sync
            def _(sp):
                sp_unit(sp, t['nsa_wo'][0], u_wo2)
                sp_mlp(sp, 1, mlp1['chunk'], mlp1['slab'])
                for tt in range(TT):
                    sp.wait_ge(out_ready, tt + 1)
                    sp.dma_start(t['y'][0].rearrange("(t p) d -> p t d", p=P)[:, tt], xs2[:, tt])\
                        .then_inc(y_out, 16)
                sp.wait_ge(y_out, 16 * (TT))

            @block.gpsimd
            def _(pool):
                pool.dma_start(fg[:], t['final_norm_g'].partition_broadcast(P)).then_inc(fg_in, 16)
                pool_mlp(pool, 1, mlp1['chunk'], mlp1['slab'])

            @block.scalar
            def _(act):
                act_unit(act, u_wo2, nothing)
                act_norm_sum(act, 3, lambda s: act.wait_ge(acc_free, mlp1['slab'] - (NS - 1 - s)), xs2)
                act_norm_sqrt(act, 3)
                act_split_norm(act, 3, 'm1', xah)
                act_mlp(act, 1, mlp1['chunk'], mlp1['slab'])
                act_norm_sum(act, 4, lambda s: act.wait_ge(acc_free, stream['slab'] - (NS - 1 - s)), xs2)
                act_norm_sqrt(act, 4)

            @block.vector
            def _(dve):
                dve_unit(dve, u_wo2, lambda s: add_slab(dve, u_wo2['slab'] + s, s, s % 2))
                dve_norm(dve, 3, xs2)
                dve_split_norm(dve, 3 * KT, 'm1', xah, xal)
                dve_mlp(dve, 1, mlp1['chunk'], mlp1['slab'])
                dve_rstd(dve, 4)
                dve.wait_ge(fg_in, 16)
                for tt in range(TT):
                    nc.vector.scalar_tensor_tensor(out=xs2[:, tt], in0=h[:, tt], scalar=rstd[:, tt:tt + 1], in1=fg[:],
                                                   op0=ALU.mult, op1=ALU.mult).then_inc(out_ready, 1)

            @block.tensor
            def _(pe):
                pe_unit(pe, u_wo2, xbh, xbl)
                pe_norm(pe, 3, xs2)
                pe_mlp(pe, 1, mlp1['chunk'], mlp1['slab'], 3 * KT)

INS = ['x', 'consts', 'consts2', 'par_rows', 'rw_w1', 'rw_a1', 'rw_g1', 'rw_wr', 'rw_wk', 'rw_wv', 'rw_w2', 'rw_a2',
       'rw_g2', 'rw_wo', 'mlp_up', 'mlp_down', 'w_kv', 'nsa_wq', 'nsa_wo', 'rel_bias', 'cmp_pe', 'cmp_w1', 'cmp_b1',
       'cmp_w2', 'final_norm_g']
OUTS = {'y': (1, T, D)}


def kernel(**inputs):
    import numpy as _np
    import concourse.bacc as _bacc
    from concourse import mybir as _mybir
    from concourse.bass_utils import run_bass_kernel_spmd as _run
    nc = _bacc.Bacc("TRN2", target_bir_lowering=False, num_devices=1)
    ins = {k: _np.asarray(v) for k, v in inputs.items()}
    rows = {n: ins[n] for n in PARAMS if n in ins}
    for j in range(6):
        rows[f'mu{j}'] = ins['rw_mu'][0, j]
    for j in range(2):
        rows[f'm{j}'] = ins['m_norm_g'][j]
    ins['par_rows'] = _np.concatenate([_np.reshape(rows[n], (KT, P)) for n in PARAMS]).reshape(3, PROW, P)
    ins['consts'], ins['consts2'] = constants(), constants2()
    arrays, args = {}, {}
    for name in INS:
        a = _np.ascontiguousarray(ins[name])
        arrays[f"in_{name}"] = a
        args[name] = nc.dram_tensor(f"in_{name}", a.shape, _mybir.dt.from_np(a.dtype), kind="ExternalInput").ap()
    for name, shape in OUTS.items():
        args[name] = nc.dram_tensor(f"out_{name}", shape, _mybir.dt.float32, kind="ExternalOutput").ap()
    build(nc, **args)
    r = _run(nc, [arrays], core_ids=[0])
    got = tuple(r.results[0][f"out_{n}"] for n in OUTS)
    return got[0]
```
